# Optimizing a Trainium2 kernel written in Bass

```python
import math
import jax, jax.numpy as jnp
from jax import lax
import numpy as np

D_MODEL = 1024
BATCH = 1
SEQ = 1024
DEPTH = 1

CHUNK = 64
MEM_LEN = 256
Q_BLOCK = 128

FOX_HEADS = 8
FOX_HEAD_DIM = 64
FOX_WIDTH = FOX_HEADS * FOX_HEAD_DIM
FORGET_BIAS = 2.0
SSM_GROUP = 16
SSM_WIDTH = 512
SSM_GROUPS = SSM_WIDTH // SSM_GROUP
SSM_STATE = 64
DT_MIN = 1e-3
DT_MAX = 1e-1
CA_HEADS = 8
CA_HEAD_DIM = 64
CA_WIDTH = CA_HEADS * CA_HEAD_DIM
CA_LEFT_CHUNKS = 8
CA_BAND = (CA_LEFT_CHUNKS + 1) * CHUNK
REL_MIN = -(CHUNK - 1)
REL_MAX = 4 * CHUNK
N_REL = REL_MAX - REL_MIN + 1
N_BRANCH = 3
XA_HEADS = 4
XA_HEAD_DIM = D_MODEL // XA_HEADS
D_FF = 2816
CONV_WIDTH = 3
DN_ALPHA = (2 * DEPTH) ** 0.25
DN_BETA = (8 * DEPTH) ** -0.25
LN_EPS = 1e-5
NEG_INF = -1e30

_SPLITS = (FOX_WIDTH, FOX_WIDTH, FOX_WIDTH, FOX_HEADS, SSM_WIDTH,
           CA_WIDTH, CA_WIDTH, CA_WIDTH, D_MODEL, D_MODEL, D_MODEL)
N_IN = sum(_SPLITS)

kernel_name = "hybrid_fox_s5_chunkattn_deepnorm"

def _layer_norm(x, g, b):
    xf = x.astype(jnp.float32)
    mu = jnp.mean(xf, axis=-1, keepdims=True)
    var = jnp.mean(jnp.square(xf - mu), axis=-1, keepdims=True)
    y = (xf - mu) * lax.rsqrt(var + LN_EPS) * g.astype(jnp.float32) + b.astype(jnp.float32)
    return y.astype(x.dtype)

def _forgetting_attention(q, k, v, f_logit):
    S = q.shape[1]
    cum = jnp.cumsum(jax.nn.log_sigmoid(f_logit.astype(jnp.float32)), axis=1)
    cum = jnp.transpose(cum, (0, 2, 1))
    scale = FOX_HEAD_DIM ** -0.5
    outs = []
    for blk in range(S // Q_BLOCK):
        q0, q1 = blk * Q_BLOCK, (blk + 1) * Q_BLOCK
        s = jnp.einsum('bqhd,bkhd->bhqk', q[:, q0:q1], k[:, :q1]).astype(jnp.float32) * scale
        s = s + cum[:, :, q0:q1, None] - cum[:, :, None, :q1]
        causal = jnp.arange(q0, q1)[:, None] >= jnp.arange(q1)[None, :]
        p = jax.nn.softmax(jnp.where(causal, s, NEG_INF), axis=-1)
        outs.append(jnp.einsum('bhqk,bkhd->bqhd', p.astype(v.dtype), v[:, :q1]))
    return jnp.concatenate(outs, axis=1)

def _complex_linear_combine(e1, e2):
    a1r, a1i, b1r, b1i = e1
    a2r, a2i, b2r, b2i = e2
    ar = a2r * a1r - a2i * a1i
    ai = a2r * a1i + a2i * a1r
    br = a2r * b1r - a2i * b1i + b2r
    bi = a2r * b1i + a2i * b1r + b2i
    return ar, ai, br, bi

def _s5(u, lam_re, lam_im, log_dt, b_re, b_im, c_re, c_im, d):
    f32 = jnp.float32
    Bsz, S, _ = u.shape
    uf = u.astype(f32)
    ug = uf.reshape(Bsz, S, SSM_GROUPS, SSM_GROUP)
    lr = jnp.minimum(lam_re.astype(f32), -1e-4)
    li = lam_im.astype(f32)
    dt = jnp.exp(log_dt.astype(f32))[:, None]
    mag = jnp.exp(lr * dt)
    ar = mag * jnp.cos(li * dt)
    ai = mag * jnp.sin(li * dt)
    den = lr * lr + li * li
    gr = ((ar - 1.0) * lr + ai * li) / den
    gi = (ai * lr - (ar - 1.0) * li) / den
    br, bi = b_re.astype(f32), b_im.astype(f32)
    bbr = gr[..., None] * br - gi[..., None] * bi
    bbi = gr[..., None] * bi + gi[..., None] * br
    xr = jnp.einsum('bsgc,gpc->bsgp', ug, bbr)
    xi = jnp.einsum('bsgc,gpc->bsgp', ug, bbi)
    a_r = jnp.broadcast_to(ar, xr.shape)
    a_i = jnp.broadcast_to(ai, xr.shape)
    _, _, hr, hi = lax.associative_scan(_complex_linear_combine, (a_r, a_i, xr, xi), axis=1)
    y = (jnp.einsum('bsgp,gcp->bsgc', hr, c_re.astype(f32))
         - jnp.einsum('bsgp,gcp->bsgc', hi, c_im.astype(f32)))
    y = y.reshape(Bsz, S, SSM_WIDTH) + d.astype(f32) * uf
    return y.astype(u.dtype)

def _chunk_attention(q, k, v, rel_bias):
    Bsz, S, H, Dh = q.shape
    NC = S // CHUNK
    qc = q.reshape(Bsz, NC, CHUNK, H, Dh)

    def band(t):
        tc = t.reshape(Bsz, NC, CHUNK, H, Dh)
        tp = jnp.pad(tc, ((0, 0), (CA_LEFT_CHUNKS, 0), (0, 0), (0, 0), (0, 0)))
        return jnp.concatenate([tp[:, j:j + NC] for j in range(CA_LEFT_CHUNKS + 1)], axis=2)

    kb, vb = band(k), band(v)
    s = jnp.einsum('bnqhd,bnkhd->bnhqk', qc, kb).astype(jnp.float32) * (CA_HEAD_DIM ** -0.5)
    qi = jnp.arange(CHUNK)
    kk = jnp.arange(CA_BAND)
    rel = CA_LEFT_CHUNKS * CHUNK + qi[:, None] - kk[None, :]
    idx = jnp.clip(rel, REL_MIN, REL_MAX) - REL_MIN
    bias = rel_bias.astype(jnp.float32)[:, idx]
    valid = (jnp.arange(NC)[:, None] + (kk // CHUNK)[None, :] - CA_LEFT_CHUNKS) >= 0
    s = jnp.where(valid[None, :, None, None, :], s + bias[None, None], NEG_INF)
    p = jax.nn.softmax(s, axis=-1)
    o = jnp.einsum('bnhqk,bnkhd->bnqhd', p.astype(v.dtype), vb)
    return o.reshape(Bsz, S, H * Dh)

def _hybrid_mixer(x, w_in, b_in, lam_re, lam_im, log_dt, b_re, b_im, c_re, c_im, ssm_d,
                  rel_bias, w_fox_o, w_ssm_glu, w_ca_o, w_o):
    Bsz, S, _ = x.shape
    z = x @ w_in + b_in
    fq, fk, fv, ff, su, cq, ck, cv, g_fox, g_ssm, g_ca = jnp.split(z, np.cumsum(_SPLITS)[:-1], axis=-1)
    hs = lambda t, h, dh: t.reshape(Bsz, S, h, dh)
    ya = _forgetting_attention(hs(fq, FOX_HEADS, FOX_HEAD_DIM), hs(fk, FOX_HEADS, FOX_HEAD_DIM),
                               hs(fv, FOX_HEADS, FOX_HEAD_DIM), ff)
    ya = ya.reshape(Bsz, S, FOX_WIDTH) @ w_fox_o
    yb = jax.nn.gelu(_s5(su, lam_re, lam_im, log_dt, b_re, b_im, c_re, c_im, ssm_d)) @ w_ssm_glu
    yb_val, yb_gate = jnp.split(yb, 2, axis=-1)
    yb = yb_val * jax.nn.sigmoid(yb_gate)
    yc = _chunk_attention(hs(cq, CA_HEADS, CA_HEAD_DIM), hs(ck, CA_HEADS, CA_HEAD_DIM),
                          hs(cv, CA_HEADS, CA_HEAD_DIM), rel_bias) @ w_ca_o
    merged = (jax.nn.sigmoid(g_fox) * ya + jax.nn.sigmoid(g_ssm) * yb + jax.nn.sigmoid(g_ca) * yc)
    return merged @ w_o

def _memory_cross_attention(x, mem, wq, wkv, wo):
    Bsz, S, _ = x.shape
    M = mem.shape[1]
    q = (x @ wq).reshape(Bsz, S, XA_HEADS, XA_HEAD_DIM)
    k, v = jnp.split(mem @ wkv, 2, axis=-1)
    k = k.reshape(Bsz, M, XA_HEADS, XA_HEAD_DIM)
    v = v.reshape(Bsz, M, XA_HEADS, XA_HEAD_DIM)
    s = jnp.einsum('bqhd,bkhd->bhqk', q, k).astype(jnp.float32) * (XA_HEAD_DIM ** -0.5)
    p = jax.nn.softmax(s, axis=-1)
    o = jnp.einsum('bhqk,bkhd->bqhd', p.astype(v.dtype), v)
    return o.reshape(Bsz, S, D_MODEL) @ wo

def _conv_ffn(x, w_up, conv_w, conv_b, w_down):
    a, g = jnp.split(x @ w_up, 2, axis=-1)
    a = lax.conv_general_dilated(a, conv_w[:, None, :], window_strides=(1,),
                                 padding=[(CONV_WIDTH - 1, 0)],
                                 dimension_numbers=('NWC', 'WIO', 'NWC'),
                                 feature_group_count=D_FF) + conv_b
    return (jax.nn.gelu(a) * g) @ w_down

def setup_inputs(seed: int = 0) -> dict:
    key = jax.random.key(seed)
    ks = jax.random.split(key, 26)
    f32 = jnp.float32
    L, D = DEPTH, D_MODEL
    nrm = lambda k, shape, s: jax.random.normal(k, shape, f32) * s
    sd = D ** -0.5
    col_scale = jnp.concatenate([
        jnp.full((FOX_WIDTH,), sd, f32), jnp.full((FOX_WIDTH,), sd, f32),
        jnp.full((FOX_WIDTH,), sd * DN_BETA, f32), jnp.full((FOX_HEADS,), sd, f32),
        jnp.full((SSM_WIDTH,), sd, f32),
        jnp.full((CA_WIDTH,), sd, f32), jnp.full((CA_WIDTH,), sd, f32),
        jnp.full((CA_WIDTH,), sd * DN_BETA, f32),
        jnp.full((N_BRANCH * D,), sd, f32)])
    col_offset = jnp.concatenate([
        jnp.zeros((3 * FOX_WIDTH,), f32), jnp.full((FOX_HEADS,), FORGET_BIAS, f32),
        jnp.zeros((N_IN - 3 * FOX_WIDTH - FOX_HEADS,), f32)])
    xa_kv_scale = jnp.concatenate([jnp.full((D,), sd, f32), jnp.full((D,), sd * DN_BETA, f32)])
    lam_im0 = math.pi * jnp.arange(SSM_STATE, dtype=f32)
    return {
        "x": nrm(ks[0], (BATCH, SEQ, D), 1.0),
        "mem": nrm(ks[1], (BATCH, MEM_LEN, D), 1.0),
        "w_in": jax.random.normal(ks[2], (L, D, N_IN), f32) * col_scale,
        "b_in": nrm(ks[3], (L, N_IN), 0.02) + col_offset,
        "ssm_lambda_re": -0.5 + nrm(ks[4], (L, SSM_GROUPS, SSM_STATE), 1e-3),
        "ssm_lambda_im": lam_im0 + nrm(ks[5], (L, SSM_GROUPS, SSM_STATE), 1e-3),
        "ssm_log_dt": jax.random.uniform(ks[6], (L, SSM_GROUPS), f32, math.log(DT_MIN), math.log(DT_MAX)),
        "ssm_b_re": nrm(ks[7], (L, SSM_GROUPS, SSM_STATE, SSM_GROUP), (2 * SSM_GROUP) ** -0.5),
        "ssm_b_im": nrm(ks[8], (L, SSM_GROUPS, SSM_STATE, SSM_GROUP), (2 * SSM_GROUP) ** -0.5),
        "ssm_c_re": nrm(ks[9], (L, SSM_GROUPS, SSM_GROUP, SSM_STATE), SSM_STATE ** -0.5),
        "ssm_c_im": nrm(ks[10], (L, SSM_GROUPS, SSM_GROUP, SSM_STATE), SSM_STATE ** -0.5),
        "ssm_d": nrm(ks[11], (L, SSM_WIDTH), 1.0),
        "ca_rel_bias": nrm(ks[12], (L, CA_HEADS, N_REL), 0.1),
        "w_fox_o": nrm(ks[13], (L, FOX_WIDTH, D), DN_BETA * FOX_WIDTH ** -0.5),
        "w_ssm_glu": nrm(ks[14], (L, SSM_WIDTH, 2 * D), DN_BETA * SSM_WIDTH ** -0.5),
        "w_ca_o": nrm(ks[15], (L, CA_WIDTH, D), DN_BETA * CA_WIDTH ** -0.5),
        "w_o": nrm(ks[16], (L, D, D), DN_BETA * sd),
        "xa_wq": nrm(ks[17], (L, D, D), sd),
        "xa_wkv": jax.random.normal(ks[18], (L, D, 2 * D), f32) * xa_kv_scale,
        "xa_wo": nrm(ks[19], (L, D, D), DN_BETA * sd),
        "ffn_w_up": nrm(ks[20], (L, D, 2 * D_FF), DN_BETA * sd),
        "ffn_conv_w": nrm(ks[21], (L, CONV_WIDTH, D_FF), CONV_WIDTH ** -0.5),
        "ffn_conv_b": nrm(ks[22], (L, D_FF), 0.02),
        "ffn_w_down": nrm(ks[23], (L, D_FF, D), DN_BETA * D_FF ** -0.5),
        "ln_g": 1.0 + nrm(ks[24], (L, 3, D), 0.02),
        "ln_b": nrm(ks[25], (L, 3, D), 0.02),
    }

def reference(x, mem, w_in, b_in, ssm_lambda_re, ssm_lambda_im, ssm_log_dt, ssm_b_re, ssm_b_im,
              ssm_c_re, ssm_c_im, ssm_d, ca_rel_bias, w_fox_o, w_ssm_glu, w_ca_o, w_o,
              xa_wq, xa_wkv, xa_wo, ffn_w_up, ffn_conv_w, ffn_conv_b, ffn_w_down, ln_g, ln_b):
    for l in range(DEPTH):
        h = _hybrid_mixer(x, w_in[l], b_in[l], ssm_lambda_re[l], ssm_lambda_im[l], ssm_log_dt[l],
                          ssm_b_re[l], ssm_b_im[l], ssm_c_re[l], ssm_c_im[l], ssm_d[l],
                          ca_rel_bias[l], w_fox_o[l], w_ssm_glu[l], w_ca_o[l], w_o[l])
        x = _layer_norm(DN_ALPHA * x + h, ln_g[l, 0], ln_b[l, 0])
        h = _memory_cross_attention(x, mem, xa_wq[l], xa_wkv[l], xa_wo[l])
        x = _layer_norm(DN_ALPHA * x + h, ln_g[l, 1], ln_b[l, 1])
        h = _conv_ffn(x, ffn_w_up[l], ffn_conv_w[l], ffn_conv_b[l], ffn_w_down[l])
        x = _layer_norm(DN_ALPHA * x + h, ln_g[l, 2], ln_b[l, 2])
    return x


_drawn_inputs = setup_inputs


def setup_inputs(seed=0):
    import zlib

    import numpy as np

    out = dict(_drawn_inputs(seed))
    spreads = {}
    factors = {'ssm_lambda_re': 64.0,
     'ssm_lambda_im': 64.0,
     'ssm_log_dt': 64.0,
     'ssm_b_re': 64.0,
     'ssm_b_im': 64.0,
     'ssm_c_re': 64.0,
     'ssm_c_im': 64.0,
     'ca_rel_bias': 8.0,
     'w_ca_o': 5.54,
     'ffn_conv_b': 8.0}
    for name, (base, spread) in spreads.items():
        noise = np.random.default_rng([zlib.crc32(name.encode()), seed]).standard_normal(out[name].shape)
        drawn = base * np.exp(spread * noise) if base else spread * noise
        out[name] = __import__('jax').numpy.asarray(drawn.astype(out[name].dtype))
    for name, factor in factors.items():
        out[name] = (out[name] * factor).astype(out[name].dtype)
    return out
```

```python
from contextlib import ExitStack

import concourse.bass as bass
from concourse import mybir

F32 = mybir.dt.float32
F32R = mybir.dt.float32r
BF16 = mybir.dt.bfloat16
ALU = mybir.AluOpType
ACT = mybir.ActivationFunctionType

P = 128
D = 1024
S = 1024
KD = D // P
NB = S // P
HALF = 512
HD = 64
PAIRS = 4
MEM = 256
XH_HEADS = 4
TQ = 256
NPRM = 25
CA_BACK = 4
CA_KEYS = (CA_BACK + 1) * P
FF_TILES = 22
FF_GROUPS = (8, 8, 6)
ALPHA = 2.0 ** 0.25
LN_EPS = 1e-5
NEG = -1e30
LOWEST = -3.0e38
TWO_PI = 6.283185307179586
RND = 12582912.0
PI_A = 6.28125
PI_B = 1014.0 / 2 ** 19
PI_C = TWO_PI - PI_A - PI_B

FOX_SLOTS, CA_SLOTS = 4, 3
N_FOX = 0
N_CA = N_FOX + FOX_SLOTS * PAIRS
N_EF = N_CA + CA_SLOTS * PAIRS
N_EC = N_EF + 2 * KD
N_ES = N_EC + 2 * KD
N_WO = N_ES + 2 * KD
N_KV = N_WO + KD
N_XQ = N_KV + 2 * KD
N_XO = N_XQ + KD
N_FF = N_XO + KD
N_SMALL = 13
EXP_STEP, SIN_STEP, BP_STEP, BT_STEP, FFEXP_STEP, CUM_STEP = 3, 14, 50, 151, 153, 156
N_SLOTS = N_FF + sum(2 * g + KD for g in FF_GROUPS)


def hybrid_layer(nc, xT, memT, w_ff, b_ff, w_fox, w_ca, w_gate, w_foxo, w_cao, w_glu, w_o,
                 w_kv, w_xq, w_xo, w_up, w_dn0, w_dn1, w_dn2, b_cols, lam_re, lam_im, log_dt,
                 b_re, b_im, c_re, c_im, ssm_d, rel, conv, ln_cols, ln_rows, cum_scratch, out):
    w_dn = (w_dn0, w_dn1, w_dn2)
    with ExitStack() as ctx:
        sems = {}

        def sem(name):
            sems[name] = ctx.enter_context(nc.semaphore(name))
            return sems[name]

        base = 16512
        KB = 1024

        def at(name, kb, cols, dt=F32):
            return nc.alloc_sbuf_tensor_at(name, [P, cols], dt, offset=base + int(kb * KB))

        XH, XL = at("XH", 0, KD * S, F32R), at("XL", 32, KD * S, F32R)
        WR, WH, WL = at("WR", 64, 2 * D), at("WH", 72, 2 * D, F32R), at("WL", 80, 2 * D, F32R)
        YS = at("YS", 88, 4 * S)
        OF, OC = at("OF", 104, 4 * S), at("OC", 120, 4 * S)
        XRAW = at("XRAW", 136, KD * S)
        QT, KT, VT, VV = (at(n, 136 + 4 * j, S) for j, n in enumerate(("QT", "KT", "VT", "VV")))
        MB = at("MB", 152, 2 * S)
        SB = at("SB", 160, 2 * S)
        PT = at("PT", 168, 2 * S)
        US = at("US", 176, S)
        T4 = at("T4", 180, 4 * TQ)
        YG = at("YG", 184, 4 * TQ)
        P4 = at("P4", 188, 4 * TQ)
        HH = at("HH", 192, 4 * TQ)
        BS, CS = at("BS", 196, 256), at("CS", 197, 256)
        W16 = at("W16", 198, 16 * 32)
        WT = at("WT", 120, 2 * 3 * TQ)
        BT, CT = at("BT", 126, 4 * 256), at("CT", 130, 16 * 64)
        PRM = at("PRM", 134, 16 * NPRM)
        BRAW = at("BRAW", 168, 2 * 256)
        BBAR = at("BBAR", 170, 2 * 256)
        CRAW = at("CRAW", 172, 2 * 256)
        BP = at("BP", 184, 2 * 512)
        BTMP = at("BTMP", 188, 256)
        W16T = at("W16T", 190, 2 * 256)
        WFF = at("WFF", 174, 64)
        FFB = at("FFB", 192, S)
        FFE = at("FFE", 180, S)
        OH, OL = at("OH", 136, 4 * S, F32R), at("OL", 152, 4 * S, F32R)
        MT = at("MT", 168, KD * S)
        ML = at("ML", 168, KD * S, F32R)
        MH = at("MH", 104, KD * S, F32R)
        GF = at("GF", 104, S)
        GS, G2 = at("GS", 88, S), at("G2", 92, S)
        RT1 = at("RT1", 136, KD * S)
        XN1 = at("XN1", 168, KD * S)
        XF = at("XF", 88, 2 * S)
        MRAW = at("MRAW", 96, KD * MEM)
        MMH, MML = at("MMH", 104, KD * MEM, F32R), at("MML", 112, KD * MEM, F32R)
        KM, VM = at("KM", 120, KD * MEM), at("VM", 128, 2 * D)
        VMT = at("VMT", 100, 2 * MEM)
        QX = at("QX", 88, 2 * S)
        SX = at("SX", 104, 2 * MEM)
        VX = at("VX", 108, 2 * MEM)
        OHX, OLX = at("OHX", 136, KD * S, F32R), at("OLX", 168, KD * S, F32R)
        PTX = at("PTX", 112, 2 * 2 * HALF)
        RT2 = at("RT2", 104, KD * S)
        XN2 = at("XN2", 136, KD * S)
        YT = at("YT", 104, KD * S)
        HDH, HDL = at("HDH", 136, KD * S, F32R), at("HDL", 168, KD * S, F32R)
        CV = at("CV", 88, S)
        GL = at("GL", 92, S)
        HF = at("HF", 96, S)
        XN3 = at("XN3", 136, KD * S)
        LGB = at("LGB", 88, 2 * D)
        c0 = 200.25
        IDN = at("IDN", c0, P)
        IDB = at("IDB", c0 + .5, P, BF16)
        CMB = at("CMB", c0 + .75, P, BF16)
        BC = at("BC", c0 + 1, 52)
        CONV = at("CONV", c0 + 1.25, FF_TILES * 4)
        LNC = at("LNC", c0 + 1.625, 6 * KD)
        DC = at("DC", c0 + 1.875, 8)
        PS = at("PS", c0 + 1.9375, 4 * NPRM)
        MX = at("MX", c0 + 2.375, 8)
        ST = at("ST", c0 + 2.5, 8 * 12)
        MV = at("MV", c0 + 2.9375, 8 * 8)
        SP = at("SP", c0 + 3.1875, 16 * 24)

        PA = ctx.enter_context(nc.psum_tensor("PA", [P, S], F32))
        PB = ctx.enter_context(nc.psum_tensor("PB", [P, S], F32))
        TB = ctx.enter_context(nc.psum_tensor("TB", [P, S], F32))
        OB = ctx.enter_context(nc.psum_tensor("OB", [P, HALF], F32))
        XB = ctx.enter_context(nc.psum_tensor("XB", [P, HALF], F32))
        PAIR = (PA, PB)

        params = sem("params_loaded")
        consts = sem("consts_built")
        xraw = [sem(f"x_loaded{h}") for h in range(4)]
        x_hi, x_lo = sem("x_hi"), sem("x_lo")
        raw = [sem(f"w_loaded{b}") for b in range(2)]
        w_hi, w_lo, w_used = sem("w_hi"), sem("w_lo"), sem("w_used")
        su = sem("setup_dve")
        sa = sem("setup_act")
        sp = sem("setup_pool")
        st_pe = sem("setup_pe")
        cum_out = sem("cum_stored")
        spv = lambda j: SP[:, 16 * j:16 * j + 16]

        def pair(b):
            return PAIR[b % 2]

        def split_hi(act, n, b, raw_count, after_last=False):
            act.wait_ge(raw[b], 16 * raw_count)
            act.wait_ge(w_used, n + (2 if after_last else 1))
            act.activation(WH[:, b * D:(b + 1) * D], WR[:, b * D:(b + 1) * D],
                           ACT.Copy).then_inc(w_hi, 1)

        def split_lo(dve, n, b):
            dve.wait_ge(w_hi, n + 1)
            dve.tensor_tensor(WL[:, b * D:(b + 1) * D], WR[:, b * D:(b + 1) * D],
                              WH[:, b * D:(b + 1) * D].bitcast(F32), ALU.subtract).then_inc(w_lo, 1)

        def product(pe, n, b, dst, xh, xl, nk=KD, width=S, k0=0, part=None):
            ks = range(nk) if part is None else range(part * nk // 2, (part + 1) * nk // 2)
            if part in (None, 0):
                pe.wait_ge(w_lo, n + 3)
            for k in ks:
                w0 = b * D + (k0 + k) * P
                for pas, (w, x) in enumerate(((WH, xh), (WH, xl), (WL, xh))):
                    for t in range(0, width, HALF):
                        tw = min(HALF, width - t)
                        mm = pe.matmul(dst[:, t:t + tw], w[:, w0:w0 + P],
                                       x[:, k * width + t:k * width + t + tw],
                                       start=(k == 0 and pas == 0), stop=(k == nk - 1 and pas == 2))
            return mm

        def attention_events(tag):
            names = ("proj_ready", "s_ready", "s_summed", "nmax_ready", "exp_done", "rsum_ready",
                     "p_ready", "t_ready", "t_copied", "pv_done", "o_copied")
            return {n: sem(f"{tag}_{n}") for n in names}

        fox, ca = attention_events("fox"), attention_events("ca")
        mb_loaded = {"fox": [sem(f"fox_rows_loaded{h}") for h in range(2)],
                     "ca": [sem(f"ca_bias_loaded{h}") for h in range(2)]}
        ca_masked = sem("ca_bias_masked")
        CHUNKS = 26

        def key_blocks(kind, blk):
            return list(range(0 if kind == "fox" else max(0, blk - CA_BACK), blk + 1))

        def cut(blocks):
            return [blocks[a:a + 4] for a in range(0, len(blocks), 4)]

        def first_chunk(kind, u):
            return 2 + sum(len(cut(key_blocks(kind, v % NB))) for v in range(u))

        assert first_chunk("fox", 16) == CHUNKS and first_chunk("ca", 16) == CHUNKS

        def pe_scores(pe, kind, ev, u):
            hh, blk = divmod(u, NB)
            kb = key_blocks(kind, blk)
            r = slice(HD * hh, HD * hh + HD)
            dst = pair(u)
            n = len(kb) * P
            for c in range(0, n, HALF):
                w = min(HALF, n - c)
                last = c + w == n and kind == "fox"
                mm = pe.matmul(dst[:, c:c + w], QT[r, blk * P:(blk + 1) * P],
                               KT[r, kb[0] * P + c:kb[0] * P + c + w], start=True, stop=not last)
            if kind == "fox":
                mm = pe.matmul(dst[:, n - P:n], IDB[:, :], CMB[:, :], start=False, stop=True)
            mm.then_inc(ev["s_ready"], 1)

        def pe_transposes(pe, kind, ev, i, u):
            pe.wait_ge(ev["p_ready"], 16 * i + u + 1)
            c = first_chunk(kind, u)
            for j, blocks in enumerate(cut(key_blocks(kind, u % NB))):
                pe.wait_ge(ev["t_copied"], CHUNKS * i + c + j - 1)
                bank = (c + j) % 2 * HALF
                for m in range(len(blocks)):
                    col = (u % 2) * S + (4 * j + m) * P
                    mm = pe.transpose(TB[:, bank + m * P:bank + (m + 1) * P], SB[:, col:col + P],
                                      IDN[:, :])
                mm.then_inc(ev["t_ready"], 1)

        def pe_values(pe, kind, ev, i, u):
            hh, blk = divmod(u, NB)
            kb = key_blocks(kind, blk)
            pe.wait_ge(ev["t_copied"], CHUNKS * i + first_chunk(kind, u + 1))
            if u % 4 == 0 and u:
                pe.wait_ge(ev["o_copied"], 4 * i + u // 4)
            for m, key in enumerate(kb):
                mm = pe.matmul(OB[HD * hh:HD * hh + HD, blk % 4 * P:(blk % 4 + 1) * P],
                               VV[:, key * P + HD * hh:key * P + HD * hh + HD],
                               PT[:, (u % 2) * S + m * P:(u % 2) * S + (m + 1) * P],
                               start=(m == 0), stop=(m == len(kb) - 1))
            mm.then_inc(ev["pv_done"], 1)

        def pe_turn_v(pe, ev, per, at_, i):
            pe.wait_ge(ev["proj_ready"], per * i + at_ + 1)
            for j in range(2):
                for m in range(4):
                    mm = pe.transpose(TB[:, j * HALF + m * P:j * HALF + (m + 1) * P],
                                      VT[:, (4 * j + m) * P:(4 * j + m + 1) * P], IDN[:, :])
                mm.then_inc(ev["t_ready"], 1)

        def dve_rowmax(dve, kind, ev, i, u):
            hh, blk = divmod(u, NB)
            kb = key_blocks(kind, blk)
            n, b = len(kb) * P, u % 2
            if blk == 0:
                if kind == "fox":
                    dve.wait_ge(mb_loaded["fox"][hh], 16 * i + 16)
                else:
                    dve.wait_ge(ca_masked, 4 * i + 2 * hh + 3)
            col = hh * S + (0 if kind == "fox" else (kb[0] - blk + CA_BACK) * P)
            dve.wait_ge(ev["s_ready"], 16 * i + u + 1)
            dve.sem_inc(scores_seen, 1)
            dve.tensor_tensor_reduce(SB[:, b * S:b * S + n], pair(u)[:, 0:n], MB[:, col:col + n],
                                     1.0, LOWEST, ALU.add, ALU.max,
                                     MX[:, b:b + 1]).then_inc(ev["s_summed"], 1)
            dve.wait_ge(ev["s_summed"], 16 * i + u + 17)
            dve.tensor_scalar(MX[:, 2 + b:3 + b], MX[:, b:b + 1], -1.0, None,
                              ALU.mult).then_inc(ev["nmax_ready"], 1)

        def dve_normalise(dve, kind, ev, i, u):
            b = u % 2
            n = len(key_blocks(kind, u % NB)) * P
            dve.wait_ge(ev["exp_done"], 16 * i + u + 1)
            dve.reciprocal(MX[:, 6 + b:7 + b], MX[:, 4 + b:5 + b]).then_inc(ev["rsum_ready"], 1)
            dve.wait_ge(ev["rsum_ready"], 16 * i + u + 1)
            dve.tensor_scalar(SB[:, b * S:b * S + n], SB[:, b * S:b * S + n],
                              MX[:, 6 + b:7 + b], None, ALU.mult).then_inc(ev["p_ready"], 1)

        def act_exp(act, kind, ev, i, u):
            b = u % 2
            n = len(key_blocks(kind, u % NB)) * P
            act.wait_ge(ev["nmax_ready"], 16 * i + u + 1)
            act.activation(SB[:, b * S:b * S + n], SB[:, b * S:b * S + n], ACT.Exp,
                           bias=MX[:, 2 + b:3 + b],
                           accum_out=MX[:, 4 + b:5 + b]).then_inc(ev["exp_done"], 1)

        def act_copy_turned(act, kind, ev, i, u):
            c = first_chunk(kind, u)
            for j, blocks in enumerate(cut(key_blocks(kind, u % NB))):
                if j == 0 and u >= 2:
                    act.wait_ge(ev["pv_done"], 16 * i + u - 1)
                act.wait_ge(ev["t_ready"], CHUNKS * i + c + j + 1)
                w, bank, col = len(blocks) * P, (c + j) % 2 * HALF, (u % 2) * S + 4 * j * P
                act.activation(PT[:, col:col + w], TB[:, bank:bank + w],
                               ACT.Copy).then_inc(ev["t_copied"], 1)

        def act_copy_v(act, ev, i):
            for j in range(2):
                act.wait_ge(ev["t_ready"], CHUNKS * i + j + 1)
                act.activation(VV[:, j * HALF:(j + 1) * HALF], TB[:, j * HALF:(j + 1) * HALF],
                               ACT.Copy).then_inc(ev["t_copied"], 1)

        def act_copy_o(act, ev, i, g, dst):
            r = slice(HD * (g // 2), HD * (g // 2) + HD)
            act.wait_ge(ev["pv_done"], 16 * i + 4 * g + 4)
            act.activation(dst[r, bass.ds(i * S + g % 2 * HALF, HALF)], OB[r, :],
                           ACT.Copy).then_inc(ev["o_copied"], 1)

        NQ = 16
        staged = sem("ssm_params_staged")
        table_step = sem("ssm_table_step")
        x_ready = sem("ssm_bu_ready")
        turned = sem("ssm_bu_turned")
        yadd = sem("ssm_input_ready")
        scanned = sem("ssm_scanned")
        back = sem("ssm_back_turned")
        h_ready = sem("ssm_state_ready")
        y_ready = sem("ssm_ch_ready")
        y_done = sem("ssm_y_done")
        TSTEPS = 1 + 4 * 2 + 1
        B_AT = {(0 if k == 0 else 2 * k - 1): k for k in range(NQ)}
        C_AT = {2 * k + 2: k for k in range(NQ)}

        def pe_ssm(pe, i, pos):
            if pos in B_AT:
                k = B_AT[pos]
                tau, q = divmod(k, 4)
                r = slice(32 * tau, 32 * tau + 32)
                if k == 0:
                    pe.wait_ge(fox["proj_ready"], 4 * i + 1)
                    pe.wait_ge(staged, 4 * i + 4)
                pe.wait_ge(y_done, NQ * i + 1 + max(k - 1, 0))
                if k:
                    pe.wait_ge(turned, NQ * i + k)
                for m in range(2):
                    mm = pe.matmul(XB[:, m * TQ:(m + 1) * TQ], BS[r, m * P:(m + 1) * P],
                                   US[r, q * TQ:(q + 1) * TQ], start=True, stop=True)
                mm.then_inc(x_ready, 1)
            if pos in C_AT:
                k = C_AT[pos]
                tau = k // 4
                pe.wait_ge(h_ready, NQ * i + k + 1)
                pe.wait_ge(turned, NQ * i + min(k + 2, NQ))
                if k == NQ - 1:
                    pe.wait_ge(y_done, NQ * i + NQ)
                for m in range(2):
                    h0 = (k % 2) * 2 * TQ + m * TQ
                    mm = pe.matmul(XB[32 * tau:32 * tau + 32, 0:TQ],
                                   CS[:, tau * 64 + m * 32:tau * 64 + m * 32 + 32],
                                   HH[:, h0:h0 + TQ], start=(m == 0), stop=(m == 1))
                mm.then_inc(y_ready, 1)

        def dve_table(dve, i, tau):
            b = tau % 2 * 3 * TQ
            p0, s0 = tau * NPRM, (4 * i + tau) * TSTEPS
            wr = lambda a, n: WT[:, b + a:b + a + n]
            wi = lambda a, n: WT[:, b + TQ + a:b + TQ + a + n]
            tmp = lambda m, n: T4[:, m * TQ:m * TQ + n]
            dve.tensor_copy(WT[:, b:b + 2 * TQ].rearrange("p (c t) -> p c t", c=2)[:, :, 0:16],
                            W16[:, bass.ds(i * 128 + tau * 32, 32)].rearrange("p (c t) -> p c t", c=2)
                            ).then_inc(table_step, 1)
            for m in range(4, 8):
                n, s1 = 2 ** m, s0 + 1 + 2 * (m - 4)
                er, ei, ne = (PS[:, p0 + 8 * c + m:p0 + 8 * c + m + 1] for c in range(3))
                dve.wait_ge(table_step, s1)
                dve.tensor_scalar(tmp(0, n), wi(0, n), ne, None, ALU.mult)
                dve.tensor_scalar(tmp(1, n), wi(0, n), er, None, ALU.mult).then_inc(table_step, 1)
                dve.wait_ge(table_step, s1 + 1)
                dve.scalar_tensor_tensor(wr(n, n), wr(0, n), er, tmp(0, n), ALU.mult, ALU.add)
                dve.scalar_tensor_tensor(wi(n, n), wr(0, n), ei, tmp(1, n), ALU.mult,
                                         ALU.add).then_inc(table_step, 1)
            dve.wait_ge(table_step, s0 + 9)
            dve.tensor_copy(WT[:, b + 2 * TQ:b + 3 * TQ], wr(0, TQ)).then_inc(table_step, 1)
            dve.wait_ge(table_step, s0 + 10)

        def dve_stage(dve, i):
            dve.wait_ge(y_done, NQ * i + 1)
            dve.tensor_copy(BS[:, :], BT[:, bass.ds(i * 256, 256)]).then_inc(staged, 1)
            dve.tensor_copy(CS[:, :], CT[:, bass.ds(i * 256, 256)]).then_inc(staged, 1)
            dve.tensor_copy(PS[:, :], PRM[:, bass.ds(i * 4 * NPRM, 4 * NPRM)]).then_inc(staged, 1)
            dve.tensor_copy(DC[:, 4:5], DC[:, bass.ds(i, 1)]).then_inc(staged, 1)

        def dve_ssm(dve, i, k):
            if 0 <= k - 2 < NQ:
                j = k - 2
                tau, q = divmod(j, 4)
                r = slice(32 * tau, 32 * tau + 32)
                dve.wait_ge(y_ready, NQ * i + j + 1)
                dve.scalar_tensor_tensor(YS[r, bass.ds(i * S + q * TQ, TQ)], US[r, q * TQ:(q + 1) * TQ],
                                         DC[r, 4:5], XB[r, 0:TQ], ALU.mult, ALU.add).then_inc(y_done, 1)
            if k < NQ:
                tau, q = divmod(k, 4)
                w = tau % 2 * 3 * TQ
                if q == 0:
                    dve.wait_ge(table_step, (4 * i + tau + 1) * TSTEPS)
                if k:
                    dve.wait_ge(yadd, 2 * NQ * i + 2 * k)
                dve.wait_ge(x_ready, NQ * i + k + 1)
                dve.tensor_tensor(T4[:, 0:2 * TQ], XB[:, :], WT[:, w:w + 2 * TQ], ALU.mult)
                dve.tensor_tensor(T4[:, 2 * TQ:4 * TQ], XB[:, :], WT[:, w + TQ:w + 3 * TQ],
                                  ALU.mult).then_inc(turned, 1)
            if 0 <= k - 1 < NQ:
                j = k - 1
                tau, q = divmod(j, 4)
                w, g = tau % 2 * 3 * TQ, j % 2 * 2 * TQ
                decay = PS[:, tau * NPRM + 24:tau * NPRM + 25].to_broadcast([P, TQ])
                dve.wait_ge(yadd, 2 * NQ * i + 2 * j + 2)
                if j:
                    dve.wait_ge(h_ready, NQ * i + j)
                for m in range(2):
                    h0 = (1 - j % 2) * 2 * TQ + (m + 1) * TQ - 1
                    sc = dve.tensor_tensor_scan(YG[:, g + m * TQ:g + (m + 1) * TQ], decay,
                                                YG[:, g + m * TQ:g + (m + 1) * TQ],
                                                HH[:, h0:h0 + 1] if q else 0.0, ALU.mult, ALU.add)
                sc.then_inc(scanned, 1)
                dve.wait_ge(scanned, NQ * i + j + 1)
                dve.tensor_tensor(P4[:, 0:2 * TQ], YG[:, g:g + 2 * TQ], WT[:, w:w + 2 * TQ], ALU.mult)
                dve.tensor_tensor(P4[:, 2 * TQ:4 * TQ], YG[:, g:g + 2 * TQ],
                                  WT[:, w + TQ:w + 3 * TQ], ALU.mult).then_inc(back, 1)

        def pool_ssm(pool, i, k):
            if k < NQ:
                g = k % 2 * 2 * TQ
                pool.wait_ge(turned, NQ * i + k + 1)
                if k >= 2:
                    pool.wait_ge(back, NQ * i + k - 1)
                pool.tensor_tensor(YG[:, g:g + TQ], T4[:, 0:TQ], T4[:, TQ:2 * TQ],
                                   ALU.add).then_inc(yadd, 1)
                pool.tensor_tensor(YG[:, g + TQ:g + 2 * TQ], T4[:, 3 * TQ:4 * TQ],
                                   T4[:, 2 * TQ:3 * TQ], ALU.subtract).then_inc(yadd, 1)
            if k:
                j = k - 1
                h = j % 2 * 2 * TQ
                pool.wait_ge(back, NQ * i + j + 1)
                if j >= 2:
                    pool.wait_ge(y_ready, NQ * i + j - 1)
                pool.tensor_tensor(HH[:, h:h + TQ], P4[:, 0:TQ], P4[:, TQ:2 * TQ], ALU.subtract)
                pool.tensor_tensor(HH[:, h + TQ:h + 2 * TQ], P4[:, 2 * TQ:3 * TQ],
                                   P4[:, 3 * TQ:4 * TQ], ALU.add).then_inc(h_ready, 1)

        g_ready = {t: sem(f"{t}_gate_ready") for t in ("ef", "ec", "es")}
        o_hi = {t: sem(f"{t}_branch_hi") for t in ("ef", "ec", "es")}
        o_lo = {t: sem(f"{t}_branch_lo") for t in ("ef", "ec", "es")}
        m_step = {t: sem(f"{t}_merge_step") for t in ("ef", "ec", "es")}
        m_hi, m_lo = sem("merged_hi"), sem("merged_lo")
        y_act = sem("ssm_gelu")
        rt_step = {t: sem(f"{t}_residual_step") for t in ("wo", "xo")}
        mem_loaded, mem_hi, mem_lo = sem("mem_loaded"), sem("mem_hi"), sem("mem_lo")
        kv_ready = sem("kv_ready")
        v_turned, v_ready = sem("mem_v_turned"), sem("mem_v_ready")
        lns = [{n: sem(f"ln{k}_{n}") for n in
                ("turned", "copied", "step", "sqrt", "normed", "back", "scaled", "hi", "lo")}
               for k in range(3)]
        xa = {n: sem(f"xa_{n}") for n in ("q_ready", "v_staged", "s_ready", "max", "nmax", "exp",
                                          "rsum", "p_ready", "t_ready", "t_copied", "pv", "hi", "lo")}
        cv_step, gelu_done, hid, hid_hi, hid_lo, y_sum = (sem(n) for n in (
            "conv_step", "gelu_done", "hidden_ready", "hidden_hi", "hidden_lo", "down_added"))
        rows_loaded, final_step, out_stored = sem("ln_rows_loaded"), sem("final_step"), sem("out_stored")
        scores_seen, masks_due = sem("scores_seen"), sem("masks_due")

        def rc(n0, k):
            return (16 if k % 2 == 0 else 12) + (n0 - N_EF) // 2 + k // 2 + 1

        RES = {"wo": (RT1, N_WO), "xo": (RT2, N_XO)}

        def pe_ln_forward(pe, ln, rt, tau, ready):
            if tau == 0:
                pe.wait_ge(*ready)
            if tau >= 2:
                pe.wait_ge(ln["copied"], tau - 1)
            for j in range(KD):
                mm = pe.transpose(pair(tau)[:, j * P:(j + 1) * P],
                                  rt[:, j * S + tau * P:j * S + (tau + 1) * P], IDN[:, :])
            mm.then_inc(ln["turned"], 1)

        def act_ln_copy(act, ln, xn, tau):
            act.wait_ge(ln["turned"], tau + 1)
            act.activation(xn[:, tau * D:(tau + 1) * D], pair(tau)[:, :], ACT.Copy).then_inc(ln["copied"], 1)

        def dve_ln_stats(dve, ln, xn, tau):
            dve.wait_ge(ln["copied"], tau + 1)
            for h in range(2):
                dve.bn_stats(ST[:, tau * 12 + 6 * h:tau * 12 + 6 * h + 6],
                             xn[:, tau * D + h * HALF:tau * D + (h + 1) * HALF]).then_inc(ln["step"], 1)
            dve.wait_ge(ln["step"], 3 * tau + 2)
            dve.bn_aggr(MV[:, 2 * tau:2 * tau + 2], ST[:, tau * 12:tau * 12 + 12]).then_inc(ln["step"], 1)

        mean = lambda tau: MV[:, 2 * tau:2 * tau + 1]
        var = MV[:, 0:16].rearrange("p (t c) -> p t c", c=2)[:, :, 1]
        sd, rstd, tmp8 = (MV[:, 16 + 8 * j:24 + 8 * j] for j in range(3))

        def act_ln_sqrt(act, ln):
            act.wait_ge(ln["step"], 25)
            act.activation(sd, var, ACT.Sqrt).then_inc(ln["sqrt"], 1)

        def dve_ln_normalise(dve, ln, xn):
            step = ln["step"]

            def link(ins, n):
                ins.then_inc(step, 1)
                dve.wait_ge(step, n)

            dve.wait_ge(step, 24)
            link(dve.tensor_scalar(var, var, LN_EPS, None, ALU.add), 25)
            dve.wait_ge(ln["sqrt"], 1)
            link(dve.reciprocal(rstd, sd), 26)
            link(dve.tensor_tensor(tmp8, rstd, rstd, ALU.mult), 27)
            link(dve.tensor_tensor(tmp8, tmp8, var, ALU.mult), 28)
            link(dve.tensor_scalar(tmp8, tmp8, -0.5, 1.5, ALU.mult, ALU.add), 29)
            link(dve.tensor_tensor(rstd, rstd, tmp8, ALU.mult), 30)
            for tau in range(NB):
                x = xn[:, tau * D:(tau + 1) * D]
                dve.tensor_scalar(x, x, mean(tau), rstd[:, tau:tau + 1], ALU.subtract,
                                  ALU.mult).then_inc(ln["normed"], 1)

        def pe_ln_back(pe, ln, xn, k):
            if k == 0:
                pe.wait_ge(ln["normed"], NB)
            if k >= 2:
                pe.wait_ge(ln["scaled"], k - 1)
            for tau in range(NB):
                mm = pe.transpose(pair(k)[:, tau * P:(tau + 1) * P],
                                  xn[:, tau * D + k * P:tau * D + (k + 1) * P], IDN[:, :])
            mm.then_inc(ln["back"], 1)

        def act_ln_scale(act, ln, which, k):
            g, b = (LNC[:, (2 * which + c) * KD + k:(2 * which + c) * KD + k + 1] for c in range(2))
            act.wait_ge(ln["back"], k + 1)
            if k >= 2:
                act.wait_ge(ln["lo"], k - 1)
            act.activation(XF[:, k % 2 * S:(k % 2 + 1) * S], pair(k)[:, :], ACT.Identity,
                           bias=b, scale=g).then_inc(ln["scaled"], 1)

        def dve_ln_split(dve, ln, k):
            f = XF[:, k % 2 * S:(k % 2 + 1) * S]
            h = XH[:, k * S:(k + 1) * S]
            dve.wait_ge(ln["scaled"], k + 1)
            dve.tensor_copy(h, f).then_inc(ln["hi"], 1)
            dve.wait_ge(ln["hi"], k + 1)
            dve.tensor_tensor(XL[:, k * S:(k + 1) * S], f, h.bitcast(F32),
                              ALU.subtract).then_inc(ln["lo"], 1)

        block = ctx.enter_context(nc.Block())

        @block.sync
        def _(sp_):
            def load(n, b, src, width=D, after_last=False, free=True):
                if free:
                    sp_.wait_ge(w_lo, n + (2 if after_last else 1))
                sp_.dma_start(WR[:, b * D:b * D + width], src).then_inc(raw[b], 16)

            for h in range(4):
                sp_.dma_start(XRAW[:, h * 2 * S:(h + 1) * 2 * S].rearrange("p (k t) -> p k t", k=2),
                              xT[2 * h:2 * h + 2].rearrange("k p t -> p k t")).then_inc(xraw[h], 16)
            with sp_.Fori(0, PAIRS) as i:
                for k in range(FOX_SLOTS):
                    load(FOX_SLOTS * i + k, k % 2, w_fox[FOX_SLOTS * i + k])
            with sp_.Fori(0, PAIRS) as i:
                for k in range(CA_SLOTS):
                    load(N_CA + CA_SLOTS * i + k, k % 2, w_ca[CA_SLOTS * i + k], after_last=(k == 0))
            sp_.wait_ge(w_lo, N_EF + 2)
            for br, (n0, src, width) in enumerate(((N_EF, w_foxo, HALF), (N_EC, w_cao, HALF),
                                                   (N_ES, w_glu, D))):
                with sp_.Fori(0, KD) as i:
                    load(n0 + 2 * i, 0, w_gate[KD * br + i])
                    load(n0 + 2 * i + 1, 1, src[i], width)
            sp_.wait_ge(o_lo["es"], 4)
            sp_.dma_start(MRAW[:, :].rearrange("p (k t) -> p k t", k=KD),
                          memT.rearrange("k p t -> p k t")).then_inc(mem_loaded, 16)
            for n0, src, count in ((N_WO, w_o, KD), (N_KV, w_kv, 2 * KD), (N_XQ, w_xq, KD),
                                   (N_XO, w_xo, KD)):
                with sp_.Fori(0, count // 2) as i:
                    for k in range(2):
                        load(n0 + 2 * i + k, k, src[2 * i + k])
            n0, t0 = N_FF, 0
            for g, tiles in enumerate(FF_GROUPS):
                with sp_.Fori(0, tiles) as i:
                    for k in range(2):
                        load(n0 + 2 * i + k, k, w_up[2 * t0 + 2 * i + k])
                n0, t0 = n0 + 2 * tiles, t0 + tiles
                with sp_.Fori(0, KD // 2) as i:
                    for k in range(2):
                        load(n0 + 2 * i + k, k, w_dn[g][2 * i + k], tiles * P)
                n0 += KD
            for tau in range(NB):
                sp_.wait_ge(final_step, 2 * tau + 2)
                sp_.dma_start(out[0, tau * P:(tau + 1) * P, :],
                              XN3[:, tau * D:(tau + 1) * D]).then_inc(out_stored, 16)
            sp_.wait_ge(out_stored, 16 * NB)

        @block.gpsimd
        def _(pool):
            pool.memset(IDN[:, :], 0.0)
            pool.memset(IDB[:, :], 0.0)
            pool.memset(CMB[:, :], 0.0)
            pool.memset(BP[:, :], 0.0)
            pool.memset(CT[:, :], 0.0).then_inc(sp, 1)
            pool.wait_ge(sp, 1)
            pool.affine_select(out=IDN[:, :], in_=IDN[:, :], compare_op=ALU.not_equal, fill=1.0,
                               base=0, pattern=[[-1, P]], channel_multiplier=1)
            pool.affine_select(out=IDB[:, :], in_=IDB[:, :], compare_op=ALU.not_equal, fill=1.0,
                               base=0, pattern=[[-1, P]], channel_multiplier=1)
            pool.affine_select(out=CMB[:, :], in_=CMB[:, :], compare_op=ALU.is_ge, fill=NEG,
                               base=0, pattern=[[-1, P]], channel_multiplier=1).then_inc(consts, 1)
            pool.engine_nop().then_inc(fox["s_summed"], 16)
            pool.engine_nop().then_inc(ca["s_summed"], 16)
            pool.engine_nop().then_inc(ca_masked, 1)
            pool.wait_ge(su, CUM_STEP)
            pool.dma_start(cum_scratch, FFE[0:8, :]).then_inc(cum_out, 16)
            pool.wait_ge(cum_out, 16)
            pool.wait_ge(w_used, 3)
            with pool.Fori(0, PAIRS) as i:
                for hh in range(2):
                    pool.wait_ge(fox["s_summed"], 16 * i + 8 * hh + 8)
                    pool.dma_start(MB[:, hh * S:(hh + 1) * S],
                                   cum_scratch[bass.ds(2 * i + hh, 1), :].partition_broadcast(P)
                                   ).then_inc(mb_loaded["fox"][hh], 16)
                for k in range(NQ + 1):
                    pool_ssm(pool, i, k)
            pool.wait_ge(h_ready, NQ * PAIRS)
            with pool.Fori(0, PAIRS) as i:
                for hh in range(2):
                    pool.wait_ge(ca["s_summed"], 16 * i + 8 * hh + 8)
                    if hh == 0:
                        pool.wait_ge(fox["s_summed"], 16 * PAIRS + 16)
                    pool.dma_start(MB[:, hh * S:hh * S + CA_KEYS],
                                   rel[2 * i + hh]
                                   ).then_inc(mb_loaded["ca"][hh], 16)
                for hh in range(2):
                    pool.wait_ge(mb_loaded["ca"][hh], 16 * i + 16)
                    pool.wait_ge(ca_masked, 4 * i + 2 * hh + 1)
                    pool.sem_inc(masks_due, 1)
                    pool.memset(MB[0:64, hh * S + CA_KEYS - 64:hh * S + CA_KEYS],
                                NEG).then_inc(ca_masked, 1)
                    pool.wait_ge(ca_masked, 4 * i + 2 * hh + 2)
                    pool.sem_inc(masks_due, 1)
                    pool.memset(MB[64:128, hh * S:hh * S + 64], NEG).then_inc(ca_masked, 1)
            pool.wait_ge(hid_lo, FF_TILES)
            pool.dma_start(LGB[:, 0:D], ln_rows[0:1, :].partition_broadcast(P)).then_inc(rows_loaded, 16)
            pool.dma_start(LGB[:, D:2 * D], ln_rows[1:2, :].partition_broadcast(P)).then_inc(rows_loaded, 16)

        @block.scalar
        def _(act):
            small = ((SP[:, 0:16], lam_re), (SP[:, 16:32], lam_im), (SP[:, 32:48], log_dt),
                     (BRAW[:, 0:256], b_re), (BRAW[:, 256:512], b_im),
                     (CRAW[:, 0:256], c_re), (CRAW[:, 256:512], c_im),
                     (DC[:, 0:4], ssm_d), (BC[:, :], b_cols), (DC[0:8, 6:7], b_ff),
                     (WFF[:, :], w_ff), (CONV[:, :], conv), (LNC[:, :], ln_cols))
            assert len(small) == N_SMALL
            for dst, src in small:
                act.dma_start(dst, src).then_inc(params, 16)
            act.wait_ge(params, 16 * N_SMALL)
            act.activation(spv(4), spv(2), ACT.Exp).then_inc(sa, 1)
            act.wait_ge(su, EXP_STEP)
            act.activation(spv(6), spv(5), ACT.Exp).then_inc(sa, 1)
            act.wait_ge(su, SIN_STEP)
            act.activation(spv(11), spv(9), ACT.Sin)
            act.activation(spv(12), spv(10), ACT.Sin).then_inc(sa, 1)
            for k in range(KD):
                act.wait_ge(xraw[k // 2], 16)
                act.activation(XH[:, k * S:(k + 1) * S], XRAW[:, k * S:(k + 1) * S],
                               ACT.Copy).then_inc(x_hi, 1)
            for n in range(2):
                act.wait_ge(raw[n], 16)
                act.activation(WH[:, n * D:(n + 1) * D], WR[:, n * D:(n + 1) * D],
                               ACT.Copy).then_inc(w_hi, 1)
            act.wait_ge(su, FFEXP_STEP)
            act.activation(FFE[0:8, :], FFE[0:8, :], ACT.Exp, scale=-1.0).then_inc(sa, 1)
            act.wait_ge(sa, 4)
            act.activation(FFE[0:8, :], FFE[0:8, :], ACT.Ln, bias=DC[0:8, 5:6]).then_inc(sa, 1)

            def attention(kind, ev, i, dst):
                act_copy_v(act, ev, i)
                act_exp(act, kind, ev, i, 0)
                for u in range(16):
                    if u % 4 == 0 and u:
                        act_copy_o(act, ev, i, u // 4 - 1, dst)
                    if u < 15:
                        act_exp(act, kind, ev, i, u + 1)
                    act_copy_turned(act, kind, ev, i, u)
                act_copy_o(act, ev, i, 3, dst)

            with act.Fori(0, PAIRS) as i:
                for k, dst in enumerate((US, QT, KT, VT)):
                    n = FOX_SLOTS * i + k
                    act.wait_ge(w_used, n + 3)
                    if k == 0:
                        act.wait_ge(y_done, NQ * i + 1)
                    act.activation(dst[:, :], pair(k)[:, :], ACT.Identity,
                                   bias=BC[:, bass.ds(FOX_SLOTS * i + k, 1)],
                                   scale=0.125 if dst is QT else 1.0).then_inc(fox["proj_ready"], 1)
                    split_hi(act, n + 2, k % 2, 2 * i + (k + 2) // 2 + 1)
                attention("fox", fox, i, OF)
            with act.Fori(0, PAIRS) as i:
                for k, dst in enumerate((QT, KT, VT)):
                    n = N_CA + CA_SLOTS * i + k
                    act.wait_ge(w_used, n + 3)
                    act.activation(dst[:, :], pair(k)[:, :], ACT.Identity,
                                   bias=BC[:, bass.ds(16 + CA_SLOTS * i + k, 1)],
                                   scale=0.125 if dst is QT else 1.0).then_inc(ca["proj_ready"], 1)
                    if k == 0:
                        split_hi(act, n + 2, 0, 2 * PAIRS + 2 * i + 2)
                n = N_CA + CA_SLOTS * i + CA_SLOTS
                split_hi(act, n, 0, 2 * PAIRS + 2 * i + 3, after_last=True)
                split_hi(act, n + 1, 1, 2 * PAIRS + i + 2)
                attention("ca", ca, i, OC)

            for t, n0, br, src in (("ef", N_EF, 0, OF), ("ec", N_EC, 1, OC), ("es", N_ES, 2, YS)):
                if t == "es":
                    for c in range(4):
                        act.activation(YS[:, c * S:(c + 1) * S], YS[:, c * S:(c + 1) * S],
                                       ACT.Gelu_apprx_tanh).then_inc(y_act, 1)
                    act.wait_ge(y_act, 4)
                act.wait_ge(w_used, n0 + 2)
                if t == "ef":
                    act.wait_ge(ca["o_copied"], 4 * PAIRS)
                for c in range(4):
                    act.activation(OH[:, c * S:(c + 1) * S], src[:, c * S:(c + 1) * S],
                                   ACT.Copy).then_inc(o_hi[t], 1)
                gate = GS if t == "es" else GF
                if t == "ec":
                    act.wait_ge(m_step["ef"], KD + 1)
                with act.Fori(0, KD) as i:
                    n = n0 + 2 * i
                    act.wait_ge(w_used, n + 3)
                    if t == "ef":
                        act.wait_ge(o_lo[t], 4)
                        act.wait_ge(m_step["ef"], i + 1)
                    elif t == "ec":
                        act.wait_ge(m_step["ec"], 2 * i + 1)
                    else:
                        act.wait_ge(o_lo[t], 4)
                        act.wait_ge(m_step["es"], 3 * i + 1)
                    act.activation(gate[:, :], PA[:, :], ACT.Sigmoid,
                                   bias=BC[:, bass.ds(28 + KD * br + i, 1)]).then_inc(g_ready[t], 1)
                    split_hi(act, n + 2, 0, i + (rc(n0, 2)))
                    if t == "es":
                        act.wait_ge(w_used, n + 4)
                        act.activation(G2[:, :], TB[:, :], ACT.Sigmoid).then_inc(g_ready[t], 1)
                        split_hi(act, n + 3, 1, i + rc(n0, 3))
                        act.wait_ge(m_step["es"], 3 * i + 4)
                        act.activation(MH[:, bass.ds(i * S, S)], MT[:, bass.ds(i * S, S)],
                                       ACT.Copy).then_inc(m_hi, 1)
                    else:
                        split_hi(act, n + 3, 1, i + rc(n0, 3))

            act.wait_ge(mem_loaded, 16)

            def ring_only(n0, count):
                with act.Fori(0, count) as i:
                    for k in range(2):
                        split_hi(act, n0 + 2 * i + k + 2, k, i + rc(n0, k + 2))

            ring_only(N_WO, KD // 2)
            act.wait_ge(w_used, N_WO + KD + 2)
            act.activation(MMH[:, :], MRAW[:, :], ACT.Copy).then_inc(mem_hi, 1)

            def kv_slot(j):
                n = N_KV + j
                bank = (OB, XB)[j % 2][:, 0:MEM]
                act.wait_ge(w_used, n + 3)
                if j < KD:
                    dst = KM[:, j * MEM:(j + 1) * MEM]
                else:
                    dst = VMT[:, j % 2 * MEM:(j % 2 + 1) * MEM]
                    if j >= KD + 2:
                        act.wait_ge(v_turned, j - KD - 1)
                act.activation(dst, bank, ACT.Copy).then_inc(kv_ready, 1)
                split_hi(act, n + 2, j % 2, rc(N_KV, j + 2))

            def copy_mem_v(j):
                act.wait_ge(v_turned, j + 1)
                act.activation(VM[:, :].rearrange("p (c f) -> p c f", c=2)[:, :, j * P:(j + 1) * P],
                               TB[:, j % 2 * HALF:j % 2 * HALF + MEM].rearrange("p (c f) -> p c f", c=2),
                               ACT.Copy).then_inc(v_ready, 1)

            for tau in range(NB):
                act_ln_copy(act, lns[0], XN1, tau)
                kv_slot(tau)
            act_ln_sqrt(act, lns[0])
            for k in range(KD):
                kv_slot(KD + k)
                act_ln_scale(act, lns[0], 0, k)
                copy_mem_v(k)

            with act.Fori(0, XH_HEADS) as i:
                for k in range(2):
                    n = N_XQ + 2 * i + k
                    act.wait_ge(w_used, n + 3)
                    act.activation(QX[:, k * S:(k + 1) * S], pair(k)[:, :], ACT.Copy,
                                   scale=0.0625).then_inc(xa["q_ready"], 1)
                    split_hi(act, n + 2, k, i + rc(N_XQ, k + 2))
                act.activation(VX[:, :].rearrange("p (c f) -> p c f", c=2),
                               VM[:, :].rearrange("p (c f) -> p c f", c=2)[:, :, bass.ds(i * MEM, MEM)],
                               ACT.Copy).then_inc(xa["v_staged"], 1)

                def x_exp(u):
                    act.wait_ge(xa["nmax"], 8 * i + u + 1)
                    act.activation(SX[:, u % 2 * MEM:(u % 2 + 1) * MEM],
                                   TB[:, u % 2 * HALF:u % 2 * HALF + MEM], ACT.Exp,
                                   bias=MX[:, 2 + u % 2:3 + u % 2],
                                   accum_out=MX[:, 4 + u % 2:5 + u % 2]).then_inc(xa["exp"], 1)

                def x_copy(u):
                    act.wait_ge(xa["t_ready"], 8 * i + u + 1)
                    g, q = divmod(u, 4)
                    act.activation(
                        PTX[:, g * 2 * HALF:(g + 1) * 2 * HALF].rearrange("p (c t) -> p c t", c=2)[
                            :, :, q * P:(q + 1) * P],
                        (XB, OB)[u % 2][:, 0:MEM].rearrange("p (c t) -> p c t", c=2),
                        ACT.Copy).then_inc(xa["t_copied"], 1)

                def x_hi_part(g):
                    act.wait_ge(xa["pv"], 2 * i + g + 1)
                    for c in range(2):
                        act.activation(OHX[:, bass.ds(i * 2 * S + c * S + g * HALF, HALF)],
                                       pair(g)[:, c * HALF:(c + 1) * HALF],
                                       ACT.Copy).then_inc(xa["hi"], 1)

                x_exp(0)
                for u in range(8):
                    if u < 7:
                        x_exp(u + 1)
                    x_copy(u)
                    if u == 4:
                        x_hi_part(0)
                x_hi_part(1)

            ring_only(N_XO, KD // 2)
            for tau in range(NB):
                act_ln_copy(act, lns[1], XN2, tau)
            act_ln_sqrt(act, lns[1])
            for k in range(KD):
                act_ln_scale(act, lns[1], 1, k)
                act.wait_ge(lns[1]["scaled"], k + 1)
                act.activation(YT[:, k * S:(k + 1) * S], XF[:, k % 2 * S:(k % 2 + 1) * S], ACT.Copy,
                               scale=ALPHA).then_inc(lns[1]["sqrt"], 1)

            act.wait_ge(lns[1]["sqrt"], 1 + KD)
            act.preload_act_table(ACT.Gelu_apprx_tanh)
            n0, t0 = N_FF, 0
            for g, tiles in enumerate(FF_GROUPS):
                with act.Fori(0, tiles) as i:
                    n = n0 + 2 * i
                    split_hi(act, n + 2, 0, i + rc(n0, 2))
                    act.wait_ge(cv_step, 3 * (t0 + i) + 3)
                    act.activation(GL[:, :], CV[:, :], ACT.Gelu_apprx_tanh).then_inc(gelu_done, 1)
                    split_hi(act, n + 3, 1, i + rc(n0, 3))
                    act.wait_ge(hid, t0 + i + 1)
                    act.activation(HDH[:, bass.ds(i * S, S)], HF[:, :], ACT.Copy).then_inc(hid_hi, 1)
                n0, t0 = n0 + 2 * tiles, t0 + tiles
                last = g == len(FF_GROUPS) - 1
                ring_only(n0, KD // 2 - (1 if last else 0))
                n0 += KD
            for tau in range(NB):
                act_ln_copy(act, lns[2], XN3, tau)
            act_ln_sqrt(act, lns[2])

        @block.tensor
        def _(pe):
            pe.wait_ge(params, 16 * N_SMALL)
            for k in range(KD):
                pe.wait_ge(xraw[k // 2], 16)
                for t in range(2):
                    mm = pe.matmul(PA[0:8, t * HALF:(t + 1) * HALF], WFF[:, 8 * k:8 * k + 8],
                                   XRAW[:, k * S + t * HALF:k * S + (t + 1) * HALF],
                                   start=(k == 0), stop=(k == KD - 1))
            mm.then_inc(st_pe, 1)
            pe.wait_ge(consts, 1)
            pe.wait_ge(su, BP_STEP)
            for t in range(4):
                for c in range(2):
                    mm = pe.transpose(PB[:, (2 * t + c) * P:(2 * t + c + 1) * P],
                                      BP[:, c * 512 + t * P:c * 512 + (t + 1) * P], IDN[:, :])
            mm.then_inc(st_pe, 1)
            pe.nop().then_inc(w_used, 2)
            pe.wait_ge(x_lo, KD)
            pe.wait_ge(su, FFEXP_STEP)
            pe.wait_ge(su, BT_STEP)

            with pe.Fori(0, PAIRS) as i:
                pos = 0
                for k in range(FOX_SLOTS):
                    n = FOX_SLOTS * i + k
                    if k >= 2:
                        pe.wait_ge(fox["proj_ready"], 4 * i + k - 1)
                    if k == 0:
                        product(pe, n, 0, PA, XH, XL).then_inc(w_used, 1)
                        pe_ssm(pe, i, 0)
                    else:
                        product(pe, n, k % 2, pair(k), XH, XL, part=0)
                        pe_ssm(pe, i, 2 * k - 1)
                        product(pe, n, k % 2, pair(k), XH, XL, part=1).then_inc(w_used, 1)
                        pe_ssm(pe, i, 2 * k)
                pe_turn_v(pe, fox, 4, 3, i)
                pe_scores(pe, "fox", fox, 0)
                pe_ssm(pe, i, 7)
                pe_scores(pe, "fox", fox, 1)
                pe_ssm(pe, i, 8)
                for u in range(16):
                    pe_transposes(pe, "fox", fox, i, u)
                    p = SSM_POS[u]
                    pe_ssm(pe, i, p[0])
                    if u < 14:
                        pe_scores(pe, "fox", fox, u + 2)
                    if len(p) > 1:
                        pe_ssm(pe, i, p[1])
                    pe_values(pe, "fox", fox, i, u)
            with pe.Fori(0, PAIRS) as i:
                for k in range(CA_SLOTS):
                    n = N_CA + CA_SLOTS * i + k
                    if k == 2:
                        pe.wait_ge(ca["proj_ready"], 3 * i + 1)
                    product(pe, n, k % 2, pair(k), XH, XL).then_inc(w_used, 1)
                pe.wait_ge(ca["proj_ready"], 3 * i + 2)
                pe_turn_v(pe, ca, 3, 2, i)
                pe_scores(pe, "ca", ca, 0)
                pe_scores(pe, "ca", ca, 1)
                for u in range(16):
                    pe_transposes(pe, "ca", ca, i, u)
                    if u < 14:
                        pe_scores(pe, "ca", ca, u + 2)
                    pe_values(pe, "ca", ca, i, u)

            for t, n0 in (("ef", N_EF), ("ec", N_EC), ("es", N_ES)):
                with pe.Fori(0, KD) as i:
                    n = n0 + 2 * i
                    product(pe, n, 0, PA, XH, XL).then_inc(w_used, 1)
                    pe.wait_ge(o_lo[t], 4)
                    if t == "es":
                        product(pe, n + 1, 1, PB, OH, OL, nk=4)
                        product(pe, n + 1, 1, TB, OH, OL, nk=4, k0=4).then_inc(w_used, 1)
                    else:
                        product(pe, n + 1, 1, PB, OH, OL, nk=4).then_inc(w_used, 1)
            pe.wait_ge(m_lo, KD)

            def dense(n0, xh, xl, nk=KD):
                with pe.Fori(0, KD // 2) as i:
                    for k in range(2):
                        product(pe, n0 + 2 * i + k, k, pair(k), xh, xl, nk=nk).then_inc(w_used, 1)

            dense(N_WO, MH, ML)
            pe.wait_ge(mem_lo, 1)

            def kv_slot(j):
                if j >= 2:
                    pe.wait_ge(kv_ready, j - 1)
                product(pe, N_KV + j, j % 2, (OB, XB)[j % 2], MMH, MML, width=MEM).then_inc(w_used, 1)

            for tau in range(NB):
                pe_ln_forward(pe, lns[0], RT1, tau, (rt_step["wo"], 2 * KD))
                kv_slot(tau)
            for k in range(KD):
                kv_slot(KD + k)
                pe_ln_back(pe, lns[0], XN1, k)
                pe.wait_ge(kv_ready, KD + k + 1)
                if k >= 2:
                    pe.wait_ge(v_ready, k - 1)
                for c in range(2):
                    mm = pe.transpose(TB[:, k % 2 * HALF + c * P:k % 2 * HALF + (c + 1) * P],
                                      VMT[:, k % 2 * MEM + c * P:k % 2 * MEM + (c + 1) * P], IDN[:, :])
                mm.then_inc(v_turned, 1)
            pe.wait_ge(lns[0]["lo"], KD)
            pe.wait_ge(v_ready, KD)

            with pe.Fori(0, XH_HEADS) as i:
                for k in range(2):
                    product(pe, N_XQ + 2 * i + k, k, pair(k), XH, XL).then_inc(w_used, 1)
                pe.wait_ge(xa["q_ready"], 2 * i + 2)
                pe.wait_ge(xa["v_staged"], i + 1)

                def scores(u):
                    for c in range(2):
                        mm = pe.matmul(TB[:, u % 2 * HALF:u % 2 * HALF + MEM],
                                       QX[:, c * S + u * P:c * S + (u + 1) * P],
                                       KM[:, bass.ds(i * 2 * MEM + c * MEM, MEM)],
                                       start=(c == 0), stop=(c == 1))
                    mm.then_inc(xa["s_ready"], 1)

                scores(0)
                scores(1)
                for u in range(8):
                    pe.wait_ge(xa["p_ready"], 8 * i + u + 1)
                    if u >= 2:
                        pe.wait_ge(xa["t_copied"], 8 * i + u - 1)
                    for c in range(2):
                        mm = pe.transpose((XB, OB)[u % 2][:, c * P:(c + 1) * P],
                                          SX[:, u % 2 * MEM + c * P:u % 2 * MEM + (c + 1) * P], IDN[:, :])
                    mm.then_inc(xa["t_ready"], 1)
                    if u < 6:
                        scores(u + 2)
                    if u in (4, 7):
                        g = u // 5
                        pe.wait_ge(xa["t_copied"], 8 * i + 4 * g + 4)
                        for c2 in range(2):
                            for c in range(2):
                                mm = pe.matmul(pair(g)[:, c2 * HALF:(c2 + 1) * HALF],
                                               VX[:, c * MEM + c2 * P:c * MEM + (c2 + 1) * P],
                                               PTX[:, (2 * g + c) * HALF:(2 * g + c + 1) * HALF],
                                               start=(c == 0), stop=(c == 1))
                        mm.then_inc(xa["pv"], 1)
                pe.wait_ge(xa["lo"], 4 * i + 4)
            dense(N_XO, OHX, OLX)
            for tau in range(NB):
                pe_ln_forward(pe, lns[1], RT2, tau, (rt_step["xo"], 2 * KD))
            for k in range(KD):
                pe_ln_back(pe, lns[1], XN2, k)
            pe.wait_ge(lns[1]["lo"], KD)

            n0, t0 = N_FF, 0
            for g, tiles in enumerate(FF_GROUPS):
                with pe.Fori(0, tiles) as i:
                    for k in range(2):
                        product(pe, n0 + 2 * i + k, k, pair(k), XH, XL).then_inc(w_used, 1)
                n0, t0 = n0 + 2 * tiles, t0 + tiles
                pe.wait_ge(hid_lo, t0)
                dense(n0, HDH, HDL, nk=tiles)
                n0 += KD
            for tau in range(NB):
                pe_ln_forward(pe, lns[2], YT, tau, (y_sum, len(FF_GROUPS) * KD))

        @block.vector
        def _(dve):
            chain = [0]

            def link(ins):
                chain[0] += 1
                ins.then_inc(su, 1)
                dve.wait_ge(su, chain[0])

            v = spv
            E = lambda c, m: PRM[:, :].rearrange("p (t n) -> p t n", n=NPRM)[:, :, 8 * c + m]
            TT, TS, STT = dve.tensor_tensor, dve.tensor_scalar, dve.scalar_tensor_tensor

            dve.memset(DC[:, 5:6], 1.0).then_inc(su, 1)
            chain[0] += 1
            dve.wait_ge(params, 16 * N_SMALL)
            link(TS(v(3), v(0), -1e-4, None, ALU.min))
            dve.wait_ge(sa, 1)
            link(TT(v(5), v(3), v(4), ALU.mult))
            assert chain[0] == EXP_STEP
            link(TT(v(7), v(1), v(4), ALU.mult))
            link(TS(v(8), v(7), 1.0 / TWO_PI, RND, ALU.mult, ALU.add))
            link(TS(v(8), v(8), -RND, None, ALU.add))
            link(STT(v(9), v(8), -PI_A, v(7), ALU.mult, ALU.add))
            link(STT(v(9), v(8), -PI_B, v(9), ALU.mult, ALU.add))
            link(STT(v(9), v(8), -PI_C, v(9), ALU.mult, ALU.add))
            link(TS(v(9), v(9), 0.5, -1.5707963, ALU.mult, ALU.max))
            link(TS(v(9), v(9), 1.5707963, None, ALU.min))
            link(STT(v(10), v(9), -1.0, v(9), ALU.mult, ALU.max))
            link(TS(v(10), v(10), -1.0, 1.5707963267948966, ALU.mult, ALU.add))
            link(TS(v(10), v(10), 0.0, None, ALU.max))
            assert chain[0] == SIN_STEP
            dve.wait_ge(sa, 3)
            link(TT(v(13), v(11), v(11), ALU.mult))
            link(TS(E(0, 0), v(13), -2.0, 1.0, ALU.mult, ALU.add))
            link(STT(E(1, 0), v(11), 2.0, v(12), ALU.mult, ALU.mult))

            def unit(c, s):
                link(TT(v(16), c, c, ALU.mult))
                link(TT(v(17), s, s, ALU.mult))
                link(TT(v(16), v(16), v(17), ALU.add))
                link(TS(v(16), v(16), -0.5, 1.5, ALU.mult, ALU.add))
                link(TT(c, c, v(16), ALU.mult))
                link(TT(s, s, v(16), ALU.mult))

            unit(E(0, 0), E(1, 0))
            link(TT(v(14), v(6), E(0, 0), ALU.mult))
            link(TS(v(14), v(14), -1.0, None, ALU.add))
            link(TT(v(15), v(6), E(1, 0), ALU.mult))
            link(TT(v(16), v(3), v(3), ALU.mult))
            link(TT(v(17), v(1), v(1), ALU.mult))
            link(TT(v(16), v(16), v(17), ALU.add))
            link(dve.reciprocal(v(18), v(16)))
            link(TT(v(16), v(14), v(3), ALU.mult))
            link(TT(v(17), v(15), v(1), ALU.mult))
            link(TT(v(16), v(16), v(17), ALU.add))
            link(TT(v(19), v(16), v(18), ALU.mult))
            link(TT(v(16), v(15), v(3), ALU.mult))
            link(TT(v(17), v(14), v(1), ALU.mult))
            link(TT(v(16), v(16), v(17), ALU.subtract))
            link(TT(v(20), v(16), v(18), ALU.mult))
            gb = lambda a: v(a).unsqueeze(2).to_broadcast([P, 16, 16])
            t3 = lambda a: a.rearrange("p (t c) -> p t c", t=16)
            br, bi = t3(BRAW[:, 0:256]), t3(BRAW[:, 256:512])
            dve.wait_ge(sp, 1)
            for c, (x1, x2, op) in enumerate(((br, bi, ALU.subtract), (bi, br, ALU.add))):
                link(TT(t3(BTMP[:, 0:256]), x2, gb(20), ALU.mult))
                link(TT(t3(BBAR[:, c * 256:(c + 1) * 256]), x1, gb(19), ALU.mult))
                for g in range(2):
                    r = slice(64 * g, 64 * g + 64)
                    link(TT(BP[r, c * 512:(c + 1) * 512].rearrange("p (t c) -> p t c", t=16)[
                                :, :, 16 * g:16 * g + 16],
                            t3(BBAR[r, c * 256:(c + 1) * 256]), t3(BTMP[r, 0:256]), op))
                    link(TS(CT[r, :].rearrange("p (t q c) -> p t q c", t=16, q=2)[
                                :, :, c, 16 * g:16 * g + 16],
                            t3(CRAW[r, c * 256:(c + 1) * 256]), 1.0 - 2.0 * c, None, ALU.mult))
            assert chain[0] == BP_STEP, chain[0]
            link(dve.tensor_copy(PRM[:, :].rearrange("p (t n) -> p t n", n=NPRM)[:, :, 24], v(6)))
            for m in range(1, 8):
                c, s = E(0, m - 1), E(1, m - 1)
                link(TT(v(16), c, c, ALU.mult))
                link(TT(v(17), s, s, ALU.mult))
                link(TT(E(0, m), v(16), v(17), ALU.subtract))
                link(STT(E(1, m), c, 2.0, s, ALU.mult, ALU.mult))
                unit(E(0, m), E(1, m))
            pr = PRM[:, :].rearrange("p (t n) -> p t n", n=NPRM)
            link(TS(pr[:, :, 16:24], pr[:, :, 8:16], -1.0, None, ALU.mult))
            w16 = W16[:, :].rearrange("p (t c n) -> p t c n", t=16, c=2)
            link(dve.tensor_copy(w16[:, :, 0, 0:1], pr[:, :, 0:1]))
            link(dve.tensor_copy(w16[:, :, 1, 0:1], pr[:, :, 8:9]))
            for m in range(4):
                n = 2 ** m
                wt = lambda c: W16T[:, c * 256:c * 256 + 16 * n].rearrange("p (t n) -> p t n", n=n)
                eb = lambda c: pr[:, :, 8 * c + m:8 * c + m + 1].to_broadcast([P, 16, n])
                wr, wi = w16[:, :, 0, 0:n], w16[:, :, 1, 0:n]
                link(TT(wt(0), wr, eb(0), ALU.mult))
                link(TT(wt(1), wi, eb(1), ALU.mult))
                link(TT(w16[:, :, 0, n:2 * n], wt(0), wt(1), ALU.subtract))
                link(TT(wt(0), wr, eb(1), ALU.mult))
                link(TT(wt(1), wi, eb(0), ALU.mult))
                link(TT(w16[:, :, 1, n:2 * n], wt(0), wt(1), ALU.add))
            link(TS(BC[:, 1:17:4], BC[:, 1:17:4], 0.125, None, ALU.mult))
            link(TS(BC[:, 16:28:3], BC[:, 16:28:3], 0.125, None, ALU.mult))
            for k in range(KD):
                dve.wait_ge(x_hi, k + 1)
                dve.tensor_tensor(XL[:, k * S:(k + 1) * S], XRAW[:, k * S:(k + 1) * S],
                                  XH[:, k * S:(k + 1) * S].bitcast(F32), ALU.subtract).then_inc(x_lo, 1)
            dve.engine_nop().then_inc(w_lo, 2)
            split_lo(dve, 0, 0)
            split_lo(dve, 1, 1)
            dve.wait_ge(st_pe, 2)
            link(dve.tensor_copy(BT[:, :], PB[:, :]))
            assert chain[0] == BT_STEP, chain[0]
            link(TS(FFB[0:8, :], PA[0:8, :], DC[0:8, 6:7], None, ALU.add))
            link(STT(FFE[0:8, :], FFB[0:8, :], -1.0, FFB[0:8, :], ALU.mult, ALU.max))
            assert chain[0] == FFEXP_STEP, chain[0]
            link(TS(FFB[0:8, :], FFB[0:8, :], 0.0, None, ALU.min))
            dve.wait_ge(sa, 5)
            link(TT(FFB[0:8, :], FFB[0:8, :], FFE[0:8, :], ALU.subtract))
            link(dve.tensor_tensor_scan(FFE[0:8, :], DC[0:8, 5:6].to_broadcast([8, S]), FFB[0:8, :],
                                        0.0, ALU.mult, ALU.subtract))
            assert chain[0] == CUM_STEP, chain[0]
            dve.engine_nop().then_inc(y_done, 1)
            dve.engine_nop().then_inc(m_step["ef"], 1)
            dve.engine_nop().then_inc(m_step["ec"], 1)
            dve.engine_nop().then_inc(m_step["es"], 1)

            def ssm_group(i, k):
                dve_ssm(dve, i, k)
                if k in (2, 6, 10):
                    dve.wait_ge(yadd, 2 * NQ * i + 2 * k + 2)
                    dve_table(dve, i, k // 4 + 1)

            dve.wait_ge(cum_out, 16)
            with dve.Fori(0, PAIRS) as i:
                dve_stage(dve, i)
                dve.wait_ge(staged, 4 * i + 4)
                dve_table(dve, i, 0)
                split_lo(dve, FOX_SLOTS * i + 2, 0)
                ssm_group(i, 0)
                ssm_group(i, 1)
                split_lo(dve, FOX_SLOTS * i + 3, 1)
                ssm_group(i, 2)
                split_lo(dve, FOX_SLOTS * i + 4, 0)
                ssm_group(i, 3)
                split_lo(dve, FOX_SLOTS * i + 5, 1)
                dve_rowmax(dve, "fox", fox, i, 0)
                ssm_group(i, 4)
                for u in range(16):
                    if u < 15:
                        dve_rowmax(dve, "fox", fox, i, u + 1)
                    dve_normalise(dve, "fox", fox, i, u)
                    for p in SSM_POS[u]:
                        if p % 2:
                            ssm_group(i, (p + 1) // 2)
                ssm_group(i, NQ + 1)
            with dve.Fori(0, PAIRS) as i:
                n = N_CA + CA_SLOTS * i
                split_lo(dve, n + 2, 0)
                split_lo(dve, n + 3, 0)
                split_lo(dve, n + 4, 1)
                dve_rowmax(dve, "ca", ca, i, 0)
                for u in range(16):
                    if u < 15:
                        dve_rowmax(dve, "ca", ca, i, u + 1)
                    dve_normalise(dve, "ca", ca, i, u)

            for t, n0, src in (("ef", N_EF, OF), ("ec", N_EC, OC), ("es", N_ES, YS)):
                for c in range(4):
                    dve.wait_ge(o_hi[t], c + 1)
                    dve.tensor_tensor(OL[:, c * S:(c + 1) * S], src[:, c * S:(c + 1) * S],
                                      OH[:, c * S:(c + 1) * S].bitcast(F32),
                                      ALU.subtract).then_inc(o_lo[t], 1)
                with dve.Fori(0, KD) as i:
                    n = n0 + 2 * i
                    split_lo(dve, n + 2, 0)
                    mt = MT[:, bass.ds(i * S, S)]
                    dve.wait_ge(w_used, n + 4)
                    if t == "ef":
                        dve.wait_ge(g_ready[t], i + 1)
                        dve.tensor_tensor(mt, PB[:, :], GF[:, :], ALU.mult).then_inc(m_step[t], 1)
                    elif t == "ec":
                        dve.wait_ge(g_ready[t], i + 1)
                        dve.tensor_tensor(GF[:, :], PB[:, :], GF[:, :], ALU.mult).then_inc(m_step[t], 1)
                        dve.wait_ge(m_step[t], 2 * i + 2)
                        dve.tensor_tensor(mt, mt, GF[:, :], ALU.add).then_inc(m_step[t], 1)
                    else:
                        dve.wait_ge(g_ready[t], 2 * i + 2)
                        dve.tensor_tensor(GS[:, :], PB[:, :], GS[:, :], ALU.mult).then_inc(m_step[t], 1)
                        dve.wait_ge(m_step[t], 3 * i + 2)
                        dve.tensor_tensor(GS[:, :], GS[:, :], G2[:, :], ALU.mult).then_inc(m_step[t], 1)
                        dve.wait_ge(m_step[t], 3 * i + 3)
                        dve.tensor_tensor(mt, mt, GS[:, :], ALU.add).then_inc(m_step[t], 1)
                    split_lo(dve, n + 3, 1)
                    if t == "es":
                        dve.wait_ge(m_hi, i + 1)
                        dve.tensor_tensor(ML[:, bass.ds(i * S, S)], mt,
                                          MH[:, bass.ds(i * S, S)].bitcast(F32),
                                          ALU.subtract).then_inc(m_lo, 1)

            def residual(tag):
                rt, n0 = RES[tag]
                with dve.Fori(0, KD // 2) as i:
                    for k in range(2):
                        n = n0 + 2 * i + k
                        sl = bass.ds(i * 2 * S + k * S, S)
                        dve.wait_ge(w_used, n + 3)
                        dve.scalar_tensor_tensor(rt[:, sl], XH[:, sl].bitcast(F32), ALPHA, pair(k)[:, :],
                                                 ALU.mult, ALU.add).then_inc(rt_step[tag], 1)
                        split_lo(dve, n + 2, k)
                        dve.wait_ge(rt_step[tag], 4 * i + 2 * k + 1)
                        dve.scalar_tensor_tensor(rt[:, sl], XL[:, sl].bitcast(F32), ALPHA, rt[:, sl],
                                                 ALU.mult, ALU.add).then_inc(rt_step[tag], 1)

            residual("wo")
            dve.wait_ge(mem_hi, 1)
            dve.tensor_tensor(MML[:, :], MRAW[:, :], MMH[:, :].bitcast(F32),
                              ALU.subtract).then_inc(mem_lo, 1)
            for tau in range(NB):
                dve_ln_stats(dve, lns[0], XN1, tau)
                split_lo(dve, N_KV + tau + 2, tau % 2)
            dve_ln_normalise(dve, lns[0], XN1)
            for k in range(KD):
                split_lo(dve, N_KV + KD + k + 2, k % 2)
                dve_ln_split(dve, lns[0], k)

            with dve.Fori(0, XH_HEADS) as i:
                for k in range(2):
                    split_lo(dve, N_XQ + 2 * i + k + 2, k)

                def x_max(u):
                    b = u % 2
                    dve.wait_ge(xa["s_ready"], 8 * i + u + 1)
                    dve.reduce_max(MX[:, b:b + 1], TB[:, b * HALF:b * HALF + MEM],
                                   mybir.AxisListType.X).then_inc(xa["max"], 1)
                    dve.wait_ge(xa["max"], 8 * i + u + 1)
                    dve.tensor_scalar(MX[:, 2 + b:3 + b], MX[:, b:b + 1], -1.0, None,
                                      ALU.mult).then_inc(xa["nmax"], 1)

                def x_norm(u):
                    b = u % 2
                    dve.wait_ge(xa["exp"], 8 * i + u + 1)
                    dve.reciprocal(MX[:, 6 + b:7 + b], MX[:, 4 + b:5 + b]).then_inc(xa["rsum"], 1)
                    dve.wait_ge(xa["rsum"], 8 * i + u + 1)
                    x = SX[:, b * MEM:(b + 1) * MEM]
                    dve.tensor_scalar(x, x, MX[:, 6 + b:7 + b], None, ALU.mult).then_inc(xa["p_ready"], 1)

                def x_lo_part(g):
                    for c in range(2):
                        sl = bass.ds(i * 2 * S + c * S + g * HALF, HALF)
                        dve.wait_ge(xa["hi"], 4 * i + 2 * g + c + 1)
                        dve.tensor_tensor(OLX[:, sl], pair(g)[:, c * HALF:(c + 1) * HALF],
                                          OHX[:, sl].bitcast(F32), ALU.subtract).then_inc(xa["lo"], 1)

                x_max(0)
                for u in range(8):
                    if u < 7:
                        x_max(u + 1)
                    x_norm(u)
                    if u == 6:
                        x_lo_part(0)
                x_lo_part(1)

            residual("xo")
            for tau in range(NB):
                dve_ln_stats(dve, lns[1], XN2, tau)
            dve_ln_normalise(dve, lns[1], XN2)
            for k in range(KD):
                dve_ln_split(dve, lns[1], k)

            dve.wait_ge(lns[1]["sqrt"], 1 + KD)
            n0, t0 = N_FF, 0
            for g, tiles in enumerate(FF_GROUPS):
                with dve.Fori(0, tiles) as i:
                    n = n0 + 2 * i
                    col = lambda m: CONV[:, bass.ds(4 * t0 + 4 * i + m, 1)]
                    dve.wait_ge(w_used, n + 3)
                    if g == 0:
                        pass
                    dve.tensor_scalar(CV[:, :], PA[:, :], col(2), col(3), ALU.mult,
                                      ALU.add).then_inc(cv_step, 1)
                    dve.wait_ge(cv_step, 3 * (t0 + i) + 1)
                    dve.scalar_tensor_tensor(CV[:, 1:S], PA[:, 0:S - 1], col(1), CV[:, 1:S], ALU.mult,
                                             ALU.add).then_inc(cv_step, 1)
                    dve.wait_ge(cv_step, 3 * (t0 + i) + 2)
                    dve.scalar_tensor_tensor(CV[:, 2:S], PA[:, 0:S - 2], col(0), CV[:, 2:S], ALU.mult,
                                             ALU.add).then_inc(cv_step, 1)
                    split_lo(dve, n + 2, 0)
                    dve.wait_ge(w_used, n + 4)
                    dve.wait_ge(gelu_done, t0 + i + 1)
                    dve.tensor_tensor(HF[:, :], PB[:, :], GL[:, :], ALU.mult).then_inc(hid, 1)
                    split_lo(dve, n + 3, 1)
                    dve.wait_ge(hid_hi, t0 + i + 1)
                    dve.tensor_tensor(HDL[:, bass.ds(i * S, S)], HF[:, :],
                                      HDH[:, bass.ds(i * S, S)].bitcast(F32),
                                      ALU.subtract).then_inc(hid_lo, 1)
                n0, t0 = n0 + 2 * tiles, t0 + tiles
                last = g == len(FF_GROUPS) - 1

                def down(i, split):
                    for k in range(2):
                        n = n0 + 2 * i + k
                        yt = YT[:, bass.ds(i * 2 * S + k * S, S)]
                        dve.wait_ge(w_used, n + 3)
                        dve.tensor_tensor(yt, pair(k)[:, :], yt, ALU.add).then_inc(y_sum, 1)
                        if split:
                            split_lo(dve, n + 2, k)

                with dve.Fori(0, KD // 2 - (1 if last else 0)) as i:
                    down(i, True)
                if last:
                    down(KD // 2 - 1, False)
                n0 += KD
            for tau in range(NB):
                dve_ln_stats(dve, lns[2], XN3, tau)
            dve_ln_normalise(dve, lns[2], XN3)
            dve.wait_ge(rows_loaded, 32)
            for tau in range(NB):
                x = XN3[:, tau * D:(tau + 1) * D]
                dve.wait_ge(lns[2]["normed"], tau + 1)
                dve.tensor_tensor(x, x, LGB[:, 0:D], ALU.mult).then_inc(final_step, 1)
                dve.wait_ge(final_step, 2 * tau + 1)
                dve.tensor_tensor(x, x, LGB[:, D:2 * D], ALU.add).then_inc(final_step, 1)


SSM_POS = []
_p = 9
for _u in range(16):
    _n = 2 - _u % 2
    SSM_POS.append(tuple(range(_p, _p + _n)))
    _p += _n
assert _p == 33


def kernel(**inputs):
    import numpy as np
    import concourse.bacc as bacc
    from concourse.bass_utils import run_bass_kernel_spmd

    g = {k: np.asarray(v) for k, v in inputs.items()}
    chunks = lambda a: a.reshape(-1, P, a.shape[-1])

    def tiles(w):
        k, m = w.shape
        return w.reshape(k // P, P, m // P, P).transpose(2, 1, 0, 3).reshape(m // P, P, k)

    w_in, b_in = g["w_in"][0], g["b_in"][0]
    cuts = np.cumsum([0, 512, 512, 512, 8, 512, 512, 512, 512, 1024, 1024, 1024])
    part = {n: (w_in[:, a:b], b_in[a:b]) for n, a, b in
            zip(("fq", "fk", "fv", "ff", "su", "cq", "ck", "cv", "gf", "gs", "gc"), cuts, cuts[1:])}
    wt = {n: tiles(w) for n, (w, _) in part.items() if n != "ff"}
    bt = {n: b.reshape(-1, P) for n, (_, b) in part.items() if n != "ff"}
    inter = lambda d, names: np.stack([d[n] for n in names], 1).reshape((-1,) + d[names[0]].shape[1:])
    fox, ca = ("su", "fq", "fk", "fv"), ("cq", "ck", "cv")
    gates = ("gf", "gc", "gs")
    glu = g["w_ssm_glu"][0]
    dn = g["ffn_w_down"][0]
    up = tiles(g["ffn_w_up"][0])
    state = lambda a: a.reshape(16, P, *a.shape[2:]).swapaxes(0, 1).reshape(P, -1)
    edges = np.cumsum((0,) + FF_GROUPS) * P
    rel_at = np.clip(CA_BACK * P + np.arange(P)[:, None] - np.arange(CA_KEYS), -63, 256) + 63
    cw = np.concatenate([g["ffn_conv_w"][0], g["ffn_conv_b"]], 0)
    arrays = {
        "xT": chunks(g["x"][0].T), "memT": chunks(g["mem"][0].T),
        "w_ff": chunks(part["ff"][0]).transpose(1, 0, 2).reshape(P, 64),
        "b_ff": part["ff"][1].reshape(8, 1),
        "w_fox": inter(wt, fox), "w_ca": inter(wt, ca),
        "w_gate": np.concatenate([wt[n] for n in gates]),
        "w_foxo": tiles(g["w_fox_o"][0]), "w_cao": tiles(g["w_ca_o"][0]),
        "w_glu": np.concatenate([tiles(glu[:, :D]), tiles(glu[:, D:])], 2),
        "w_o": tiles(g["w_o"][0]), "w_kv": tiles(g["xa_wkv"][0]),
        "w_xq": tiles(g["xa_wq"][0]), "w_xo": tiles(g["xa_wo"][0]),
        "w_up": np.stack([up[:FF_TILES], up[FF_TILES:]], 1).reshape(2 * FF_TILES, P, D),
        **{f"w_dn{j}": tiles(dn[edges[j]:edges[j + 1]]) for j in range(3)},
        "b_cols": np.concatenate([inter(bt, fox), inter(bt, ca)] + [bt[n] for n in gates]).T,
        "lam_re": state(g["ssm_lambda_re"].reshape(1, -1)), "lam_im": state(g["ssm_lambda_im"].reshape(1, -1)),
        "log_dt": state(np.repeat(g["ssm_log_dt"], 64, axis=1)),
        "b_re": state(g["ssm_b_re"].reshape(1, -1, 16)), "b_im": state(g["ssm_b_im"].reshape(1, -1, 16)),
        "c_re": state(g["ssm_c_re"].swapaxes(2, 3).reshape(1, -1, 16)),
        "c_im": state(g["ssm_c_im"].swapaxes(2, 3).reshape(1, -1, 16)),
        "ssm_d": g["ssm_d"].reshape(4, P).T,
        "rel": g["ca_rel_bias"][0][:, rel_at],
        "conv": cw.reshape(4, FF_TILES, P).transpose(2, 1, 0).reshape(P, -1),
        "ln_cols": np.stack([g["ln_g"][0], g["ln_b"][0]], 1).reshape(6 * KD, P).T,
        "ln_rows": np.stack([g["ln_g"][0, 2], g["ln_b"][0, 2]]),
    }
    nc = bacc.Bacc("TRN2", target_bir_lowering=False, num_devices=1)
    arrays = {k: np.ascontiguousarray(a) for k, a in arrays.items()}
    args = {k: nc.dram_tensor(f"in_{k}", a.shape, mybir.dt.from_np(a.dtype), kind="ExternalInput").ap()
            for k, a in arrays.items()}
    args["cum_scratch"] = nc.dram_tensor("cum_scratch", (8, S), F32, kind="Internal").ap()
    args["out"] = nc.dram_tensor("out_dram", (1, S, D), F32, kind="ExternalOutput").ap()
    hybrid_layer(nc, **args)
    r = run_bass_kernel_spmd(nc, [{f"in_{k}": a for k, a in arrays.items()}], core_ids=[0])
    return r.results[0]["out_dram"]
```

```python
from contextlib import ExitStack

import concourse.bass as bass
from concourse import mybir

F32 = mybir.dt.float32
F32R = mybir.dt.float32r
BF16 = mybir.dt.bfloat16
ALU = mybir.AluOpType
ACT = mybir.ActivationFunctionType

P = 128
D = 1024
S = 1024
KD = D // P
NB = S // P
HALF = 512
HD = 64
PAIRS = 4
MEM = 256
XH_HEADS = 4
TQ = 256
NPRM = 25
CA_BACK = 4
CA_KEYS = (CA_BACK + 1) * P
FF_TILES = 22
FF_GROUPS = (8, 8, 6)
ALPHA = 2.0 ** 0.25
LN_EPS = 1e-5
NEG = -1e30
LOWEST = -3.0e38
TWO_PI = 6.283185307179586
RND = 12582912.0
PI_A = 6.28125
PI_B = 1014.0 / 2 ** 19
PI_C = TWO_PI - PI_A - PI_B

FOX_SLOTS, CA_SLOTS = 4, 3
SLOTS = {"fox": FOX_SLOTS, "ca": CA_SLOTS}
N_FOX = 0
N_CA = N_FOX + FOX_SLOTS * PAIRS
N_EF = N_CA + CA_SLOTS * PAIRS
N_EC = N_EF + 2 * KD
N_ES = N_EC + 2 * KD
N_WO = N_ES + 2 * KD
N_KV = N_WO + KD
N_XQ = N_KV + 2 * KD
N_XO = N_XQ + KD
N_FF = N_XO + KD
N_SMALL = 12
EXP_STEP, SIN_STEP, BP_STEP, BT_STEP, FFEXP_STEP, CUM_STEP = 8, 19, 55, 157, 6, 69
N_SLOTS = N_FF + sum(2 * g + KD for g in FF_GROUPS)


def hybrid_layer(nc, xT, memT, w_ff, b_ff, w_fox, w_ca, w_gate, w_foxo, w_cao, w_glu, w_o,
                 w_kv, w_xq, w_xo, w_up, w_dn0, w_dn1, w_dn2, b_cols, lam_re, lam_im, log_dt,
                 b_re, b_im, c_re, c_im, ssm_d, rel, conv, ln_cols, ln_rows, cum_scratch, out):
    w_dn = (w_dn0, w_dn1, w_dn2)
    with ExitStack() as ctx:
        sems = {}

        def sem(name):
            sems[name] = ctx.enter_context(nc.semaphore(name))
            return sems[name]

        base = 16512
        KB = 1024

        def at(name, kb, cols, dt=F32):
            return nc.alloc_sbuf_tensor_at(name, [P, cols], dt, offset=base + int(kb * KB))

        XH, XL = at("XH", 0, KD * S, F32R), at("XL", 32, KD * S, F32R)
        WR, WH, WL = at("WR", 64, 2 * D), at("WH", 72, 2 * D, F32R), at("WL", 80, 2 * D, F32R)
        YS = at("YS", 88, 4 * S)
        OF, OC = at("OF", 104, 4 * S), at("OC", 120, 4 * S)
        XRAW = at("XRAW", 136, KD * S)
        QT, KT, VT, VV = (at(n, 136 + 4 * j, S) for j, n in enumerate(("QT", "KT", "VT", "VV")))
        MB = at("MB", 152, 2 * S)
        SB = at("SB", 160, 2 * S)
        PT = at("PT", 168, 2 * S)
        K2 = at("K2", 176, S)
        Q2_FIRST_CA, Q2_CA = at("Q2_FIRST_CA", 126, S), at("Q2_CA", 180, S)
        T4 = at("T4", 180, 4 * TQ)
        YG = at("YG", 184, 4 * TQ)
        P4 = at("P4", 188, 4 * TQ)
        HH = at("HH", 192, 4 * TQ)
        BS, CS = at("BS", 196, 256), at("CS", 197, 256)
        W16 = at("W16", 198, 16 * 32)
        WT = at("WT", 120, 2 * 3 * TQ)
        BT, CT = at("BT", 126, 4 * 256), at("CT", 130, 16 * 64)
        PRM = at("PRM", 134, 16 * NPRM)
        BRAW = at("BRAW", 168, 2 * 256)
        BBAR = at("BBAR", 170, 2 * 256)
        CRAW = at("CRAW", 172, 2 * 256)
        BP = at("BP", 184, 2 * 512)
        BTMP = at("BTMP", 188, 256)
        W16T = at("W16T", 190, 2 * 256)
        WFF = at("WFF", 174, 64)
        FFB = at("FFB", 192, S)
        FFE = at("FFE", 180, S)
        OH, OL = at("OH", 136, 4 * S, F32R), at("OL", 152, 4 * S, F32R)
        MT = at("MT", 168, KD * S)
        ML = at("ML", 168, KD * S, F32R)
        MH = at("MH", 104, KD * S, F32R)
        GF = at("GF", 104, S)
        GS, G2 = at("GS", 88, S), at("G2", 92, S)
        RT1 = at("RT1", 136, KD * S)
        XN1 = at("XN1", 168, KD * S)
        XF = at("XF", 88, 2 * S)
        MRAW = at("MRAW", 96, KD * MEM)
        MMH, MML = at("MMH", 104, KD * MEM, F32R), at("MML", 112, KD * MEM, F32R)
        KM, VM = at("KM", 120, KD * MEM), at("VM", 128, 2 * D)
        VMT = at("VMT", 100, 2 * MEM)
        QX = at("QX", 88, 2 * S)
        SX = at("SX", 104, 2 * MEM)
        VX = at("VX", 108, 2 * MEM)
        OHX, OLX = at("OHX", 136, KD * S, F32R), at("OLX", 168, KD * S, F32R)
        PTX = at("PTX", 112, 2 * 2 * HALF)
        RT2 = at("RT2", 104, KD * S)
        XN2 = at("XN2", 136, KD * S)
        YT = at("YT", 104, KD * S)
        HDH, HDL = at("HDH", 136, KD * S, F32R), at("HDL", 168, KD * S, F32R)
        CV = at("CV", 88, S)
        GL = at("GL", 92, S)
        HF = at("HF", 96, S)
        XN3 = at("XN3", 136, KD * S)
        LGB = at("LGB", 88, 2 * D)
        c0 = 200.25
        IDN = at("IDN", c0, P)
        IDB = at("IDB", c0 + .5, P, BF16)
        CMB = at("CMB", c0 + .75, P, BF16)
        BC = at("BC", c0 + 1, 52)
        CONV = at("CONV", c0 + 1.25, FF_TILES * 4)
        LNC = at("LNC", c0 + 1.625, 6 * KD)
        DC = at("DC", c0 + 1.875, 8)
        PS = at("PS", c0 + 1.9375, 4 * NPRM)
        MX = at("MX", c0 + 2.375, 8)
        ST = at("ST", c0 + 2.5, 8 * 12)
        MV = at("MV", c0 + 2.9375, 8 * 8)
        SP = at("SP", c0 + 3.1875, 16 * 24)
        US = at("US", c0 + 3.1875, S)

        PA = ctx.enter_context(nc.psum_tensor("PA", [P, S], F32))
        PB = ctx.enter_context(nc.psum_tensor("PB", [P, S], F32))
        TB = ctx.enter_context(nc.psum_tensor("TB", [P, S], F32))
        OB = ctx.enter_context(nc.psum_tensor("OB", [P, HALF], F32))
        XB = ctx.enter_context(nc.psum_tensor("XB", [P, HALF], F32))
        PAIR = (PA, PB)

        params = sem("params_loaded")
        wff_loaded = sem("forget_weights_loaded")
        consts = sem("consts_built")
        xraw = [sem(f"x_loaded{h}") for h in range(4)]
        x_hi, x_lo = sem("x_hi"), sem("x_lo")
        raw = [sem(f"w_loaded{b}") for b in range(2)]
        w_hi, w_lo, w_used = sem("w_hi"), sem("w_lo"), sem("w_used")
        su = sem("setup_dve")
        sa = sem("setup_act")
        sp = sem("setup_pool")
        st_pe = sem("setup_pe")
        cum_out = sem("cum_stored")
        half_done = sem("projection_half_done")
        q_staged, k_staged = sem("q_staged"), sem("k_staged")
        spv = lambda j: SP[:, 16 * j:16 * j + 16]

        def pair(b):
            return PAIR[b % 2]

        def split_hi(act, n, b, raw_count, after_last=False):
            act.wait_ge(raw[b], 16 * raw_count)
            act.wait_ge(w_used, n + (2 if after_last else 1))
            act.activation(WH[:, b * D:(b + 1) * D], WR[:, b * D:(b + 1) * D],
                           ACT.Copy).then_inc(w_hi, 1)

        def split_lo(dve, n, b):
            dve.wait_ge(w_hi, n + 1)
            dve.tensor_tensor(WL[:, b * D:(b + 1) * D], WR[:, b * D:(b + 1) * D],
                              WH[:, b * D:(b + 1) * D].bitcast(F32), ALU.subtract).then_inc(w_lo, 1)

        def product(pe, n, b, dst, xh, xl, nk=KD, width=S, k0=0, first=False):
            pe.wait_ge(w_lo, n + 3)
            for k in range(nk):
                if first:
                    pe.wait_ge(x_lo, k + 1)
                w0 = b * D + (k0 + k) * P
                for pas, (w, x) in enumerate(((WH, xh), (WH, xl), (WL, xh))):
                    for t in range(0, width, HALF):
                        tw = min(HALF, width - t)
                        mm = pe.matmul(dst[:, t:t + tw], w[:, w0:w0 + P],
                                       x[:, k * width + t:k * width + t + tw],
                                       start=(k == 0 and pas == 0), stop=(k == nk - 1 and pas == 2))
            return mm

        def attention_events(tag):
            names = ("proj_ready", "s_ready", "s_summed", "nmax_ready", "exp_done", "rsum_ready",
                     "p_ready", "t_ready", "t_copied", "pv_done", "o_copied")
            return {n: sem(f"{tag}_{n}") for n in names}

        fox, ca = attention_events("fox"), attention_events("ca")
        mb_loaded = {"fox": [sem(f"fox_rows_loaded{h}") for h in range(2)],
                     "ca": [sem(f"ca_bias_loaded{h}") for h in range(2)]}
        ca_masked = sem("ca_bias_masked")
        CHUNKS = 26

        def key_blocks(kind, blk):
            return list(range(0 if kind == "fox" else max(0, blk - CA_BACK), blk + 1))

        def cut(blocks):
            return [blocks[a:a + 4] for a in range(0, len(blocks), 4)]

        def first_chunk(kind, u):
            return 2 + sum(len(cut(key_blocks(kind, v % NB))) for v in range(u))

        assert first_chunk("fox", 16) == CHUNKS and first_chunk("ca", 16) == CHUNKS

        def pe_scores(pe, kind, ev, u):
            hh, blk = divmod(u, NB)
            kb = key_blocks(kind, blk)
            r = slice(HD * hh, HD * hh + HD)
            dst = PA
            n = len(kb) * P
            for c in range(0, n, HALF):
                w = min(HALF, n - c)
                last = c + w == n and kind == "fox"
                mm = pe.matmul(dst[:, c:c + w], QT[r, blk * P:(blk + 1) * P],
                               KT[r, kb[0] * P + c:kb[0] * P + c + w], start=True, stop=not last)
            if kind == "fox":
                mm = pe.matmul(dst[:, n - P:n], IDB[:, :], CMB[:, :], start=False, stop=True)
            mm.then_inc(ev["s_ready"], 1)

        def pe_transposes(pe, kind, ev, i, u):
            pe.wait_ge(ev["p_ready"], 16 * i + u + 1)
            c = first_chunk(kind, u)
            for j, blocks in enumerate(cut(key_blocks(kind, u % NB))):
                pe.wait_ge(ev["t_copied"], CHUNKS * i + c + j - 1)
                bank = (c + j) % 2 * HALF
                for m in range(len(blocks)):
                    col = (u % 2) * S + (4 * j + m) * P
                    mm = pe.transpose(TB[:, bank + m * P:bank + (m + 1) * P], SB[:, col:col + P],
                                      IDN[:, :])
                mm.then_inc(ev["t_ready"], 1)

        def pe_values(pe, kind, ev, i, u):
            hh, blk = divmod(u, NB)
            kb = key_blocks(kind, blk)
            pe.wait_ge(ev["t_copied"], CHUNKS * i + first_chunk(kind, u + 1))
            if u % 4 == 0 and u:
                pe.wait_ge(ev["o_copied"], 4 * i + u // 4)
            for m, key in enumerate(kb):
                mm = pe.matmul(OB[HD * hh:HD * hh + HD, blk % 4 * P:(blk % 4 + 1) * P],
                               VV[:, key * P + HD * hh:key * P + HD * hh + HD],
                               PT[:, (u % 2) * S + m * P:(u % 2) * S + (m + 1) * P],
                               start=(m == 0), stop=(m == len(kb) - 1))
            mm.then_inc(ev["pv_done"], 1)

        def pe_turn_v(pe, kind, ev, i):
            pe.wait_ge(ev["proj_ready"], 2 * SLOTS[kind] * i + 6)
            for j in range(2):
                for m in range(4):
                    mm = pe.transpose(TB[:, j * HALF + m * P:j * HALF + (m + 1) * P],
                                      VT[:, (4 * j + m) * P:(4 * j + m + 1) * P], IDN[:, :])
                mm.then_inc(ev["t_ready"], 1)

        PIECES = 48
        EVENTS = {"fox": fox, "ca": ca}

        def slot_of(kind, p, k):
            return (N_FOX if kind == "fox" else N_CA) + SLOTS[kind] * p + k

        def filled(kind, p, k):
            return (FOX_SLOTS * (p - 1) if kind == "fox" else FOX_SLOTS * (PAIRS - 1) + CA_SLOTS * p) + k

        def staged_before(kind, p):
            return p - 1 if kind == "fox" else PAIRS - 1 + p

        def halves_ending(kind, u):
            per = PIECES // (2 * SLOTS[kind])
            return [divmod(h, 2) for h in range(2 * SLOTS[kind]) if ((h + 1) * per - 1) // 3 == u]

        def bank_of(banks, h):
            return h % 2 * HALF if banks == 2 else 0

        def pe_piece(pe, fill, g):
            if fill is None:
                return
            kind, p, banks = fill
            per = PIECES // (2 * SLOTS[kind])
            size = 3 * KD // per
            h, at_ = divmod(g, per)
            k, t = divmod(h, 2)
            n, b = slot_of(kind, p, k), k % 2
            if at_ == 0:
                if t == 0:
                    pe.wait_ge(w_lo, n + 3)
                if kind == "ca" and banks == 1 and h == 0:
                    pe.wait_ge(fox["proj_ready"], 2 * FOX_SLOTS * PAIRS)
                elif not (banks == 2 and h == 0):
                    pe.wait_ge(EVENTS[kind]["proj_ready"], 2 * SLOTS[kind] * p + h - (banks - 1))
            for j in range(at_ * size, (at_ + 1) * size):
                k0, pas = divmod(j, 3)
                w, x = ((WH, XH), (WH, XL), (WL, XH))[pas]
                w0, x0 = b * D + k0 * P, k0 * S + t * HALF
                mm = pe.matmul(PB[:, bank_of(banks, h):bank_of(banks, h) + HALF], w[:, w0:w0 + P],
                               x[:, x0:x0 + HALF], start=(j == 0), stop=(j == 3 * KD - 1))
            if at_ == per - 1:
                mm.then_inc(w_used if t else half_done, 1)

        def act_projection(act, fill, k, t):
            kind, p, banks = fill
            n = slot_of(kind, p, k)
            if t == 0:
                act.wait_ge(half_done, filled(kind, p, k) + 1)
            else:
                act.wait_ge(w_used, n + 3)
            sl = slice(t * HALF, (t + 1) * HALF)
            if k == 0:
                if kind == "fox":
                    dst = OF[:, bass.ds(p * S + t * HALF, HALF)]
                elif banks == 1:
                    act.wait_ge(staged, 5 * PAIRS)
                    dst = Q2_FIRST_CA[:, sl]
                else:
                    dst = Q2_CA[:, sl]
            elif k == 1:
                act.wait_ge(k_staged, staged_before(kind, p) + 1)
                dst = K2[:, sl]
            elif k == 2:
                dst = VT[:, sl]
            else:
                dst = YS[:, bass.ds(p * S + t * HALF, HALF)]
            bank = bank_of(banks, 2 * k + t)
            act.sem_inc(act_waits, 1)
            c0_ = 0 if kind == "fox" else FOX_SLOTS * PAIRS
            act.activation(dst, PB[:, bank:bank + HALF], ACT.Identity,
                           bias=BC[:, bass.ds(c0_ + SLOTS[kind] * p + k, 1)],
                           scale=0.125 if k == 0 else 1.0).then_inc(EVENTS[kind]["proj_ready"], 1)
            if t == 1:
                for m, b, count, after_last in next_splits(kind, p, k):
                    split_hi(act, m, b, count, after_last)

        def next_splits(kind, p, k):
            n = slot_of(kind, p, k)
            if kind == "fox":
                return [(n + 2, k % 2, 2 * p + (k + 2) // 2 + 1, False)]
            if k == 0:
                return [(n + 2, 0, 2 * PAIRS + 2 * p + 2, False)]
            if k == 1:
                return []
            return [(n + 1, 0, 2 * PAIRS + 2 * p + 3, True), (n + 2, 1, 2 * PAIRS + p + 2, False)]

        def stage_source(fill):
            kind, p, banks = fill
            if kind == "fox":
                return OF[:, bass.ds(p * S, S)]
            return (Q2_FIRST_CA if banks == 1 else Q2_CA)[:, :]

        def pe_attention(pe, kind, i, fill):
            ev = EVENTS[kind]
            ssm = kind == "fox"
            pe_turn_v(pe, kind, ev, i)
            if ssm:
                pe_ssm_in(pe, i, 0)
            pe.wait_ge(ev["s_summed"], 16 * i + 17)
            pe_scores(pe, kind, ev, 1)
            for u in range(16):
                if ssm and u < 15:
                    pe_ssm_in(pe, i, u + 1)
                pe_piece(pe, fill, 3 * u)
                pe_transposes(pe, kind, ev, i, u)
                if u < 14:
                    pe.wait_ge(ev["s_summed"], 16 * i + u + 18)
                    pe_scores(pe, kind, ev, u + 2)
                elif u == 15 and fill:
                    pe.wait_ge(q_staged, staged_before(fill[0], fill[1]) + 1)
                    pe.wait_ge(k_staged, staged_before(fill[0], fill[1]) + 2)
                    pe.wait_ge(ev["s_summed"], 16 * i + 32)
                    pe_scores(pe, fill[0], EVENTS[fill[0]], 0)
                pe_piece(pe, fill, 3 * u + 1)
                if ssm and u:
                    pe_ssm_out(pe, i, u - 1)
                pe_piece(pe, fill, 3 * u + 2)
                pe_values(pe, kind, ev, i, u)
            if ssm:
                pe_ssm_out(pe, i, 15)

        def act_attention(act, kind, i, dst, fill):
            ev = EVENTS[kind]
            act_copy_v(act, ev, i)
            act_exp(act, kind, ev, i, 0)
            for u in range(16):
                if u % 4 == 0 and u:
                    act_copy_o(act, ev, i, u // 4 - 1, dst)
                act_copy_turned(act, kind, ev, i, u)
                if u < 15:
                    act_exp(act, kind, ev, i, u + 1)
                if fill:
                    for k, t in halves_ending(fill[0], u):
                        act_projection(act, fill, k, t)
                    if u == 14:
                        act.wait_ge(ev["s_ready"], 16 * i + 16)
                        act.sem_inc(act_waits, 1)
                        act.activation(QT[:, :], stage_source(fill), ACT.Copy).then_inc(q_staged, 1)
            act_copy_o(act, ev, i, 3, dst)

        def dve_attention(dve, kind, i, fill):
            ev = EVENTS[kind]
            ssm = kind == "fox"
            dve_rowmax(dve, kind, ev, i, 0)
            if ssm:
                dve_stage(dve, i)
                dve.wait_ge(staged, 5 * i + 5)
                dve_table(dve, i, 0)
                dve_ssm(dve, i, 0)
            for u in range(16):
                dve_normalise(dve, kind, ev, i, u)
                if u < 15:
                    dve_rowmax(dve, kind, ev, i, u + 1)
                if u == 14 and fill:
                    dve.tensor_copy(KT[:, :], K2[:, :]).then_inc(k_staged, 1)
                if ssm:
                    dve_ssm(dve, i, u + 1)
                if fill and u:
                    for k, t in halves_ending(fill[0], u - 1):
                        if t == 1:
                            for m, b, _, _ in next_splits(fill[0], fill[1], k):
                                split_lo(dve, m, b)
            if ssm:
                dve_ssm(dve, i, NQ + 1)
            if fill:
                for k, t in halves_ending(fill[0], 15):
                    if t == 1:
                        for m, b, _, _ in next_splits(fill[0], fill[1], k):
                            split_lo(dve, m, b)

        def dve_rowmax(dve, kind, ev, i, u):
            hh, blk = divmod(u, NB)
            kb = key_blocks(kind, blk)
            n, b = len(kb) * P, u % 2
            if blk == 0:
                if kind == "fox":
                    dve.wait_ge(mb_loaded["fox"][hh], 16 * i + 16)
                else:
                    dve.wait_ge(ca_masked, 4 * i + 2 * hh + 3)
            col = hh * S + (0 if kind == "fox" else (kb[0] - blk + CA_BACK) * P)
            dve.wait_ge(ev["s_ready"], 16 * i + u + 1)
            dve.sem_inc(scores_seen, 1)
            dve.tensor_tensor_reduce(SB[:, b * S:b * S + n], PA[:, 0:n], MB[:, col:col + n],
                                     1.0, LOWEST, ALU.add, ALU.max,
                                     MX[:, b:b + 1]).then_inc(ev["s_summed"], 1)
            dve.wait_ge(ev["s_summed"], 16 * i + u + 17)
            dve.tensor_scalar(MX[:, 2 + b:3 + b], MX[:, b:b + 1], -1.0, None,
                              ALU.mult).then_inc(ev["nmax_ready"], 1)

        def dve_normalise(dve, kind, ev, i, u):
            b = u % 2
            n = len(key_blocks(kind, u % NB)) * P
            dve.wait_ge(ev["exp_done"], 16 * i + u + 1)
            dve.reciprocal(MX[:, 6 + b:7 + b], MX[:, 4 + b:5 + b]).then_inc(ev["rsum_ready"], 1)
            dve.wait_ge(ev["rsum_ready"], 16 * i + u + 1)
            dve.tensor_scalar(SB[:, b * S:b * S + n], SB[:, b * S:b * S + n],
                              MX[:, 6 + b:7 + b], None, ALU.mult).then_inc(ev["p_ready"], 1)

        def act_exp(act, kind, ev, i, u):
            b = u % 2
            n = len(key_blocks(kind, u % NB)) * P
            act.wait_ge(ev["nmax_ready"], 16 * i + u + 1)
            act.activation(SB[:, b * S:b * S + n], SB[:, b * S:b * S + n], ACT.Exp,
                           bias=MX[:, 2 + b:3 + b],
                           accum_out=MX[:, 4 + b:5 + b]).then_inc(ev["exp_done"], 1)

        def act_copy_turned(act, kind, ev, i, u):
            c = first_chunk(kind, u)
            for j, blocks in enumerate(cut(key_blocks(kind, u % NB))):
                if j == 0 and u >= 2:
                    act.wait_ge(ev["pv_done"], 16 * i + u - 1)
                act.wait_ge(ev["t_ready"], CHUNKS * i + c + j + 1)
                w, bank, col = len(blocks) * P, (c + j) % 2 * HALF, (u % 2) * S + 4 * j * P
                act.activation(PT[:, col:col + w], TB[:, bank:bank + w],
                               ACT.Copy).then_inc(ev["t_copied"], 1)

        def act_copy_v(act, ev, i):
            for j in range(2):
                act.wait_ge(ev["t_ready"], CHUNKS * i + j + 1)
                act.activation(VV[:, j * HALF:(j + 1) * HALF], TB[:, j * HALF:(j + 1) * HALF],
                               ACT.Copy).then_inc(ev["t_copied"], 1)

        def act_copy_o(act, ev, i, g, dst):
            r = slice(HD * (g // 2), HD * (g // 2) + HD)
            act.wait_ge(ev["pv_done"], 16 * i + 4 * g + 4)
            act.activation(dst[r, bass.ds(i * S + g % 2 * HALF, HALF)], OB[r, :],
                           ACT.Copy).then_inc(ev["o_copied"], 1)

        NQ = 16
        staged = sem("ssm_params_staged")
        table_step = sem("ssm_table_step")
        x_ready = sem("ssm_bu_ready")
        turned = sem("ssm_bu_turned")
        yadd = sem("ssm_input_ready")
        scanned = sem("ssm_scanned")
        back = sem("ssm_back_turned")
        h_ready = sem("ssm_state_ready")
        y_ready = sem("ssm_ch_ready")
        y_done = sem("ssm_y_done")
        TSTEPS = 1 + 4 * 2 + 1
        YB = PB[:, HALF:HALF + TQ]

        def pe_ssm_in(pe, i, k):
            tau, q = divmod(k, 4)
            r = slice(32 * tau, 32 * tau + 32)
            if k == 0:
                pe.wait_ge(staged, 5 * i + 5)
            else:
                pe.wait_ge(turned, NQ * i + k)
            for m in range(2):
                mm = pe.matmul(XB[:, m * TQ:(m + 1) * TQ], BS[r, m * P:(m + 1) * P],
                               US[r, q * TQ:(q + 1) * TQ], start=True, stop=True)
            mm.then_inc(x_ready, 1)

        def pe_ssm_out(pe, i, k):
            tau = k // 4
            pe.wait_ge(h_ready, NQ * i + k + 1)
            pe.wait_ge(y_done, NQ * i + k + 1)
            for m in range(2):
                h0 = (k % 2) * 2 * TQ + m * TQ
                mm = pe.matmul(YB[32 * tau:32 * tau + 32, :],
                               CS[:, tau * 64 + m * 32:tau * 64 + m * 32 + 32],
                               HH[:, h0:h0 + TQ], start=(m == 0), stop=(m == 1))
            mm.then_inc(y_ready, 1)

        def dve_table(dve, i, tau):
            b = tau % 2 * 3 * TQ
            p0, s0 = tau * NPRM, (4 * i + tau) * TSTEPS
            wr = lambda a, n: WT[:, b + a:b + a + n]
            wi = lambda a, n: WT[:, b + TQ + a:b + TQ + a + n]
            tmp = lambda m, n: T4[:, m * TQ:m * TQ + n]
            dve.tensor_copy(WT[:, b:b + 2 * TQ].rearrange("p (c t) -> p c t", c=2)[:, :, 0:16],
                            W16[:, bass.ds(i * 128 + tau * 32, 32)].rearrange("p (c t) -> p c t", c=2)
                            ).then_inc(table_step, 1)
            for m in range(4, 8):
                n, s1 = 2 ** m, s0 + 1 + 2 * (m - 4)
                er, ei, ne = (PS[:, p0 + 8 * c + m:p0 + 8 * c + m + 1] for c in range(3))
                dve.wait_ge(table_step, s1)
                dve.tensor_scalar(tmp(0, n), wi(0, n), ne, None, ALU.mult)
                dve.tensor_scalar(tmp(1, n), wi(0, n), er, None, ALU.mult).then_inc(table_step, 1)
                dve.wait_ge(table_step, s1 + 1)
                dve.scalar_tensor_tensor(wr(n, n), wr(0, n), er, tmp(0, n), ALU.mult, ALU.add)
                dve.scalar_tensor_tensor(wi(n, n), wr(0, n), ei, tmp(1, n), ALU.mult,
                                         ALU.add).then_inc(table_step, 1)
            dve.wait_ge(table_step, s0 + 9)
            dve.tensor_copy(WT[:, b + 2 * TQ:b + 3 * TQ], wr(0, TQ)).then_inc(table_step, 1)
            dve.wait_ge(table_step, s0 + 10)

        def dve_stage(dve, i):
            dve.wait_ge(y_done, NQ * i + 1)
            dve.tensor_copy(BS[:, :], BT[:, bass.ds(i * 256, 256)]).then_inc(staged, 1)
            dve.tensor_copy(CS[:, :], CT[:, bass.ds(i * 256, 256)]).then_inc(staged, 1)
            dve.tensor_copy(PS[:, :], PRM[:, bass.ds(i * 4 * NPRM, 4 * NPRM)]).then_inc(staged, 1)
            dve.tensor_copy(DC[:, 4:5], DC[:, bass.ds(i, 1)]).then_inc(staged, 1)
            dve.wait_ge(fox["proj_ready"], 8 * i + 8)
            dve.tensor_copy(US[:, :], YS[:, bass.ds(i * S, S)]).then_inc(staged, 1)

        def dve_ssm(dve, i, k):
            if k < NQ:
                tau, q = divmod(k, 4)
                w = tau % 2 * 3 * TQ
                if q == 0:
                    dve.wait_ge(table_step, (4 * i + tau + 1) * TSTEPS)
                if k:
                    dve.wait_ge(yadd, 2 * NQ * i + 2 * k)
                if k in (3, 7, 11):
                    dve_table(dve, i, tau + 1)
                dve.wait_ge(x_ready, NQ * i + k + 1)
                dve.tensor_tensor(T4[:, 0:2 * TQ], XB[:, :], WT[:, w:w + 2 * TQ], ALU.mult)
                dve.tensor_tensor(T4[:, 2 * TQ:4 * TQ], XB[:, :], WT[:, w + TQ:w + 3 * TQ],
                                  ALU.mult).then_inc(turned, 1)
            if 0 <= k - 1 < NQ:
                j = k - 1
                tau, q = divmod(j, 4)
                w, g = tau % 2 * 3 * TQ, j % 2 * 2 * TQ
                decay = PS[:, tau * NPRM + 24:tau * NPRM + 25].to_broadcast([P, TQ])
                dve.wait_ge(yadd, 2 * NQ * i + 2 * j + 2)
                if j:
                    dve.wait_ge(h_ready, NQ * i + j)
                for m in range(2):
                    h0 = (1 - j % 2) * 2 * TQ + (m + 1) * TQ - 1
                    sc = dve.tensor_tensor_scan(YG[:, g + m * TQ:g + (m + 1) * TQ], decay,
                                                YG[:, g + m * TQ:g + (m + 1) * TQ],
                                                HH[:, h0:h0 + 1] if q else 0.0, ALU.mult, ALU.add)
                sc.then_inc(scanned, 1)
                dve.wait_ge(scanned, NQ * i + j + 1)
                dve.tensor_tensor(P4[:, 0:2 * TQ], YG[:, g:g + 2 * TQ], WT[:, w:w + 2 * TQ], ALU.mult)
                dve.tensor_tensor(P4[:, 2 * TQ:4 * TQ], YG[:, g:g + 2 * TQ],
                                  WT[:, w + TQ:w + 3 * TQ], ALU.mult).then_inc(back, 1)
            if 0 <= k - 2 < NQ:
                j = k - 2
                tau, q = divmod(j, 4)
                r = slice(32 * tau, 32 * tau + 32)
                dve.wait_ge(y_ready, NQ * i + j + 1)
                u = YS[r, bass.ds(i * S + q * TQ, TQ)]
                dve.scalar_tensor_tensor(u, u, DC[r, 4:5], YB[r, :], ALU.mult, ALU.add).then_inc(y_done, 1)

        def pool_ssm(pool, i, k):
            if k < NQ:
                g = k % 2 * 2 * TQ
                pool.wait_ge(turned, NQ * i + k + 1)
                if k >= 2:
                    pool.wait_ge(back, NQ * i + k - 1)
                pool.tensor_tensor(YG[:, g:g + TQ], T4[:, 0:TQ], T4[:, TQ:2 * TQ],
                                   ALU.add).then_inc(yadd, 1)
                pool.tensor_tensor(YG[:, g + TQ:g + 2 * TQ], T4[:, 3 * TQ:4 * TQ],
                                   T4[:, 2 * TQ:3 * TQ], ALU.subtract).then_inc(yadd, 1)
            if k:
                j = k - 1
                h = j % 2 * 2 * TQ
                pool.wait_ge(back, NQ * i + j + 1)
                if j >= 2:
                    pool.wait_ge(y_ready, NQ * i + j - 1)
                pool.tensor_tensor(HH[:, h:h + TQ], P4[:, 0:TQ], P4[:, TQ:2 * TQ], ALU.subtract)
                pool.tensor_tensor(HH[:, h + TQ:h + 2 * TQ], P4[:, 2 * TQ:3 * TQ],
                                   P4[:, 3 * TQ:4 * TQ], ALU.add).then_inc(h_ready, 1)

        g_ready = {t: sem(f"{t}_gate_ready") for t in ("ef", "ec", "es")}
        o_hi = {t: sem(f"{t}_branch_hi") for t in ("ef", "ec", "es")}
        o_lo = {t: sem(f"{t}_branch_lo") for t in ("ef", "ec", "es")}
        m_step = {t: sem(f"{t}_merge_step") for t in ("ef", "ec", "es")}
        m_hi, m_lo = sem("merged_hi"), sem("merged_lo")
        y_act = sem("ssm_gelu")
        rt_step = {t: sem(f"{t}_residual_step") for t in ("wo", "xo")}
        mem_loaded, mem_hi, mem_lo = sem("mem_loaded"), sem("mem_hi"), sem("mem_lo")
        kv_ready = sem("kv_ready")
        v_turned, v_ready = sem("mem_v_turned"), sem("mem_v_ready")
        lns = [{n: sem(f"ln{k}_{n}") for n in
                ("turned", "copied", "step", "sqrt", "normed", "back", "scaled", "hi", "lo")}
               for k in range(3)]
        xa = {n: sem(f"xa_{n}") for n in ("q_ready", "v_staged", "s_ready", "max", "nmax", "exp",
                                          "rsum", "p_ready", "t_ready", "t_copied", "pv", "hi", "lo")}
        cv_step, gelu_done, hid, hid_hi, hid_lo, y_sum = (sem(n) for n in (
            "conv_step", "gelu_done", "hidden_ready", "hidden_hi", "hidden_lo", "down_added"))
        rows_loaded, final_step, out_stored = sem("ln_rows_loaded"), sem("final_step"), sem("out_stored")
        scores_seen, masks_due, act_waits = sem("scores_seen"), sem("masks_due"), sem("act_waits")

        def rc(n0, k):
            return (16 if k % 2 == 0 else 12) + (n0 - N_EF) // 2 + k // 2 + 1

        RES = {"wo": (RT1, N_WO), "xo": (RT2, N_XO)}

        def pe_ln_forward(pe, ln, rt, tau, ready):
            if tau == 0:
                pe.wait_ge(*ready)
            if tau >= 2:
                pe.wait_ge(ln["copied"], tau - 1)
            for j in range(KD):
                mm = pe.transpose(pair(tau)[:, j * P:(j + 1) * P],
                                  rt[:, j * S + tau * P:j * S + (tau + 1) * P], IDN[:, :])
            mm.then_inc(ln["turned"], 1)

        def act_ln_copy(act, ln, xn, tau):
            act.wait_ge(ln["turned"], tau + 1)
            act.activation(xn[:, tau * D:(tau + 1) * D], pair(tau)[:, :], ACT.Copy).then_inc(ln["copied"], 1)

        def dve_ln_stats(dve, ln, xn, tau):
            dve.wait_ge(ln["copied"], tau + 1)
            for h in range(2):
                dve.bn_stats(ST[:, tau * 12 + 6 * h:tau * 12 + 6 * h + 6],
                             xn[:, tau * D + h * HALF:tau * D + (h + 1) * HALF]).then_inc(ln["step"], 1)
            dve.wait_ge(ln["step"], 3 * tau + 2)
            dve.bn_aggr(MV[:, 2 * tau:2 * tau + 2], ST[:, tau * 12:tau * 12 + 12]).then_inc(ln["step"], 1)

        mean = lambda tau: MV[:, 2 * tau:2 * tau + 1]
        var = MV[:, 0:16].rearrange("p (t c) -> p t c", c=2)[:, :, 1]
        sd, rstd, tmp8 = (MV[:, 16 + 8 * j:24 + 8 * j] for j in range(3))

        def act_ln_sqrt(act, ln):
            act.wait_ge(ln["step"], 25)
            act.activation(sd, var, ACT.Sqrt).then_inc(ln["sqrt"], 1)

        def dve_ln_normalise(dve, ln, xn):
            step = ln["step"]

            def link(ins, n):
                ins.then_inc(step, 1)
                dve.wait_ge(step, n)

            dve.wait_ge(step, 24)
            link(dve.tensor_scalar(var, var, LN_EPS, None, ALU.add), 25)
            dve.wait_ge(ln["sqrt"], 1)
            link(dve.reciprocal(rstd, sd), 26)
            link(dve.tensor_tensor(tmp8, rstd, rstd, ALU.mult), 27)
            link(dve.tensor_tensor(tmp8, tmp8, var, ALU.mult), 28)
            link(dve.tensor_scalar(tmp8, tmp8, -0.5, 1.5, ALU.mult, ALU.add), 29)
            link(dve.tensor_tensor(rstd, rstd, tmp8, ALU.mult), 30)
            for tau in range(NB):
                x = xn[:, tau * D:(tau + 1) * D]
                dve.tensor_scalar(x, x, mean(tau), rstd[:, tau:tau + 1], ALU.subtract,
                                  ALU.mult).then_inc(ln["normed"], 1)

        def pe_ln_back(pe, ln, xn, k):
            if k == 0:
                pe.wait_ge(ln["normed"], NB)
            if k >= 2:
                pe.wait_ge(ln["scaled"], k - 1)
            for tau in range(NB):
                mm = pe.transpose(pair(k)[:, tau * P:(tau + 1) * P],
                                  xn[:, tau * D + k * P:tau * D + (k + 1) * P], IDN[:, :])
            mm.then_inc(ln["back"], 1)

        def act_ln_scale(act, ln, which, k):
            g, b = (LNC[:, (2 * which + c) * KD + k:(2 * which + c) * KD + k + 1] for c in range(2))
            act.wait_ge(ln["back"], k + 1)
            if k >= 2:
                act.wait_ge(ln["lo"], k - 1)
            act.activation(XF[:, k % 2 * S:(k % 2 + 1) * S], pair(k)[:, :], ACT.Identity,
                           bias=b, scale=g).then_inc(ln["scaled"], 1)

        def dve_ln_split(dve, ln, k):
            f = XF[:, k % 2 * S:(k % 2 + 1) * S]
            h = XH[:, k * S:(k + 1) * S]
            dve.wait_ge(ln["scaled"], k + 1)
            dve.tensor_copy(h, f).then_inc(ln["hi"], 1)
            dve.wait_ge(ln["hi"], k + 1)
            dve.tensor_tensor(XL[:, k * S:(k + 1) * S], f, h.bitcast(F32),
                              ALU.subtract).then_inc(ln["lo"], 1)

        block = ctx.enter_context(nc.Block())

        @block.sync
        def _(sp_):
            def load(n, b, src, width=D, after_last=False, free=True):
                if free:
                    sp_.wait_ge(w_lo, n + (2 if after_last else 1))
                sp_.dma_start(WR[:, b * D:b * D + width], src).then_inc(raw[b], 16)

            for h in range(4):
                if h in (0, 2):
                    load(h // 2, h // 2, w_fox[h // 2], free=False)
                sp_.dma_start(XRAW[:, h * 2 * S:(h + 1) * 2 * S].rearrange("p (k t) -> p k t", k=2),
                              xT[2 * h:2 * h + 2].rearrange("k p t -> p k t")).then_inc(xraw[h], 16)
            for k in range(2, FOX_SLOTS):
                load(k, k % 2, w_fox[k])
            with sp_.Fori(1, PAIRS) as i:
                for k in range(FOX_SLOTS):
                    load(FOX_SLOTS * i + k, k % 2, w_fox[FOX_SLOTS * i + k])
            with sp_.Fori(0, PAIRS) as i:
                for k in range(CA_SLOTS):
                    load(N_CA + CA_SLOTS * i + k, k % 2, w_ca[CA_SLOTS * i + k], after_last=(k == 0))
            sp_.wait_ge(w_lo, N_EF + 2)
            for br, (n0, src, width) in enumerate(((N_EF, w_foxo, HALF), (N_EC, w_cao, HALF),
                                                   (N_ES, w_glu, D))):
                with sp_.Fori(0, KD) as i:
                    load(n0 + 2 * i, 0, w_gate[KD * br + i])
                    load(n0 + 2 * i + 1, 1, src[i], width)
            sp_.wait_ge(o_lo["es"], 4)
            sp_.dma_start(MRAW[:, :].rearrange("p (k t) -> p k t", k=KD),
                          memT.rearrange("k p t -> p k t")).then_inc(mem_loaded, 16)
            for n0, src, count in ((N_WO, w_o, KD), (N_KV, w_kv, 2 * KD), (N_XQ, w_xq, KD),
                                   (N_XO, w_xo, KD)):
                with sp_.Fori(0, count // 2) as i:
                    for k in range(2):
                        load(n0 + 2 * i + k, k, src[2 * i + k])
            n0, t0 = N_FF, 0
            for g, tiles in enumerate(FF_GROUPS):
                with sp_.Fori(0, tiles) as i:
                    for k in range(2):
                        load(n0 + 2 * i + k, k, w_up[2 * t0 + 2 * i + k])
                n0, t0 = n0 + 2 * tiles, t0 + tiles
                with sp_.Fori(0, KD // 2) as i:
                    for k in range(2):
                        load(n0 + 2 * i + k, k, w_dn[g][2 * i + k], tiles * P)
                n0 += KD
            for tau in range(NB):
                sp_.wait_ge(final_step, 2 * tau + 2)
                sp_.dma_start(out[0, tau * P:(tau + 1) * P, :],
                              XN3[:, tau * D:(tau + 1) * D]).then_inc(out_stored, 16)
            sp_.wait_ge(out_stored, 16 * NB)

        @block.gpsimd
        def _(pool):
            pool.memset(IDN[:, :], 0.0)
            pool.memset(IDB[:, :], 0.0)
            pool.memset(CMB[:, :], 0.0)
            pool.memset(BP[:, :], 0.0)
            pool.memset(CT[:, :], 0.0).then_inc(sp, 1)
            pool.wait_ge(sp, 1)
            pool.affine_select(out=IDN[:, :], in_=IDN[:, :], compare_op=ALU.not_equal, fill=1.0,
                               base=0, pattern=[[-1, P]], channel_multiplier=1)
            pool.affine_select(out=IDB[:, :], in_=IDB[:, :], compare_op=ALU.not_equal, fill=1.0,
                               base=0, pattern=[[-1, P]], channel_multiplier=1)
            pool.affine_select(out=CMB[:, :], in_=CMB[:, :], compare_op=ALU.is_ge, fill=NEG,
                               base=0, pattern=[[-1, P]], channel_multiplier=1).then_inc(consts, 1)
            pool.engine_nop().then_inc(fox["s_summed"], 16)
            pool.engine_nop().then_inc(ca["s_summed"], 16)
            pool.engine_nop().then_inc(ca_masked, 1)
            pool.wait_ge(su, CUM_STEP)
            pool.dma_start(cum_scratch, FFE[0:8, :]).then_inc(cum_out, 16)
            pool.wait_ge(cum_out, 16)
            pool.wait_ge(w_used, 3)

            def rows(i, hh):
                pool.wait_ge(fox["s_summed"], 16 * i + 8 * hh + 8)
                pool.dma_start(MB[:, hh * S:(hh + 1) * S],
                               cum_scratch[bass.ds(2 * i + hh, 1), :].partition_broadcast(P)
                               ).then_inc(mb_loaded["fox"][hh], 16)

            rows(0, 0)
            with pool.Fori(0, PAIRS - 1) as i:
                rows(i, 1)
                for k in range(NQ + 1):
                    pool_ssm(pool, i, k)
                    if k == 12:
                        rows(i + 1, 0)
            rows(PAIRS - 1, 1)
            for k in range(NQ + 1):
                pool_ssm(pool, PAIRS - 1, k)
            pool.wait_ge(h_ready, NQ * PAIRS)
            with pool.Fori(0, PAIRS) as i:
                for hh in range(2):
                    pool.wait_ge(ca["s_summed"], 16 * i + 8 * hh + 8)
                    pool.wait_ge(fox["s_summed"], 16 * PAIRS + 8 * hh + 8)
                    pool.dma_start(MB[:, hh * S:hh * S + CA_KEYS],
                                   rel[2 * i + hh]).then_inc(mb_loaded["ca"][hh], 16)
                    pool.wait_ge(mb_loaded["ca"][hh], 16 * i + 16)
                    pool.wait_ge(ca_masked, 4 * i + 2 * hh + 1)
                    pool.sem_inc(masks_due, 1)
                    pool.memset(MB[0:64, hh * S + CA_KEYS - 64:hh * S + CA_KEYS],
                                NEG).then_inc(ca_masked, 1)
                    pool.wait_ge(ca_masked, 4 * i + 2 * hh + 2)
                    pool.sem_inc(masks_due, 1)
                    pool.memset(MB[64:128, hh * S:hh * S + 64], NEG).then_inc(ca_masked, 1)
            pool.wait_ge(hid_lo, FF_TILES)
            pool.dma_start(LGB[:, 0:D], ln_rows[0:1, :].partition_broadcast(P)).then_inc(rows_loaded, 16)
            pool.dma_start(LGB[:, D:2 * D], ln_rows[1:2, :].partition_broadcast(P)).then_inc(rows_loaded, 16)

        @block.scalar
        def _(act):
            act.dma_start(WFF[:, :], w_ff).then_inc(wff_loaded, 16)
            small = ((SP[:, 0:16], lam_re), (SP[:, 16:32], lam_im), (SP[:, 32:48], log_dt),
                     (BRAW[:, 0:256], b_re), (BRAW[:, 256:512], b_im),
                     (CRAW[:, 0:256], c_re), (CRAW[:, 256:512], c_im),
                     (DC[:, 0:4], ssm_d), (BC[:, :], b_cols), (DC[0:8, 6:7], b_ff),
                     (CONV[:, :], conv), (LNC[:, :], ln_cols))
            assert len(small) == N_SMALL
            for dst, src in small:
                act.dma_start(dst, src).then_inc(params, 16)
            for k in range(KD):
                if k in (0, 4):
                    n = k // 4
                    act.wait_ge(raw[n], 16)
                    act.activation(WH[:, n * D:(n + 1) * D], WR[:, n * D:(n + 1) * D],
                                   ACT.Copy).then_inc(w_hi, 1)
                act.wait_ge(xraw[k // 2], 16)
                act.activation(XH[:, k * S:(k + 1) * S], XRAW[:, k * S:(k + 1) * S],
                               ACT.Copy).then_inc(x_hi, 1)
            act.wait_ge(params, 16 * N_SMALL)
            act.activation(spv(4), spv(2), ACT.Exp).then_inc(sa, 1)
            act.wait_ge(su, EXP_STEP)
            act.activation(spv(6), spv(5), ACT.Exp).then_inc(sa, 1)
            act.wait_ge(su, FFEXP_STEP)
            act.activation(FFE[0:8, :], FFE[0:8, :], ACT.Exp, scale=-1.0).then_inc(sa, 1)
            act.wait_ge(su, SIN_STEP)
            act.activation(spv(11), spv(9), ACT.Sin)
            act.activation(spv(12), spv(10), ACT.Sin).then_inc(sa, 1)
            act.wait_ge(sa, 3)
            act.activation(FFE[0:8, :], FFE[0:8, :], ACT.Ln, bias=DC[0:8, 5:6]).then_inc(sa, 1)

            for k, dst in enumerate((QT, KT, VT, YS)):
                act.wait_ge(w_used, k + 3)
                for t in range(2):
                    act.activation(dst[:, t * HALF:(t + 1) * HALF],
                                   pair(k)[:, t * HALF:(t + 1) * HALF], ACT.Identity,
                                   bias=BC[:, k:k + 1],
                                   scale=0.125 if k == 0 else 1.0).then_inc(fox["proj_ready"], 1)
                split_hi(act, k + 2, k % 2, (k + 2) // 2 + 1)
            with act.Fori(0, PAIRS - 1) as i:
                act_attention(act, "fox", i, OF, ("fox", i + 1, 1))
            act_attention(act, "fox", PAIRS - 1, OF, ("ca", 0, 1))
            with act.Fori(0, PAIRS - 1) as i:
                act_attention(act, "ca", i, OC, ("ca", i + 1, 2))
            act_attention(act, "ca", PAIRS - 1, OC, None)

            for t, n0, br, src in (("ef", N_EF, 0, OF), ("ec", N_EC, 1, OC), ("es", N_ES, 2, YS)):
                if t == "es":
                    for c in range(4):
                        act.activation(YS[:, c * S:(c + 1) * S], YS[:, c * S:(c + 1) * S],
                                       ACT.Gelu_apprx_tanh).then_inc(y_act, 1)
                    act.wait_ge(y_act, 4)
                act.wait_ge(w_used, n0 + 2)
                if t == "ef":
                    act.wait_ge(ca["o_copied"], 4 * PAIRS)
                for c in range(4):
                    act.activation(OH[:, c * S:(c + 1) * S], src[:, c * S:(c + 1) * S],
                                   ACT.Copy).then_inc(o_hi[t], 1)
                gate = GS if t == "es" else GF
                if t == "ec":
                    act.wait_ge(m_step["ef"], KD + 1)
                with act.Fori(0, KD) as i:
                    n = n0 + 2 * i
                    act.wait_ge(w_used, n + 3)
                    if t == "ef":
                        act.wait_ge(o_lo[t], 4)
                        act.wait_ge(m_step["ef"], i + 1)
                    elif t == "ec":
                        act.wait_ge(m_step["ec"], 2 * i + 1)
                    else:
                        act.wait_ge(o_lo[t], 4)
                        act.wait_ge(m_step["es"], 3 * i + 1)
                    act.activation(gate[:, :], PA[:, :], ACT.Sigmoid,
                                   bias=BC[:, bass.ds(28 + KD * br + i, 1)]).then_inc(g_ready[t], 1)
                    split_hi(act, n + 2, 0, i + (rc(n0, 2)))
                    if t == "es":
                        act.wait_ge(w_used, n + 4)
                        act.activation(G2[:, :], TB[:, :], ACT.Sigmoid).then_inc(g_ready[t], 1)
                        split_hi(act, n + 3, 1, i + rc(n0, 3))
                        act.wait_ge(m_step["es"], 3 * i + 4)
                        act.activation(MH[:, bass.ds(i * S, S)], MT[:, bass.ds(i * S, S)],
                                       ACT.Copy).then_inc(m_hi, 1)
                    else:
                        split_hi(act, n + 3, 1, i + rc(n0, 3))

            act.wait_ge(mem_loaded, 16)

            def ring_only(n0, count):
                with act.Fori(0, count) as i:
                    for k in range(2):
                        split_hi(act, n0 + 2 * i + k + 2, k, i + rc(n0, k + 2))

            ring_only(N_WO, KD // 2)
            act.wait_ge(w_used, N_WO + KD + 2)
            act.activation(MMH[:, :], MRAW[:, :], ACT.Copy).then_inc(mem_hi, 1)

            def kv_slot(j):
                n = N_KV + j
                bank = (OB, XB)[j % 2][:, 0:MEM]
                act.wait_ge(w_used, n + 3)
                if j < KD:
                    dst = KM[:, j * MEM:(j + 1) * MEM]
                else:
                    dst = VMT[:, j % 2 * MEM:(j % 2 + 1) * MEM]
                    if j >= KD + 2:
                        act.wait_ge(v_turned, j - KD - 1)
                act.activation(dst, bank, ACT.Copy).then_inc(kv_ready, 1)
                split_hi(act, n + 2, j % 2, rc(N_KV, j + 2))

            def copy_mem_v(j):
                act.wait_ge(v_turned, j + 1)
                act.activation(VM[:, :].rearrange("p (c f) -> p c f", c=2)[:, :, j * P:(j + 1) * P],
                               TB[:, j % 2 * HALF:j % 2 * HALF + MEM].rearrange("p (c f) -> p c f", c=2),
                               ACT.Copy).then_inc(v_ready, 1)

            for tau in range(NB):
                act_ln_copy(act, lns[0], XN1, tau)
                kv_slot(tau)
            act_ln_sqrt(act, lns[0])
            for k in range(KD):
                kv_slot(KD + k)
                act_ln_scale(act, lns[0], 0, k)
                copy_mem_v(k)

            with act.Fori(0, XH_HEADS) as i:
                for k in range(2):
                    n = N_XQ + 2 * i + k
                    act.wait_ge(w_used, n + 3)
                    act.activation(QX[:, k * S:(k + 1) * S], pair(k)[:, :], ACT.Copy,
                                   scale=0.0625).then_inc(xa["q_ready"], 1)
                    split_hi(act, n + 2, k, i + rc(N_XQ, k + 2))
                act.activation(VX[:, :].rearrange("p (c f) -> p c f", c=2),
                               VM[:, :].rearrange("p (c f) -> p c f", c=2)[:, :, bass.ds(i * MEM, MEM)],
                               ACT.Copy).then_inc(xa["v_staged"], 1)

                def x_exp(u):
                    act.wait_ge(xa["nmax"], 8 * i + u + 1)
                    act.activation(SX[:, u % 2 * MEM:(u % 2 + 1) * MEM],
                                   TB[:, u % 2 * HALF:u % 2 * HALF + MEM], ACT.Exp,
                                   bias=MX[:, 2 + u % 2:3 + u % 2],
                                   accum_out=MX[:, 4 + u % 2:5 + u % 2]).then_inc(xa["exp"], 1)

                def x_copy(u):
                    act.wait_ge(xa["t_ready"], 8 * i + u + 1)
                    g, q = divmod(u, 4)
                    act.activation(
                        PTX[:, g * 2 * HALF:(g + 1) * 2 * HALF].rearrange("p (c t) -> p c t", c=2)[
                            :, :, q * P:(q + 1) * P],
                        (XB, OB)[u % 2][:, 0:MEM].rearrange("p (c t) -> p c t", c=2),
                        ACT.Copy).then_inc(xa["t_copied"], 1)

                def x_hi_part(g):
                    act.wait_ge(xa["pv"], 2 * i + g + 1)
                    for c in range(2):
                        act.activation(OHX[:, bass.ds(i * 2 * S + c * S + g * HALF, HALF)],
                                       pair(g)[:, c * HALF:(c + 1) * HALF],
                                       ACT.Copy).then_inc(xa["hi"], 1)

                x_exp(0)
                for u in range(8):
                    if u < 7:
                        x_exp(u + 1)
                    x_copy(u)
                    if u == 4:
                        x_hi_part(0)
                x_hi_part(1)

            ring_only(N_XO, KD // 2)
            for tau in range(NB):
                act_ln_copy(act, lns[1], XN2, tau)
            act_ln_sqrt(act, lns[1])
            for k in range(KD):
                act_ln_scale(act, lns[1], 1, k)
                act.wait_ge(lns[1]["scaled"], k + 1)
                act.activation(YT[:, k * S:(k + 1) * S], XF[:, k % 2 * S:(k % 2 + 1) * S], ACT.Copy,
                               scale=ALPHA).then_inc(lns[1]["sqrt"], 1)

            act.wait_ge(lns[1]["sqrt"], 1 + KD)
            act.preload_act_table(ACT.Gelu_apprx_tanh)
            n0, t0 = N_FF, 0
            for g, tiles in enumerate(FF_GROUPS):
                with act.Fori(0, tiles) as i:
                    n = n0 + 2 * i
                    split_hi(act, n + 2, 0, i + rc(n0, 2))
                    act.wait_ge(cv_step, 3 * (t0 + i) + 3)
                    act.activation(GL[:, :], CV[:, :], ACT.Gelu_apprx_tanh).then_inc(gelu_done, 1)
                    split_hi(act, n + 3, 1, i + rc(n0, 3))
                    act.wait_ge(hid, t0 + i + 1)
                    act.activation(HDH[:, bass.ds(i * S, S)], HF[:, :], ACT.Copy).then_inc(hid_hi, 1)
                n0, t0 = n0 + 2 * tiles, t0 + tiles
                last = g == len(FF_GROUPS) - 1
                ring_only(n0, KD // 2 - (1 if last else 0))
                n0 += KD
            for tau in range(NB):
                act_ln_copy(act, lns[2], XN3, tau)
            act_ln_sqrt(act, lns[2])

        @block.tensor
        def _(pe):
            pe.wait_ge(wff_loaded, 16)
            for k in range(KD):
                pe.wait_ge(xraw[k // 2], 16)
                for t in range(2):
                    mm = pe.matmul((OB, XB)[t][0:8, :], WFF[:, 8 * k:8 * k + 8],
                                   XRAW[:, k * S + t * HALF:k * S + (t + 1) * HALF],
                                   start=(k == 0), stop=(k == KD - 1))
            mm.then_inc(st_pe, 1)
            pe.nop().then_inc(w_used, 2)
            for k in range(FOX_SLOTS):
                if k >= 2:
                    pe.wait_ge(fox["proj_ready"], 2 * (k - 1))
                product(pe, k, k % 2, pair(k), XH, XL, first=(k == 0)).then_inc(w_used, 1)
            pe.wait_ge(consts, 1)
            pe.wait_ge(su, BP_STEP)
            for t in range(4):
                for c in range(2):
                    mm = pe.transpose(TB[:, (2 * t + c) * P:(2 * t + c + 1) * P],
                              BP[:, c * 512 + t * P:c * 512 + (t + 1) * P], IDN[:, :])
            mm.then_inc(st_pe, 1)
            pe.wait_ge(fox["proj_ready"], 6)
            pe_scores(pe, "fox", fox, 0)
            pe.wait_ge(su, BT_STEP)
            with pe.Fori(0, PAIRS - 1) as i:
                pe_attention(pe, "fox", i, ("fox", i + 1, 1))
            pe_attention(pe, "fox", PAIRS - 1, ("ca", 0, 1))
            with pe.Fori(0, PAIRS - 1) as i:
                pe_attention(pe, "ca", i, ("ca", i + 1, 2))
            pe_attention(pe, "ca", PAIRS - 1, None)

            for t, n0 in (("ef", N_EF), ("ec", N_EC), ("es", N_ES)):
                with pe.Fori(0, KD) as i:
                    n = n0 + 2 * i
                    product(pe, n, 0, PA, XH, XL).then_inc(w_used, 1)
                    pe.wait_ge(o_lo[t], 4)
                    if t == "es":
                        product(pe, n + 1, 1, PB, OH, OL, nk=4)
                        product(pe, n + 1, 1, TB, OH, OL, nk=4, k0=4).then_inc(w_used, 1)
                    else:
                        product(pe, n + 1, 1, PB, OH, OL, nk=4).then_inc(w_used, 1)
            pe.wait_ge(m_lo, KD)

            def dense(n0, xh, xl, nk=KD):
                with pe.Fori(0, KD // 2) as i:
                    for k in range(2):
                        product(pe, n0 + 2 * i + k, k, pair(k), xh, xl, nk=nk).then_inc(w_used, 1)

            dense(N_WO, MH, ML)
            pe.wait_ge(mem_lo, 1)

            def kv_slot(j):
                if j >= 2:
                    pe.wait_ge(kv_ready, j - 1)
                product(pe, N_KV + j, j % 2, (OB, XB)[j % 2], MMH, MML, width=MEM).then_inc(w_used, 1)

            for tau in range(NB):
                pe_ln_forward(pe, lns[0], RT1, tau, (rt_step["wo"], 2 * KD))
                kv_slot(tau)
            for k in range(KD):
                kv_slot(KD + k)
                pe_ln_back(pe, lns[0], XN1, k)
                pe.wait_ge(kv_ready, KD + k + 1)
                if k >= 2:
                    pe.wait_ge(v_ready, k - 1)
                for c in range(2):
                    mm = pe.transpose(TB[:, k % 2 * HALF + c * P:k % 2 * HALF + (c + 1) * P],
                                      VMT[:, k % 2 * MEM + c * P:k % 2 * MEM + (c + 1) * P], IDN[:, :])
                mm.then_inc(v_turned, 1)
            pe.wait_ge(lns[0]["lo"], KD)
            pe.wait_ge(v_ready, KD)

            with pe.Fori(0, XH_HEADS) as i:
                for k in range(2):
                    product(pe, N_XQ + 2 * i + k, k, pair(k), XH, XL).then_inc(w_used, 1)
                pe.wait_ge(xa["q_ready"], 2 * i + 2)
                pe.wait_ge(xa["v_staged"], i + 1)

                def scores(u):
                    for c in range(2):
                        mm = pe.matmul(TB[:, u % 2 * HALF:u % 2 * HALF + MEM],
                                       QX[:, c * S + u * P:c * S + (u + 1) * P],
                                       KM[:, bass.ds(i * 2 * MEM + c * MEM, MEM)],
                                       start=(c == 0), stop=(c == 1))
                    mm.then_inc(xa["s_ready"], 1)

                scores(0)
                scores(1)
                for u in range(8):
                    pe.wait_ge(xa["p_ready"], 8 * i + u + 1)
                    if u >= 2:
                        pe.wait_ge(xa["t_copied"], 8 * i + u - 1)
                    for c in range(2):
                        mm = pe.transpose((XB, OB)[u % 2][:, c * P:(c + 1) * P],
                                          SX[:, u % 2 * MEM + c * P:u % 2 * MEM + (c + 1) * P], IDN[:, :])
                    mm.then_inc(xa["t_ready"], 1)
                    if u < 6:
                        scores(u + 2)
                    if u in (4, 7):
                        g = u // 5
                        pe.wait_ge(xa["t_copied"], 8 * i + 4 * g + 4)
                        for c2 in range(2):
                            for c in range(2):
                                mm = pe.matmul(pair(g)[:, c2 * HALF:(c2 + 1) * HALF],
                                               VX[:, c * MEM + c2 * P:c * MEM + (c2 + 1) * P],
                                               PTX[:, (2 * g + c) * HALF:(2 * g + c + 1) * HALF],
                                               start=(c == 0), stop=(c == 1))
                        mm.then_inc(xa["pv"], 1)
                pe.wait_ge(xa["lo"], 4 * i + 4)
            dense(N_XO, OHX, OLX)
            for tau in range(NB):
                pe_ln_forward(pe, lns[1], RT2, tau, (rt_step["xo"], 2 * KD))
            for k in range(KD):
                pe_ln_back(pe, lns[1], XN2, k)
            pe.wait_ge(lns[1]["lo"], KD)

            n0, t0 = N_FF, 0
            for g, tiles in enumerate(FF_GROUPS):
                with pe.Fori(0, tiles) as i:
                    for k in range(2):
                        product(pe, n0 + 2 * i + k, k, pair(k), XH, XL).then_inc(w_used, 1)
                n0, t0 = n0 + 2 * tiles, t0 + tiles
                pe.wait_ge(hid_lo, t0)
                dense(n0, HDH, HDL, nk=tiles)
                n0 += KD
            for tau in range(NB):
                pe_ln_forward(pe, lns[2], YT, tau, (y_sum, len(FF_GROUPS) * KD))

        @block.vector
        def _(dve):
            chain = [0]

            def link(ins):
                chain[0] += 1
                ins.then_inc(su, 1)
                dve.wait_ge(su, chain[0])

            def step(ins):
                chain[0] += 1
                ins.then_inc(su, 1)

            v = spv
            E = lambda c, m: PRM[:, :].rearrange("p (t n) -> p t n", n=NPRM)[:, :, 8 * c + m]
            TT, TS, STT = dve.tensor_tensor, dve.tensor_scalar, dve.scalar_tensor_tensor

            dve.memset(DC[:, 5:6], 1.0).then_inc(su, 1)
            chain[0] += 1
            dve.engine_nop().then_inc(w_lo, 2)
            for k in range(KD):
                if k in (0, 4):
                    split_lo(dve, k // 4, k // 4)
                dve.wait_ge(x_hi, k + 1)
                dve.tensor_tensor(XL[:, k * S:(k + 1) * S], XRAW[:, k * S:(k + 1) * S],
                                  XH[:, k * S:(k + 1) * S].bitcast(F32), ALU.subtract).then_inc(x_lo, 1)
            dve.wait_ge(params, 16 * N_SMALL)
            link(TS(BC[:, 0:16:4], BC[:, 0:16:4], 0.125, None, ALU.mult))
            link(TS(BC[:, 16:28:3], BC[:, 16:28:3], 0.125, None, ALU.mult))
            dve.wait_ge(st_pe, 1)
            for t, bank in enumerate((OB, XB)):
                link(TS(FFB[0:8, t * HALF:(t + 1) * HALF], bank[0:8, :], DC[0:8, 6:7], None, ALU.add))
            link(STT(FFE[0:8, :], FFB[0:8, :], -1.0, FFB[0:8, :], ALU.mult, ALU.max))
            assert chain[0] == FFEXP_STEP, chain[0]
            link(TS(v(3), v(0), -1e-4, None, ALU.min))
            dve.wait_ge(sa, 1)
            link(TT(v(5), v(3), v(4), ALU.mult))
            assert chain[0] == EXP_STEP, chain[0]
            link(TT(v(7), v(1), v(4), ALU.mult))
            link(TS(v(8), v(7), 1.0 / TWO_PI, RND, ALU.mult, ALU.add))
            link(TS(v(8), v(8), -RND, None, ALU.add))
            link(STT(v(9), v(8), -PI_A, v(7), ALU.mult, ALU.add))
            link(STT(v(9), v(8), -PI_B, v(9), ALU.mult, ALU.add))
            link(STT(v(9), v(8), -PI_C, v(9), ALU.mult, ALU.add))
            link(TS(v(9), v(9), 0.5, -1.5707963, ALU.mult, ALU.max))
            link(TS(v(9), v(9), 1.5707963, None, ALU.min))
            link(STT(v(10), v(9), -1.0, v(9), ALU.mult, ALU.max))
            link(TS(v(10), v(10), -1.0, 1.5707963267948966, ALU.mult, ALU.add))
            link(TS(v(10), v(10), 0.0, None, ALU.max))
            assert chain[0] == SIN_STEP, chain[0]
            dve.wait_ge(sa, 4)
            link(TT(v(13), v(11), v(11), ALU.mult))
            link(TS(E(0, 0), v(13), -2.0, 1.0, ALU.mult, ALU.add))
            link(STT(E(1, 0), v(11), 2.0, v(12), ALU.mult, ALU.mult))

            def unit(c, s):
                step(TT(v(16), c, c, ALU.mult))
                link(TT(v(17), s, s, ALU.mult))
                link(TT(v(16), v(16), v(17), ALU.add))
                link(TS(v(16), v(16), -0.5, 1.5, ALU.mult, ALU.add))
                step(TT(c, c, v(16), ALU.mult))
                link(TT(s, s, v(16), ALU.mult))

            unit(E(0, 0), E(1, 0))
            split_lo(dve, 2, 0)
            link(TT(v(14), v(6), E(0, 0), ALU.mult))
            link(TS(v(14), v(14), -1.0, None, ALU.add))
            link(TT(v(15), v(6), E(1, 0), ALU.mult))
            step(TT(v(16), v(3), v(3), ALU.mult))
            link(TT(v(17), v(1), v(1), ALU.mult))
            link(TT(v(16), v(16), v(17), ALU.add))
            link(dve.reciprocal(v(18), v(16)))
            step(TT(v(16), v(14), v(3), ALU.mult))
            link(TT(v(17), v(15), v(1), ALU.mult))
            link(TT(v(16), v(16), v(17), ALU.add))
            link(TT(v(19), v(16), v(18), ALU.mult))
            step(TT(v(16), v(15), v(3), ALU.mult))
            link(TT(v(17), v(14), v(1), ALU.mult))
            link(TT(v(16), v(16), v(17), ALU.subtract))
            link(TT(v(20), v(16), v(18), ALU.mult))
            gb = lambda a: v(a).unsqueeze(2).to_broadcast([P, 16, 16])
            t3 = lambda a: a.rearrange("p (t c) -> p t c", t=16)
            br, bi = t3(BRAW[:, 0:256]), t3(BRAW[:, 256:512])
            dve.wait_ge(sp, 1)
            for c, (x1, x2, op) in enumerate(((br, bi, ALU.subtract), (bi, br, ALU.add))):
                step(TT(t3(BTMP[:, 0:256]), x2, gb(20), ALU.mult))
                link(TT(t3(BBAR[:, c * 256:(c + 1) * 256]), x1, gb(19), ALU.mult))
                for g in range(2):
                    r = slice(64 * g, 64 * g + 64)
                    step(TT(BP[r, c * 512:(c + 1) * 512].rearrange("p (t c) -> p t c", t=16)[
                                :, :, 16 * g:16 * g + 16],
                            t3(BBAR[r, c * 256:(c + 1) * 256]), t3(BTMP[r, 0:256]), op))
                    link(TS(CT[r, :].rearrange("p (t q c) -> p t q c", t=16, q=2)[
                                :, :, c, 16 * g:16 * g + 16],
                            t3(CRAW[r, c * 256:(c + 1) * 256]), 1.0 - 2.0 * c, None, ALU.mult))
            assert chain[0] == BP_STEP, chain[0]
            link(dve.tensor_copy(PRM[:, :].rearrange("p (t n) -> p t n", n=NPRM)[:, :, 24], v(6)))
            for m in range(1, 8):
                c, s = E(0, m - 1), E(1, m - 1)
                step(TT(v(16), c, c, ALU.mult))
                link(TT(v(17), s, s, ALU.mult))
                step(TT(E(0, m), v(16), v(17), ALU.subtract))
                link(STT(E(1, m), c, 2.0, s, ALU.mult, ALU.mult))
                unit(E(0, m), E(1, m))
                if m == 1:
                    link(TS(FFB[0:8, :], FFB[0:8, :], 0.0, None, ALU.min))
                    dve.wait_ge(sa, 5)
                    link(TT(FFB[0:8, :], FFB[0:8, :], FFE[0:8, :], ALU.subtract))
                    link(dve.tensor_tensor_scan(FFE[0:8, :], DC[0:8, 5:6].to_broadcast([8, S]),
                                                FFB[0:8, :], 0.0, ALU.mult, ALU.subtract))
                    assert chain[0] == CUM_STEP, chain[0]
                    split_lo(dve, 3, 1)
            pr = PRM[:, :].rearrange("p (t n) -> p t n", n=NPRM)
            link(TS(pr[:, :, 16:24], pr[:, :, 8:16], -1.0, None, ALU.mult))
            w16 = W16[:, :].rearrange("p (t c n) -> p t c n", t=16, c=2)
            step(dve.tensor_copy(w16[:, :, 0, 0:1], pr[:, :, 0:1]))
            link(dve.tensor_copy(w16[:, :, 1, 0:1], pr[:, :, 8:9]))
            for m in range(4):
                n = 2 ** m
                wt = lambda c: W16T[:, c * 256:c * 256 + 16 * n].rearrange("p (t n) -> p t n", n=n)
                eb = lambda c: pr[:, :, 8 * c + m:8 * c + m + 1].to_broadcast([P, 16, n])
                wr, wi = w16[:, :, 0, 0:n], w16[:, :, 1, 0:n]
                step(TT(wt(0), wr, eb(0), ALU.mult))
                link(TT(wt(1), wi, eb(1), ALU.mult))
                link(TT(w16[:, :, 0, n:2 * n], wt(0), wt(1), ALU.subtract))
                step(TT(wt(0), wr, eb(1), ALU.mult))
                link(TT(wt(1), wi, eb(0), ALU.mult))
                link(TT(w16[:, :, 1, n:2 * n], wt(0), wt(1), ALU.add))
            dve.wait_ge(st_pe, 2)
            link(dve.tensor_copy(BT[:, :], TB[:, :]))
            assert chain[0] == BT_STEP, chain[0]
            dve.engine_nop().then_inc(y_done, 1)
            dve.engine_nop().then_inc(m_step["ef"], 1)
            dve.engine_nop().then_inc(m_step["ec"], 1)
            dve.engine_nop().then_inc(m_step["es"], 1)

            dve.engine_nop().then_inc(k_staged, 1)
            for k in range(2, FOX_SLOTS):
                split_lo(dve, k + 2, k % 2)
            dve.wait_ge(cum_out, 16)
            with dve.Fori(0, PAIRS - 1) as i:
                dve_attention(dve, "fox", i, ("fox", i + 1, 1))
            dve_attention(dve, "fox", PAIRS - 1, ("ca", 0, 1))
            with dve.Fori(0, PAIRS - 1) as i:
                dve_attention(dve, "ca", i, ("ca", i + 1, 2))
            dve_attention(dve, "ca", PAIRS - 1, None)

            for t, n0, src in (("ef", N_EF, OF), ("ec", N_EC, OC), ("es", N_ES, YS)):
                for c in range(4):
                    dve.wait_ge(o_hi[t], c + 1)
                    dve.tensor_tensor(OL[:, c * S:(c + 1) * S], src[:, c * S:(c + 1) * S],
                                      OH[:, c * S:(c + 1) * S].bitcast(F32),
                                      ALU.subtract).then_inc(o_lo[t], 1)
                with dve.Fori(0, KD) as i:
                    n = n0 + 2 * i
                    split_lo(dve, n + 2, 0)
                    mt = MT[:, bass.ds(i * S, S)]
                    dve.wait_ge(w_used, n + 4)
                    if t == "ef":
                        dve.wait_ge(g_ready[t], i + 1)
                        dve.tensor_tensor(mt, PB[:, :], GF[:, :], ALU.mult).then_inc(m_step[t], 1)
                    elif t == "ec":
                        dve.wait_ge(g_ready[t], i + 1)
                        dve.tensor_tensor(GF[:, :], PB[:, :], GF[:, :], ALU.mult).then_inc(m_step[t], 1)
                        dve.wait_ge(m_step[t], 2 * i + 2)
                        dve.tensor_tensor(mt, mt, GF[:, :], ALU.add).then_inc(m_step[t], 1)
                    else:
                        dve.wait_ge(g_ready[t], 2 * i + 2)
                        dve.tensor_tensor(GS[:, :], PB[:, :], GS[:, :], ALU.mult).then_inc(m_step[t], 1)
                        dve.wait_ge(m_step[t], 3 * i + 2)
                        dve.tensor_tensor(GS[:, :], GS[:, :], G2[:, :], ALU.mult).then_inc(m_step[t], 1)
                        dve.wait_ge(m_step[t], 3 * i + 3)
                        dve.tensor_tensor(mt, mt, GS[:, :], ALU.add).then_inc(m_step[t], 1)
                    split_lo(dve, n + 3, 1)
                    if t == "es":
                        dve.wait_ge(m_hi, i + 1)
                        dve.tensor_tensor(ML[:, bass.ds(i * S, S)], mt,
                                          MH[:, bass.ds(i * S, S)].bitcast(F32),
                                          ALU.subtract).then_inc(m_lo, 1)

            def residual(tag):
                rt, n0 = RES[tag]
                with dve.Fori(0, KD // 2) as i:
                    for k in range(2):
                        n = n0 + 2 * i + k
                        sl = bass.ds(i * 2 * S + k * S, S)
                        dve.wait_ge(w_used, n + 3)
                        dve.scalar_tensor_tensor(rt[:, sl], XH[:, sl].bitcast(F32), ALPHA, pair(k)[:, :],
                                                 ALU.mult, ALU.add).then_inc(rt_step[tag], 1)
                        split_lo(dve, n + 2, k)
                        dve.wait_ge(rt_step[tag], 4 * i + 2 * k + 1)
                        dve.scalar_tensor_tensor(rt[:, sl], XL[:, sl].bitcast(F32), ALPHA, rt[:, sl],
                                                 ALU.mult, ALU.add).then_inc(rt_step[tag], 1)

            residual("wo")
            dve.wait_ge(mem_hi, 1)
            dve.tensor_tensor(MML[:, :], MRAW[:, :], MMH[:, :].bitcast(F32),
                              ALU.subtract).then_inc(mem_lo, 1)
            for tau in range(NB):
                dve_ln_stats(dve, lns[0], XN1, tau)
                split_lo(dve, N_KV + tau + 2, tau % 2)
            dve_ln_normalise(dve, lns[0], XN1)
            for k in range(KD):
                split_lo(dve, N_KV + KD + k + 2, k % 2)
                dve_ln_split(dve, lns[0], k)

            with dve.Fori(0, XH_HEADS) as i:
                for k in range(2):
                    split_lo(dve, N_XQ + 2 * i + k + 2, k)

                def x_max(u):
                    b = u % 2
                    dve.wait_ge(xa["s_ready"], 8 * i + u + 1)
                    dve.reduce_max(MX[:, b:b + 1], TB[:, b * HALF:b * HALF + MEM],
                                   mybir.AxisListType.X).then_inc(xa["max"], 1)
                    dve.wait_ge(xa["max"], 8 * i + u + 1)
                    dve.tensor_scalar(MX[:, 2 + b:3 + b], MX[:, b:b + 1], -1.0, None,
                                      ALU.mult).then_inc(xa["nmax"], 1)

                def x_norm(u):
                    b = u % 2
                    dve.wait_ge(xa["exp"], 8 * i + u + 1)
                    dve.reciprocal(MX[:, 6 + b:7 + b], MX[:, 4 + b:5 + b]).then_inc(xa["rsum"], 1)
                    dve.wait_ge(xa["rsum"], 8 * i + u + 1)
                    x = SX[:, b * MEM:(b + 1) * MEM]
                    dve.tensor_scalar(x, x, MX[:, 6 + b:7 + b], None, ALU.mult).then_inc(xa["p_ready"], 1)

                def x_lo_part(g):
                    for c in range(2):
                        sl = bass.ds(i * 2 * S + c * S + g * HALF, HALF)
                        dve.wait_ge(xa["hi"], 4 * i + 2 * g + c + 1)
                        dve.tensor_tensor(OLX[:, sl], pair(g)[:, c * HALF:(c + 1) * HALF],
                                          OHX[:, sl].bitcast(F32), ALU.subtract).then_inc(xa["lo"], 1)

                x_max(0)
                for u in range(8):
                    if u < 7:
                        x_max(u + 1)
                    x_norm(u)
                    if u == 6:
                        x_lo_part(0)
                x_lo_part(1)

            residual("xo")
            for tau in range(NB):
                dve_ln_stats(dve, lns[1], XN2, tau)
            dve_ln_normalise(dve, lns[1], XN2)
            for k in range(KD):
                dve_ln_split(dve, lns[1], k)

            dve.wait_ge(lns[1]["sqrt"], 1 + KD)
            n0, t0 = N_FF, 0
            for g, tiles in enumerate(FF_GROUPS):
                with dve.Fori(0, tiles) as i:
                    n = n0 + 2 * i
                    col = lambda m: CONV[:, bass.ds(4 * t0 + 4 * i + m, 1)]
                    dve.wait_ge(w_used, n + 3)
                    dve.tensor_scalar(CV[:, :], PA[:, :], col(2), col(3), ALU.mult,
                                      ALU.add).then_inc(cv_step, 1)
                    dve.wait_ge(cv_step, 3 * (t0 + i) + 1)
                    dve.scalar_tensor_tensor(CV[:, 1:S], PA[:, 0:S - 1], col(1), CV[:, 1:S], ALU.mult,
                                             ALU.add).then_inc(cv_step, 1)
                    dve.wait_ge(cv_step, 3 * (t0 + i) + 2)
                    dve.scalar_tensor_tensor(CV[:, 2:S], PA[:, 0:S - 2], col(0), CV[:, 2:S], ALU.mult,
                                             ALU.add).then_inc(cv_step, 1)
                    split_lo(dve, n + 2, 0)
                    dve.wait_ge(w_used, n + 4)
                    dve.wait_ge(gelu_done, t0 + i + 1)
                    dve.tensor_tensor(HF[:, :], PB[:, :], GL[:, :], ALU.mult).then_inc(hid, 1)
                    split_lo(dve, n + 3, 1)
                    dve.wait_ge(hid_hi, t0 + i + 1)
                    dve.tensor_tensor(HDL[:, bass.ds(i * S, S)], HF[:, :],
                                      HDH[:, bass.ds(i * S, S)].bitcast(F32),
                                      ALU.subtract).then_inc(hid_lo, 1)
                n0, t0 = n0 + 2 * tiles, t0 + tiles
                last = g == len(FF_GROUPS) - 1

                def down(i, split):
                    for k in range(2):
                        n = n0 + 2 * i + k
                        yt = YT[:, bass.ds(i * 2 * S + k * S, S)]
                        dve.wait_ge(w_used, n + 3)
                        dve.tensor_tensor(yt, pair(k)[:, :], yt, ALU.add).then_inc(y_sum, 1)
                        if split:
                            split_lo(dve, n + 2, k)

                with dve.Fori(0, KD // 2 - (1 if last else 0)) as i:
                    down(i, True)
                if last:
                    down(KD // 2 - 1, False)
                n0 += KD
            for tau in range(NB):
                dve_ln_stats(dve, lns[2], XN3, tau)
            dve_ln_normalise(dve, lns[2], XN3)
            dve.wait_ge(rows_loaded, 32)
            for tau in range(NB):
                x = XN3[:, tau * D:(tau + 1) * D]
                dve.wait_ge(lns[2]["normed"], tau + 1)
                dve.tensor_tensor(x, x, LGB[:, 0:D], ALU.mult).then_inc(final_step, 1)
                dve.wait_ge(final_step, 2 * tau + 1)
                dve.tensor_tensor(x, x, LGB[:, D:2 * D], ALU.add).then_inc(final_step, 1)


def kernel(**inputs):
    import numpy as np
    import concourse.bacc as bacc
    from concourse.bass_utils import run_bass_kernel_spmd

    g = {k: np.asarray(v) for k, v in inputs.items()}
    chunks = lambda a: a.reshape(-1, P, a.shape[-1])

    def tiles(w):
        k, m = w.shape
        return w.reshape(k // P, P, m // P, P).transpose(2, 1, 0, 3).reshape(m // P, P, k)

    w_in, b_in = g["w_in"][0], g["b_in"][0]
    cuts = np.cumsum([0, 512, 512, 512, 8, 512, 512, 512, 512, 1024, 1024, 1024])
    part = {n: (w_in[:, a:b], b_in[a:b]) for n, a, b in
            zip(("fq", "fk", "fv", "ff", "su", "cq", "ck", "cv", "gf", "gs", "gc"), cuts, cuts[1:])}
    wt = {n: tiles(w) for n, (w, _) in part.items() if n != "ff"}
    bt = {n: b.reshape(-1, P) for n, (_, b) in part.items() if n != "ff"}
    inter = lambda d, names: np.stack([d[n] for n in names], 1).reshape((-1,) + d[names[0]].shape[1:])
    fox, ca = ("fq", "fk", "fv", "su"), ("cq", "ck", "cv")
    gates = ("gf", "gc", "gs")
    glu = g["w_ssm_glu"][0]
    dn = g["ffn_w_down"][0]
    up = tiles(g["ffn_w_up"][0])
    state = lambda a: a.reshape(16, P, *a.shape[2:]).swapaxes(0, 1).reshape(P, -1)
    edges = np.cumsum((0,) + FF_GROUPS) * P
    rel_at = np.clip(CA_BACK * P + np.arange(P)[:, None] - np.arange(CA_KEYS), -63, 256) + 63
    cw = np.concatenate([g["ffn_conv_w"][0], g["ffn_conv_b"]], 0)
    arrays = {
        "xT": chunks(g["x"][0].T), "memT": chunks(g["mem"][0].T),
        "w_ff": chunks(part["ff"][0]).transpose(1, 0, 2).reshape(P, 64),
        "b_ff": part["ff"][1].reshape(8, 1),
        "w_fox": inter(wt, fox), "w_ca": inter(wt, ca),
        "w_gate": np.concatenate([wt[n] for n in gates]),
        "w_foxo": tiles(g["w_fox_o"][0]), "w_cao": tiles(g["w_ca_o"][0]),
        "w_glu": np.concatenate([tiles(glu[:, :D]), tiles(glu[:, D:])], 2),
        "w_o": tiles(g["w_o"][0]), "w_kv": tiles(g["xa_wkv"][0]),
        "w_xq": tiles(g["xa_wq"][0]), "w_xo": tiles(g["xa_wo"][0]),
        "w_up": np.stack([up[:FF_TILES], up[FF_TILES:]], 1).reshape(2 * FF_TILES, P, D),
        **{f"w_dn{j}": tiles(dn[edges[j]:edges[j + 1]]) for j in range(3)},
        "b_cols": np.concatenate([inter(bt, fox), inter(bt, ca)] + [bt[n] for n in gates]).T,
        "lam_re": state(g["ssm_lambda_re"].reshape(1, -1)), "lam_im": state(g["ssm_lambda_im"].reshape(1, -1)),
        "log_dt": state(np.repeat(g["ssm_log_dt"], 64, axis=1)),
        "b_re": state(g["ssm_b_re"].reshape(1, -1, 16)), "b_im": state(g["ssm_b_im"].reshape(1, -1, 16)),
        "c_re": state(g["ssm_c_re"].swapaxes(2, 3).reshape(1, -1, 16)),
        "c_im": state(g["ssm_c_im"].swapaxes(2, 3).reshape(1, -1, 16)),
        "ssm_d": g["ssm_d"].reshape(4, P).T,
        "rel": g["ca_rel_bias"][0][:, rel_at],
        "conv": cw.reshape(4, FF_TILES, P).transpose(2, 1, 0).reshape(P, -1),
        "ln_cols": np.stack([g["ln_g"][0], g["ln_b"][0]], 1).reshape(6 * KD, P).T,
        "ln_rows": np.stack([g["ln_g"][0, 2], g["ln_b"][0, 2]]),
    }
    nc = bacc.Bacc("TRN2", target_bir_lowering=False, num_devices=1)
    arrays = {k: np.ascontiguousarray(a) for k, a in arrays.items()}
    args = {k: nc.dram_tensor(f"in_{k}", a.shape, mybir.dt.from_np(a.dtype), kind="ExternalInput").ap()
            for k, a in arrays.items()}
    args["cum_scratch"] = nc.dram_tensor("cum_scratch", (8, S), F32, kind="Internal").ap()
    args["out"] = nc.dram_tensor("out_dram", (1, S, D), F32, kind="ExternalOutput").ap()
    hybrid_layer(nc, **args)
    r = run_bass_kernel_spmd(nc, [{f"in_{k}": a for k, a in arrays.items()}], core_ids=[0])
    return r.results[0]["out_dram"]
```

```python
from contextlib import ExitStack

import concourse.bass as bass
from concourse import mybir

F32 = mybir.dt.float32
F32R = mybir.dt.float32r
BF16 = mybir.dt.bfloat16
ALU = mybir.AluOpType
ACT = mybir.ActivationFunctionType

P = 128
D = 1024
S = 1024
KD = D // P
NB = S // P
HALF = 512
HD = 64
PAIRS = 4
MEM = 256
XH_HEADS = 4
TQ = 256
NPRM = 25
CA_BACK = 4
CA_KEYS = (CA_BACK + 1) * P
FF_TILES = 22
FF_GROUPS = (8, 8, 6)
ALPHA = 2.0 ** 0.25
LN_EPS = 1e-5
POOL_TILES = 2
OUT_ORDER = (0, 1, 2, 6, 3, 4, 7, 5)
NEG = -1e30
LOWEST = -3.0e38
TWO_PI = 6.283185307179586
RND = 12582912.0
PI_A = 6.28125
PI_B = 1014.0 / 2 ** 19
PI_C = TWO_PI - PI_A - PI_B

FOX_SLOTS, CA_SLOTS = 4, 3
KV_LN1 = (("kv", 0), ("ln", 0), ("kv", 1), ("ln", 1), ("kv", 2), ("ln", 2), ("ln", 3), ("kv", 3),
          ("ln", 4), ("kv", 4), ("ln", 5), ("kv", 5), ("ln", 6), ("ln", 7), ("kv", 6), ("kv", 7))
SLOTS = {"fox": FOX_SLOTS, "ca": CA_SLOTS}
N_FOX = 0
N_CA = N_FOX + FOX_SLOTS * PAIRS
N_EF = N_CA + CA_SLOTS * PAIRS
N_EC = N_EF + 2 * KD
N_ES = N_EC + 2 * KD
N_WO = N_ES + 2 * KD
N_KV = N_WO + KD
N_XQ = N_KV + 2 * KD
N_XO = N_XQ + KD
N_FF = N_XO + KD
N_SMALL = 12
EXP_STEP, SIN_STEP, BP_STEP, BT_STEP, FFEXP_STEP, CUM_STEP = 8, 19, 55, 157, 6, 69


def hybrid_layer(nc, xT, memT, w_ff, b_ff, w_fox, w_ca, w_gate, w_foxo, w_cao, w_glu, w_o,
                 w_kv, w_xq, w_xo, w_up, w_dn0, w_dn1, w_dn2, b_cols, lam_re, lam_im, log_dt,
                 b_re, b_im, c_re, c_im, ssm_d, rel, conv, ln_cols, ln_rows, cum_scratch, out):
    w_dn = (w_dn0, w_dn1, w_dn2)
    with ExitStack() as ctx:
        sems = {}

        def sem(name):
            sems[name] = ctx.enter_context(nc.semaphore(name))
            return sems[name]

        base = 16512
        KB = 1024

        def at(name, kb, cols, dt=F32):
            return nc.alloc_sbuf_tensor_at(name, [P, cols], dt, offset=base + int(kb * KB))

        XH, XL = at("XH", 0, KD * S, F32R), at("XL", 32, KD * S, F32R)
        WR, WH, WL = at("WR", 64, 2 * D), at("WH", 72, 2 * D, F32R), at("WL", 80, 2 * D, F32R)
        YS = at("YS", 88, 4 * S)
        OF, OC = at("OF", 104, 4 * S), at("OC", 120, 4 * S)
        XRAW = at("XRAW", 136, KD * S)
        QT, KT, VT, VV = (at(n, 136 + 4 * j, S) for j, n in enumerate(("QT", "KT", "VT", "VV")))
        MB = at("MB", 152, 2 * S)
        SB = at("SB", 160, 2 * S)
        PT = at("PT", 168, 2 * S)
        K2 = at("K2", 176, S)
        Q2_FIRST_CA, Q2_CA = at("Q2_FIRST_CA", 126, S), at("Q2_CA", 180, S)
        T4 = at("T4", 180, 4 * TQ)
        YG = at("YG", 184, 4 * TQ)
        P4 = at("P4", 188, 4 * TQ)
        HH = at("HH", 192, 4 * TQ)
        BS, CS = at("BS", 196, 256), at("CS", 197, 256)
        W16 = at("W16", 198, 16 * 32)
        WT = at("WT", 120, 2 * 3 * TQ)
        BT, CT = at("BT", 126, 4 * 256), at("CT", 130, 16 * 64)
        PRM = at("PRM", 134, 16 * NPRM)
        BRAW = at("BRAW", 168, 2 * 256)
        BBAR = at("BBAR", 170, 2 * 256)
        CRAW = at("CRAW", 172, 2 * 256)
        BP = at("BP", 184, 2 * 512)
        BTMP = at("BTMP", 188, 256)
        W16T = at("W16T", 190, 2 * 256)
        WFF = at("WFF", 174, 64)
        FFB = at("FFB", 192, S)
        FFE = at("FFE", 180, S)
        OH, OL = at("OH", 136, 4 * S, F32R), at("OL", 152, 4 * S, F32R)
        MT = at("MT", 168, KD * S)
        ML = at("ML", 168, KD * S, F32R)
        MH = at("MH", 104, KD * S, F32R)
        GF = at("GF", 104, S)
        GS, G2 = at("GS", 88, S), at("G2", 92, S)
        RT1 = at("RT1", 136, KD * S)
        XN1 = at("XN1", 168, KD * S)
        XF = {0: at("XF0", 104, 2 * S), 1: at("XF1", 88, 2 * S)}
        MRAW = at("MRAW", 96, KD * MEM)
        MMH, MML = at("MMH", 88, KD * MEM, F32R), at("MML", 96, KD * MEM, F32R)
        KM, VM = at("KM", 120, KD * MEM), at("VM", 128, 2 * D)
        VMT = at("VMT", 112, 2 * MEM)
        QX, Q2X = at("QX", 88, 2 * S), at("Q2X", 96, 3 * HALF)
        SX = at("SX", 104, 2 * MEM)
        VX = at("VX", 108, 2 * MEM)
        OHX, OLX = at("OHX", 136, KD * S, F32R), at("OLX", 168, KD * S, F32R)
        PTX = at("PTX", 112, 2 * 2 * HALF)
        RT2 = at("RT2", 104, KD * S)
        XN2 = at("XN2", 136, KD * S)
        YT = at("YT", 104, KD * S)
        HDH, HDL = at("HDH", 136, KD * S, F32R), at("HDL", 168, KD * S, F32R)
        CV = at("CV", 88, S)
        GL = at("GL", 92, S)
        HF = at("HF", 96, S)
        XN3 = at("XN3", 136, KD * S)
        LGB = at("LGB", 88, 2 * D)
        c0 = 200.25
        IDN = at("IDN", c0, P)
        IDB = at("IDB", c0 + .5, P, BF16)
        CMB = at("CMB", c0 + .75, P, BF16)
        BC = at("BC", c0 + 1, 52)
        CONV = at("CONV", c0 + 1.25, FF_TILES * 4)
        LNC = at("LNC", c0 + 1.625, 6 * KD)
        DC = at("DC", c0 + 1.875, 8)
        PS = at("PS", c0 + 1.9375, 4 * NPRM)
        MX = at("MX", c0 + 2.375, 8)
        ST = at("ST", c0 + 2.5, 8 * 12)
        MV = at("MV", c0 + 2.9375, 8 * 8)
        SP = at("SP", c0 + 3.1875, 16 * 24)
        US = at("US", c0 + 3.1875, S)
        PSN = at("PSN", c0 + 7.1875, NPRM)

        PA = ctx.enter_context(nc.psum_tensor("PA", [P, S], F32))
        PB = ctx.enter_context(nc.psum_tensor("PB", [P, S], F32))
        TB = ctx.enter_context(nc.psum_tensor("TB", [P, S], F32))
        OB = ctx.enter_context(nc.psum_tensor("OB", [P, HALF], F32))
        XB = ctx.enter_context(nc.psum_tensor("XB", [P, HALF], F32))
        PAIR = (PA, PB)

        params = sem("params_loaded")
        wff_loaded = sem("forget_weights_loaded")
        consts = sem("consts_built")
        xraw = [sem(f"x_loaded{h}") for h in range(4)]
        x_hi, x_lo = sem("x_hi"), sem("x_lo")
        raw = [sem(f"w_loaded{b}") for b in range(2)]
        w_hi, w_lo, w_used = sem("w_hi"), sem("w_lo"), sem("w_used")
        su = sem("setup_dve")
        sa = sem("setup_act")
        sp = sem("setup_pool")
        st_pe = sem("setup_pe")
        cum_out = sem("cum_stored")
        half_done = sem("projection_half_done")
        xq_staged = sem("xa_q_staged")
        q_staged, k_staged = sem("q_staged"), sem("k_staged")
        spv = lambda j: SP[:, 16 * j:16 * j + 16]

        def pair(b):
            return PAIR[b % 2]

        def split_hi(act, n, b, raw_count, after_last=False):
            act.wait_ge(raw[b], 16 * raw_count)
            act.wait_ge(w_used, n + (2 if after_last else 1))
            act.activation(WH[:, b * D:(b + 1) * D], WR[:, b * D:(b + 1) * D],
                           ACT.Copy).then_inc(w_hi, 1)

        def split_lo(eng, n, b):
            eng.wait_ge(w_hi, n + 1)
            eng.tensor_tensor(WL[:, b * D:(b + 1) * D], WR[:, b * D:(b + 1) * D],
                              WH[:, b * D:(b + 1) * D].bitcast(F32), ALU.subtract).then_inc(w_lo, 1)

        def product(pe, n, b, dst, xh, xl, nk=KD, width=S, k0=0, before=None):
            pe.wait_ge(w_lo, n + 3)
            for k in range(nk):
                if before:
                    before(k)
                w0 = b * D + (k0 + k) * P
                for pas, (w, x) in enumerate(((WH, xh), (WH, xl), (WL, xh))):
                    for t in range(0, width, HALF):
                        tw = min(HALF, width - t)
                        mm = pe.matmul(dst[:, t:t + tw], w[:, w0:w0 + P],
                                       x[:, k * width + t:k * width + t + tw],
                                       start=(k == 0 and pas == 0), stop=(k == nk - 1 and pas == 2))
            return mm

        def attention_events(tag):
            names = ("proj_ready", "s_ready", "s_summed", "nmax_ready", "exp_done", "rsum_ready",
                     "p_ready", "t_ready", "t_copied", "pv_done", "o_copied")
            return {n: sem(f"{tag}_{n}") for n in names}

        fox, ca = attention_events("fox"), attention_events("ca")
        mb_loaded = {"fox": [sem(f"fox_rows_loaded{h}") for h in range(2)],
                     "ca": [sem(f"ca_bias_loaded{h}") for h in range(2)]}
        ca_masked = sem("ca_bias_masked")
        CHUNKS = 26

        def key_blocks(kind, blk):
            return list(range(0 if kind == "fox" else max(0, blk - CA_BACK), blk + 1))

        def cut(blocks):
            return [blocks[a:a + 4] for a in range(0, len(blocks), 4)]

        def first_chunk(kind, u):
            return 2 + sum(len(cut(key_blocks(kind, v % NB))) for v in range(u))

        assert first_chunk("fox", 16) == CHUNKS and first_chunk("ca", 16) == CHUNKS

        def pe_scores(pe, kind, ev, u):
            hh, blk = divmod(u, NB)
            kb = key_blocks(kind, blk)
            r = slice(HD * hh, HD * hh + HD)
            dst = PA
            n = len(kb) * P
            for c in range(0, n, HALF):
                w = min(HALF, n - c)
                last = c + w == n and kind == "fox"
                mm = pe.matmul(dst[:, c:c + w], QT[r, blk * P:(blk + 1) * P],
                               KT[r, kb[0] * P + c:kb[0] * P + c + w], start=True, stop=not last)
            if kind == "fox":
                mm = pe.matmul(dst[:, n - P:n], IDB[:, :], CMB[:, :], start=False, stop=True)
            mm.then_inc(ev["s_ready"], 1)

        def pe_transposes(pe, kind, ev, i, u):
            pe.wait_ge(ev["p_ready"], 16 * i + u + 1)
            c = first_chunk(kind, u)
            for j, blocks in enumerate(cut(key_blocks(kind, u % NB))):
                pe.wait_ge(ev["t_copied"], CHUNKS * i + c + j - 1)
                bank = (c + j) % 2 * HALF
                for m in range(len(blocks)):
                    col = (u % 2) * S + (4 * j + m) * P
                    mm = pe.transpose(TB[:, bank + m * P:bank + (m + 1) * P], SB[:, col:col + P],
                                      IDN[:, :])
                mm.then_inc(ev["t_ready"], 1)

        def pe_values(pe, kind, ev, i, u):
            hh, blk = divmod(u, NB)
            kb = key_blocks(kind, blk)
            pe.wait_ge(ev["t_copied"], CHUNKS * i + first_chunk(kind, u + 1))
            if u % 4 == 0 and u:
                pe.wait_ge(ev["o_copied"], 4 * i + u // 4)
            for m, key in enumerate(kb):
                mm = pe.matmul(OB[HD * hh:HD * hh + HD, blk % 4 * P:(blk % 4 + 1) * P],
                               VV[:, key * P + HD * hh:key * P + HD * hh + HD],
                               PT[:, (u % 2) * S + m * P:(u % 2) * S + (m + 1) * P],
                               start=(m == 0), stop=(m == len(kb) - 1))
            mm.then_inc(ev["pv_done"], 1)

        def pe_turn_v(pe, kind, ev, i):
            pe.wait_ge(ev["proj_ready"], 2 * SLOTS[kind] * i + 6)
            for j in range(2):
                for m in range(4):
                    mm = pe.transpose(TB[:, j * HALF + m * P:j * HALF + (m + 1) * P],
                                      VT[:, (4 * j + m) * P:(4 * j + m + 1) * P], IDN[:, :])
                mm.then_inc(ev["t_ready"], 1)

        PIECES = 48
        EVENTS = {"fox": fox, "ca": ca}

        def slot_of(kind, p, k):
            return (N_FOX if kind == "fox" else N_CA) + SLOTS[kind] * p + k

        def filled(kind, p, k):
            return (FOX_SLOTS * (p - 1) if kind == "fox" else FOX_SLOTS * (PAIRS - 1) + CA_SLOTS * p) + k

        def staged_before(kind, p):
            return p - 1 if kind == "fox" else PAIRS - 1 + p

        def halves_ending(kind, u):
            per = PIECES // (2 * SLOTS[kind])
            return [divmod(h, 2) for h in range(2 * SLOTS[kind]) if ((h + 1) * per - 1) // 3 == u]

        def bank_of(banks, h):
            return h % 2 * HALF if banks == 2 else 0

        def pe_piece(pe, fill, g):
            if fill is None:
                return
            kind, p, banks = fill
            per = PIECES // (2 * SLOTS[kind])
            size = 3 * KD // per
            h, at_ = divmod(g, per)
            k, t = divmod(h, 2)
            n, b = slot_of(kind, p, k), k % 2
            if at_ == 0:
                if t == 0:
                    pe.wait_ge(w_lo, n + 3)
                if kind == "ca" and banks == 1 and h == 0:
                    pe.wait_ge(fox["proj_ready"], 2 * FOX_SLOTS * PAIRS)
                elif not (banks == 2 and h == 0):
                    pe.wait_ge(EVENTS[kind]["proj_ready"], 2 * SLOTS[kind] * p + h - (banks - 1))
            for j in range(at_ * size, (at_ + 1) * size):
                k0, pas = divmod(j, 3)
                w, x = ((WH, XH), (WH, XL), (WL, XH))[pas]
                w0, x0 = b * D + k0 * P, k0 * S + t * HALF
                mm = pe.matmul(PB[:, bank_of(banks, h):bank_of(banks, h) + HALF], w[:, w0:w0 + P],
                               x[:, x0:x0 + HALF], start=(j == 0), stop=(j == 3 * KD - 1))
            if at_ == per - 1:
                mm.then_inc(w_used if t else half_done, 1)

        def act_projection(act, fill, k, t):
            kind, p, banks = fill
            n = slot_of(kind, p, k)
            if t == 0:
                act.wait_ge(half_done, filled(kind, p, k) + 1)
            else:
                act.wait_ge(w_used, n + 3)
            sl = slice(t * HALF, (t + 1) * HALF)
            if k == 0:
                if kind == "fox":
                    dst = OF[:, bass.ds(p * S + t * HALF, HALF)]
                elif banks == 1:
                    act.wait_ge(staged, 5 * PAIRS)
                    dst = Q2_FIRST_CA[:, sl]
                else:
                    dst = Q2_CA[:, sl]
            elif k == 1:
                act.wait_ge(k_staged, staged_before(kind, p) + 1)
                dst = K2[:, sl]
            elif k == 2:
                dst = VT[:, sl]
            else:
                dst = YS[:, bass.ds(p * S + t * HALF, HALF)]
            bank = bank_of(banks, 2 * k + t)
            act.sem_inc(act_waits, 1)
            c0_ = 0 if kind == "fox" else FOX_SLOTS * PAIRS
            act.activation(dst, PB[:, bank:bank + HALF], ACT.Identity,
                           bias=BC[:, bass.ds(c0_ + SLOTS[kind] * p + k, 1)],
                           scale=0.125 if k == 0 else 1.0).then_inc(EVENTS[kind]["proj_ready"], 1)
            if t == 1:
                for m, b, count, after_last in next_splits(kind, p, k):
                    split_hi(act, m, b, count, after_last)

        def next_splits(kind, p, k):
            n = slot_of(kind, p, k)
            if kind == "fox":
                return [(n + 2, k % 2, 2 * p + (k + 2) // 2 + 1, False)]
            if k == 0:
                return [(n + 2, 0, 2 * PAIRS + 2 * p + 2, False)]
            if k == 1:
                return []
            return [(n + 1, 0, 2 * PAIRS + 2 * p + 3, True), (n + 2, 1, 2 * PAIRS + p + 2, False)]

        def stage_source(fill):
            kind, p, banks = fill
            if kind == "fox":
                return OF[:, bass.ds(p * S, S)]
            return (Q2_FIRST_CA if banks == 1 else Q2_CA)[:, :]

        def pe_attention(pe, kind, i, fill):
            ev = EVENTS[kind]
            ssm = kind == "fox"
            pe_turn_v(pe, kind, ev, i)
            if ssm:
                pe_ssm_in(pe, i, 0)
            pe.wait_ge(ev["s_summed"], 16 * i + 17)
            pe_scores(pe, kind, ev, 1)
            for u in range(16):
                if ssm and u < 15:
                    pe_ssm_in(pe, i, u + 1)
                pe_piece(pe, fill, 3 * u)
                if u:
                    pe_values(pe, kind, ev, i, u - 1)
                pe_transposes(pe, kind, ev, i, u)
                if u < 14:
                    pe.wait_ge(ev["s_summed"], 16 * i + u + 18)
                    pe_scores(pe, kind, ev, u + 2)
                elif u == 15 and fill:
                    pe.wait_ge(q_staged, staged_before(fill[0], fill[1]) + 1)
                    pe.wait_ge(k_staged, staged_before(fill[0], fill[1]) + 2)
                    pe.wait_ge(ev["s_summed"], 16 * i + 32)
                    pe_scores(pe, fill[0], EVENTS[fill[0]], 0)
                if ssm and u:
                    pe_ssm_out(pe, i, u - 1)
                pe_piece(pe, fill, 3 * u + 1)
                pe_piece(pe, fill, 3 * u + 2)
            pe_values(pe, kind, ev, i, 15)
            if ssm:
                pe_ssm_out(pe, i, 15)

        def act_attention(act, kind, i, dst, fill):
            ev = EVENTS[kind]
            act_copy_v(act, ev, i)
            act_exp(act, kind, ev, i, 0)
            for u in range(16):
                if u % 4 == 0 and u:
                    act_copy_o(act, ev, i, u // 4 - 1, dst)
                act_copy_turned(act, kind, ev, i, u)
                if u < 15:
                    act_exp(act, kind, ev, i, u + 1)
                if fill:
                    for k, t in halves_ending(fill[0], u):
                        act_projection(act, fill, k, t)
                    if u == 14:
                        act.wait_ge(ev["s_ready"], 16 * i + 16)
                        act.wait_ge(EVENTS[fill[0]]["proj_ready"], 2 * SLOTS[fill[0]] * fill[1] + 2)
                        act.sem_inc(act_waits, 1)
                        act.activation(QT[:, :], stage_source(fill), ACT.Copy).then_inc(q_staged, 1)
            act_copy_o(act, ev, i, 3, dst)

        def dve_attention(dve, kind, i, fill):
            ev = EVENTS[kind]
            ssm = kind == "fox"
            dve_rowmax(dve, kind, ev, i, 0)
            if ssm:
                dve_stage(dve, i)
                dve.wait_ge(staged, 5 * i + 5)
                dve_ssm(dve, i, 0)
            for u in range(16):
                dve_normalise(dve, kind, ev, i, u)
                if u < 15:
                    dve_rowmax(dve, kind, ev, i, u + 1)
                if u == 14 and fill:
                    dve.tensor_copy(KT[:, :], K2[:, :]).then_inc(k_staged, 1)
                if ssm:
                    dve_ssm(dve, i, u + 1, more=fill[0] == "fox")
                if fill and u:
                    for k, t in halves_ending(fill[0], u - 1):
                        if t == 1:
                            for m, b, _, _ in next_splits(fill[0], fill[1], k):
                                split_lo(dve, m, b)
            if ssm:
                dve_ssm(dve, i, NQ + 1)
            if fill:
                for k, t in halves_ending(fill[0], 15):
                    if t == 1:
                        for m, b, _, _ in next_splits(fill[0], fill[1], k):
                            split_lo(dve, m, b)

        def dve_rowmax(dve, kind, ev, i, u):
            hh, blk = divmod(u, NB)
            kb = key_blocks(kind, blk)
            n, b = len(kb) * P, u % 2
            if blk == 0:
                if kind == "fox":
                    dve.wait_ge(mb_loaded["fox"][hh], 16 * i + 16)
                else:
                    dve.wait_ge(ca_masked, 4 * i + 2 * hh + 3)
            col = hh * S + (0 if kind == "fox" else (kb[0] - blk + CA_BACK) * P)
            dve.wait_ge(ev["s_ready"], 16 * i + u + 1)
            dve.sem_inc(scores_seen, 1)
            dve.tensor_tensor_reduce(SB[:, b * S:b * S + n], PA[:, 0:n], MB[:, col:col + n],
                                     1.0, LOWEST, ALU.add, ALU.max,
                                     MX[:, b:b + 1]).then_inc(ev["s_summed"], 1)
            dve.wait_ge(ev["s_summed"], 16 * i + u + 17)
            dve.tensor_scalar(MX[:, 2 + b:3 + b], MX[:, b:b + 1], -1.0, None,
                              ALU.mult).then_inc(ev["nmax_ready"], 1)

        def dve_normalise(dve, kind, ev, i, u):
            b = u % 2
            n = len(key_blocks(kind, u % NB)) * P
            dve.wait_ge(ev["exp_done"], 16 * i + u + 1)
            dve.reciprocal(MX[:, 6 + b:7 + b], MX[:, 4 + b:5 + b]).then_inc(ev["rsum_ready"], 1)
            dve.wait_ge(ev["rsum_ready"], 16 * i + u + 1)
            dve.tensor_scalar(SB[:, b * S:b * S + n], SB[:, b * S:b * S + n],
                              MX[:, 6 + b:7 + b], None, ALU.mult).then_inc(ev["p_ready"], 1)

        def act_exp(act, kind, ev, i, u):
            b = u % 2
            n = len(key_blocks(kind, u % NB)) * P
            act.wait_ge(ev["nmax_ready"], 16 * i + u + 1)
            act.activation(SB[:, b * S:b * S + n], SB[:, b * S:b * S + n], ACT.Exp,
                           bias=MX[:, 2 + b:3 + b],
                           accum_out=MX[:, 4 + b:5 + b]).then_inc(ev["exp_done"], 1)

        def act_copy_turned(act, kind, ev, i, u):
            c = first_chunk(kind, u)
            for j, blocks in enumerate(cut(key_blocks(kind, u % NB))):
                if j == 0 and u >= 2:
                    act.wait_ge(ev["pv_done"], 16 * i + u - 1)
                act.wait_ge(ev["t_ready"], CHUNKS * i + c + j + 1)
                w, bank, col = len(blocks) * P, (c + j) % 2 * HALF, (u % 2) * S + 4 * j * P
                act.activation(PT[:, col:col + w], TB[:, bank:bank + w],
                               ACT.Copy).then_inc(ev["t_copied"], 1)

        def act_copy_v(act, ev, i):
            for j in range(2):
                act.wait_ge(ev["t_ready"], CHUNKS * i + j + 1)
                act.activation(VV[:, j * HALF:(j + 1) * HALF], TB[:, j * HALF:(j + 1) * HALF],
                               ACT.Copy).then_inc(ev["t_copied"], 1)

        def act_copy_o(act, ev, i, g, dst):
            r = slice(HD * (g // 2), HD * (g // 2) + HD)
            act.wait_ge(ev["pv_done"], 16 * i + 4 * g + 4)
            act.activation(dst[r, bass.ds(i * S + g % 2 * HALF, HALF)], OB[r, :],
                           ACT.Copy).then_inc(ev["o_copied"], 1)

        NQ = 16
        staged = sem("ssm_params_staged")
        table_step = sem("ssm_table_step")
        next_staged = sem("ssm_next_table_staged")
        x_ready = sem("ssm_bu_ready")
        turned = sem("ssm_bu_turned")
        yadd = sem("ssm_input_ready")
        scanned = sem("ssm_scanned")
        back = sem("ssm_back_turned")
        h_ready = sem("ssm_state_ready")
        y_ready = sem("ssm_ch_ready")
        y_done = sem("ssm_y_done")
        TSTEPS = 1 + 4 * 2 + 1
        YB = PB[:, HALF:HALF + TQ]

        def pe_ssm_in(pe, i, k):
            tau, q = divmod(k, 4)
            r = slice(32 * tau, 32 * tau + 32)
            if k == 0:
                pe.wait_ge(staged, 5 * i + 5)
            else:
                pe.wait_ge(turned, NQ * i + k)
            for m in range(2):
                mm = pe.matmul(XB[:, m * TQ:(m + 1) * TQ], BS[r, m * P:(m + 1) * P],
                               US[r, q * TQ:(q + 1) * TQ], start=True, stop=True)
            mm.then_inc(x_ready, 1)

        def pe_ssm_out(pe, i, k):
            tau = k // 4
            pe.wait_ge(h_ready, NQ * i + k + 1)
            pe.wait_ge(y_done, NQ * i + k + 1)
            for m in range(2):
                h0 = (k % 2) * 2 * TQ + m * TQ
                mm = pe.matmul(YB[32 * tau:32 * tau + 32, :],
                               CS[:, tau * 64 + m * 32:tau * 64 + m * 32 + 32],
                               HH[:, h0:h0 + TQ], start=(m == 0), stop=(m == 1))
            mm.then_inc(y_ready, 1)

        def dve_table(dve, i, tau, part, prm):
            b = tau % 2 * 3 * TQ
            s0 = (4 * i + tau) * TSTEPS
            wr = lambda a, n: WT[:, b + a:b + a + n]
            wi = lambda a, n: WT[:, b + TQ + a:b + TQ + a + n]
            tmp = lambda m, n: T4[:, m * TQ:m * TQ + n]
            if part == 0:
                dve.tensor_copy(WT[:, b:b + 2 * TQ].rearrange("p (c t) -> p c t", c=2)[:, :, 0:16],
                                W16[:, bass.ds(i * 128 + tau * 32, 32)].rearrange(
                                    "p (c t) -> p c t", c=2)).then_inc(table_step, 1)
            for m in ((4, 5), (6,), (7,))[part]:
                n, s1 = 2 ** m, s0 + 1 + 2 * (m - 4)
                er, ei, ne = (prm[:, 8 * c + m:8 * c + m + 1] for c in range(3))
                dve.wait_ge(table_step, s1)
                dve.tensor_scalar(tmp(0, n), wi(0, n), ne, None, ALU.mult)
                dve.tensor_scalar(tmp(1, n), wi(0, n), er, None, ALU.mult).then_inc(table_step, 1)
                dve.wait_ge(table_step, s1 + 1)
                dve.scalar_tensor_tensor(wr(n, n), wr(0, n), er, tmp(0, n), ALU.mult, ALU.add)
                dve.scalar_tensor_tensor(wi(n, n), wr(0, n), ei, tmp(1, n), ALU.mult,
                                         ALU.add).then_inc(table_step, 1)
            dve.wait_ge(table_step, s0 + (5, 7, 9)[part])
            if part == 2:
                dve.tensor_copy(WT[:, b + 2 * TQ:b + 3 * TQ], wr(0, TQ)).then_inc(table_step, 1)

        def prm_of(tau):
            return PS[:, tau * NPRM:(tau + 1) * NPRM]

        def dve_stage(dve, i):
            dve.wait_ge(y_done, NQ * i + 1)
            dve.tensor_copy(BS[:, :], BT[:, bass.ds(i * 256, 256)]).then_inc(staged, 1)
            dve.tensor_copy(CS[:, :], CT[:, bass.ds(i * 256, 256)]).then_inc(staged, 1)
            dve.tensor_copy(PS[:, :], PRM[:, bass.ds(i * 4 * NPRM, 4 * NPRM)]).then_inc(staged, 1)
            dve.tensor_copy(DC[:, 4:5], DC[:, bass.ds(i, 1)]).then_inc(staged, 1)
            dve.wait_ge(fox["proj_ready"], 8 * i + 8)
            dve.tensor_copy(US[:, :], YS[:, bass.ds(i * S, S)]).then_inc(staged, 1)

        def dve_ssm(dve, i, k, more=False):
            if k < NQ:
                tau, q = divmod(k, 4)
                w = tau % 2 * 3 * TQ
                if q == 0:
                    dve.wait_ge(table_step, (4 * i + tau + 1) * TSTEPS)
                if k:
                    dve.wait_ge(yadd, 2 * NQ * i + 2 * k)
                if tau < 3 and q:
                    dve_table(dve, i, tau + 1, q - 1, prm_of(tau + 1))
                elif more and q:
                    if q == 1:
                        dve.tensor_copy(PSN[:, :], PRM[:, bass.ds((i + 1) * 4 * NPRM, NPRM)]
                                        ).then_inc(next_staged, 1)
                        dve.wait_ge(next_staged, i + 1)
                    dve_table(dve, i + 1, 0, q - 1, PSN)
                dve.wait_ge(x_ready, NQ * i + k + 1)
                dve.tensor_tensor(T4[:, 0:2 * TQ], XB[:, :], WT[:, w:w + 2 * TQ], ALU.mult)
                dve.tensor_tensor(T4[:, 2 * TQ:4 * TQ], XB[:, :], WT[:, w + TQ:w + 3 * TQ],
                                  ALU.mult).then_inc(turned, 1)
            if 0 <= k - 1 < NQ:
                j = k - 1
                tau, q = divmod(j, 4)
                w, g = tau % 2 * 3 * TQ, j % 2 * 2 * TQ
                decay = PS[:, tau * NPRM + 24:tau * NPRM + 25].to_broadcast([P, TQ])
                dve.wait_ge(yadd, 2 * NQ * i + 2 * j + 2)
                if j:
                    dve.wait_ge(h_ready, NQ * i + j)
                for m in range(2):
                    h0 = (1 - j % 2) * 2 * TQ + (m + 1) * TQ - 1
                    sc = dve.tensor_tensor_scan(YG[:, g + m * TQ:g + (m + 1) * TQ], decay,
                                                YG[:, g + m * TQ:g + (m + 1) * TQ],
                                                HH[:, h0:h0 + 1] if q else 0.0, ALU.mult, ALU.add)
                sc.then_inc(scanned, 1)
                dve.wait_ge(scanned, NQ * i + j + 1)
                dve.tensor_tensor(P4[:, 0:2 * TQ], YG[:, g:g + 2 * TQ], WT[:, w:w + 2 * TQ], ALU.mult)
                dve.tensor_tensor(P4[:, 2 * TQ:4 * TQ], YG[:, g:g + 2 * TQ],
                                  WT[:, w + TQ:w + 3 * TQ], ALU.mult).then_inc(back, 1)
            if 0 <= k - 2 < NQ:
                j = k - 2
                tau, q = divmod(j, 4)
                r = slice(32 * tau, 32 * tau + 32)
                dve.wait_ge(y_ready, NQ * i + j + 1)
                u = YS[r, bass.ds(i * S + q * TQ, TQ)]
                dve.scalar_tensor_tensor(u, u, DC[r, 4:5], YB[r, :], ALU.mult, ALU.add).then_inc(y_done, 1)

        def pool_ssm(pool, i, k):
            if k < NQ:
                g = k % 2 * 2 * TQ
                pool.wait_ge(turned, NQ * i + k + 1)
                if k >= 2:
                    pool.wait_ge(back, NQ * i + k - 1)
                pool.tensor_tensor(YG[:, g:g + TQ], T4[:, 0:TQ], T4[:, TQ:2 * TQ],
                                   ALU.add).then_inc(yadd, 1)
                pool.tensor_tensor(YG[:, g + TQ:g + 2 * TQ], T4[:, 3 * TQ:4 * TQ],
                                   T4[:, 2 * TQ:3 * TQ], ALU.subtract).then_inc(yadd, 1)
            if k:
                j = k - 1
                h = j % 2 * 2 * TQ
                pool.wait_ge(back, NQ * i + j + 1)
                if j >= 2:
                    pool.wait_ge(y_ready, NQ * i + j - 1)
                pool.tensor_tensor(HH[:, h:h + TQ], P4[:, 0:TQ], P4[:, TQ:2 * TQ], ALU.subtract)
                pool.tensor_tensor(HH[:, h + TQ:h + 2 * TQ], P4[:, 2 * TQ:3 * TQ],
                                   P4[:, 3 * TQ:4 * TQ], ALU.add).then_inc(h_ready, 1)

        g_ready = {t: sem(f"{t}_gate_ready") for t in ("ef", "ec", "es")}
        o_hi = {t: sem(f"{t}_branch_hi") for t in ("ef", "ec", "es")}
        o_lo = {t: sem(f"{t}_branch_lo") for t in ("ef", "ec", "es")}
        m_step = {t: sem(f"{t}_merge_step") for t in ("ef", "ec", "es")}
        m_hi, m_lo = sem("merged_hi"), sem("merged_lo")
        y_act = sem("ssm_gelu")
        rt_step = {t: sem(f"{t}_residual_step") for t in ("wo", "xo")}
        mem_loaded, mem_hi, mem_lo = sem("mem_loaded"), sem("mem_hi"), sem("mem_lo")
        kv_ready = sem("kv_ready")
        v_turned, v_ready = sem("mem_v_turned"), sem("mem_v_ready")
        lns = [{n: sem(f"ln{k}_{n}") for n in
                ("turned", "copied", "step", "sqrt", "normed", "back", "scaled", "hi", "lo")}
               for k in range(3)]
        xa = {n: sem(f"xa_{n}") for n in ("q_ready", "v_staged", "s_ready", "max", "nmax", "exp",
                                          "rsum", "p_ready", "t_ready", "t_copied", "pv", "hi", "lo")}
        cv_step, gelu_done, hid, hid_hi, hid_lo, y_sum = (sem(n) for n in (
            "conv_step", "gelu_done", "hidden_ready", "hidden_hi", "hidden_lo", "down_added"))
        final_scaled, final_pool = sem("final_scaled"), sem("final_pool")
        rows_loaded, final_step, out_stored = sem("ln_rows_loaded"), sem("final_step"), sem("out_stored")
        scores_seen, masks_due, act_waits = sem("scores_seen"), sem("masks_due"), sem("act_waits")

        def rc(n0, k):
            return (16 if k % 2 == 0 else 12) + (n0 - N_EF) // 2 + k // 2 + 1

        RES = {"wo": (RT1, N_WO), "xo": (RT2, N_XO)}

        def pe_ln_forward(pe, ln, rt, tau, ready):
            if tau == 0:
                pe.wait_ge(*ready)
            if tau >= 2:
                pe.wait_ge(ln["copied"], tau - 1)
            for j in range(KD):
                mm = pe.transpose(pair(tau)[:, j * P:(j + 1) * P],
                                  rt[:, j * S + tau * P:j * S + (tau + 1) * P], IDN[:, :])
            mm.then_inc(ln["turned"], 1)

        def act_ln_copy(act, ln, xn, tau):
            act.wait_ge(ln["turned"], tau + 1)
            act.activation(xn[:, tau * D:(tau + 1) * D], pair(tau)[:, :], ACT.Copy).then_inc(ln["copied"], 1)

        def dve_ln_stats(dve, ln, xn, tau):
            dve.wait_ge(ln["copied"], tau + 1)
            for h in range(2):
                dve.bn_stats(ST[:, tau * 12 + 6 * h:tau * 12 + 6 * h + 6],
                             xn[:, tau * D + h * HALF:tau * D + (h + 1) * HALF]).then_inc(ln["step"], 1)
            dve.wait_ge(ln["step"], 3 * tau + 2)
            dve.bn_aggr(MV[:, 2 * tau:2 * tau + 2], ST[:, tau * 12:tau * 12 + 12]).then_inc(ln["step"], 1)

        mean = lambda tau: MV[:, 2 * tau:2 * tau + 1]
        var = MV[:, 0:16].rearrange("p (t c) -> p t c", c=2)[:, :, 1]
        sd, rstd, tmp8 = (MV[:, 16 + 8 * j:24 + 8 * j] for j in range(3))

        def act_ln_sqrt(act, ln):
            act.wait_ge(ln["step"], 25)
            act.activation(sd, var, ACT.Sqrt).then_inc(ln["sqrt"], 1)

        def rstd_chain(dve, ln):
            step = ln["step"]

            def link(ins, n):
                ins.then_inc(step, 1)
                dve.wait_ge(step, n)

            dve.wait_ge(step, 24)
            link(dve.tensor_scalar(var, var, LN_EPS, None, ALU.add), 25)
            dve.wait_ge(ln["sqrt"], 1)
            link(dve.reciprocal(rstd, sd), 26)
            link(dve.tensor_tensor(tmp8, rstd, rstd, ALU.mult), 27)
            link(dve.tensor_tensor(tmp8, tmp8, var, ALU.mult), 28)
            link(dve.tensor_scalar(tmp8, tmp8, -0.5, 1.5, ALU.mult, ALU.add), 29)
            link(dve.tensor_tensor(rstd, rstd, tmp8, ALU.mult), 30)

        def dve_ln_normalise(dve, ln, xn, between=None):
            rstd_chain(dve, ln)
            if between:
                between()
            for tau in range(NB):
                x = xn[:, tau * D:(tau + 1) * D]
                dve.tensor_scalar(x, x, mean(tau), rstd[:, tau:tau + 1], ALU.subtract,
                                  ALU.mult).then_inc(ln["normed"], 1)

        LN_BANKS = {0: [(PA[:, 0:HALF], PA[:, HALF:S]), (PB[:, 0:HALF], PB[:, HALF:S])],
                    1: [(TB[:, 0:HALF], TB[:, HALF:S]), (OB[:, :], XB[:, :]),
                        (PB[:, 0:HALF], PB[:, HALF:S])]}

        def pe_ln_back(pe, which, xn, k):
            ln = lns[which]
            if k == 0:
                pe.wait_ge(ln["normed"], NB)
            sets = len(LN_BANKS[which])
            if k >= sets:
                pe.wait_ge(ln["scaled"], 2 * (k - sets + 1))
            for tau in range(NB):
                mm = pe.transpose(LN_BANKS[which][k % sets][tau // 4][:, tau % 4 * P:tau % 4 * P + P],
                                  xn[:, tau * D + k * P:tau * D + (k + 1) * P], IDN[:, :])
            mm.then_inc(ln["back"], 1)

        def act_ln_scale(act, which, k):
            ln = lns[which]
            g, b = (LNC[:, (2 * which + c) * KD + k:(2 * which + c) * KD + k + 1] for c in range(2))
            act.wait_ge(ln["back"], k + 1)
            if k >= 2:
                act.wait_ge(ln["lo"], k - 1)
            for h in range(2):
                act.activation(XF[which][:, k % 2 * S + h * HALF:k % 2 * S + (h + 1) * HALF],
                               LN_BANKS[which][k % len(LN_BANKS[which])][h], ACT.Identity,
                               bias=b, scale=g).then_inc(ln["scaled"], 1)

        def dve_ln_split(dve, which, k):
            ln = lns[which]
            f = XF[which][:, k % 2 * S:(k % 2 + 1) * S]
            h = XH[:, k * S:(k + 1) * S]
            dve.wait_ge(ln["scaled"], 2 * k + 2)
            dve.tensor_copy(h, f).then_inc(ln["hi"], 1)
            dve.wait_ge(ln["hi"], k + 1)
            dve.tensor_tensor(XL[:, k * S:(k + 1) * S], f, h.bitcast(F32),
                              ALU.subtract).then_inc(ln["lo"], 1)

        block = ctx.enter_context(nc.Block())

        @block.sync
        def _(sp_):
            def load(n, b, src, width=D, after_last=False, free=True):
                if free:
                    sp_.wait_ge(w_lo, n + (2 if after_last else 1))
                sp_.dma_start(WR[:, b * D:b * D + width], src).then_inc(raw[b], 16)

            for h in range(4):
                if h in (0, 2):
                    load(h // 2, h // 2, w_fox[h // 2], free=False)
                sp_.dma_start(XRAW[:, h * 2 * S:(h + 1) * 2 * S].rearrange("p (k t) -> p k t", k=2),
                              xT[2 * h:2 * h + 2].rearrange("k p t -> p k t")).then_inc(xraw[h], 16)
            for k in range(2, FOX_SLOTS):
                load(k, k % 2, w_fox[k])
            with sp_.Fori(1, PAIRS) as i:
                for k in range(FOX_SLOTS):
                    load(FOX_SLOTS * i + k, k % 2, w_fox[FOX_SLOTS * i + k])
            with sp_.Fori(0, PAIRS) as i:
                for k in range(CA_SLOTS):
                    load(N_CA + CA_SLOTS * i + k, k % 2, w_ca[CA_SLOTS * i + k], after_last=(k == 0))
            sp_.wait_ge(w_lo, N_EF + 2)
            for br, (n0, src, width) in enumerate(((N_EF, w_foxo, HALF), (N_EC, w_cao, HALF),
                                                   (N_ES, w_glu, D))):
                with sp_.Fori(0, KD) as i:
                    load(n0 + 2 * i, 0, w_gate[KD * br + i])
                    load(n0 + 2 * i + 1, 1, src[i], width)
            sp_.wait_ge(o_lo["es"], 4)
            sp_.dma_start(MRAW[:, :].rearrange("p (k t) -> p k t", k=KD),
                          memT.rearrange("k p t -> p k t")).then_inc(mem_loaded, 16)
            for n0, src, count in ((N_WO, w_o, KD), (N_KV, w_kv, 2 * KD), (N_XQ, w_xq, KD),
                                   (N_XO, w_xo, KD)):
                with sp_.Fori(0, count // 2) as i:
                    for k in range(2):
                        load(n0 + 2 * i + k, k, src[2 * i + k])
            n0, t0 = N_FF, 0
            for g, tiles in enumerate(FF_GROUPS):
                with sp_.Fori(0, tiles) as i:
                    for k in range(2):
                        load(n0 + 2 * i + k, k, w_up[2 * t0 + 2 * i + k])
                n0, t0 = n0 + 2 * tiles, t0 + tiles
                with sp_.Fori(0, KD // 2) as i:
                    for k in range(2):
                        load(n0 + 2 * i + k, k, w_dn[g][2 * i + k], tiles * P)
                n0 += KD
            for tau in OUT_ORDER:
                if tau < NB - POOL_TILES:
                    sp_.wait_ge(final_step, tau + 1)
                else:
                    sp_.wait_ge(final_pool, tau - (NB - POOL_TILES) + 1)
                sp_.dma_start(out[0, tau * P:(tau + 1) * P, :],
                              XN3[:, tau * D:(tau + 1) * D]).then_inc(out_stored, 16)
            sp_.wait_ge(out_stored, 16 * NB)

        @block.gpsimd
        def _(pool):
            pool.memset(IDN[:, :], 0.0)
            pool.memset(IDB[:, :], 0.0)
            pool.memset(CMB[:, :], 0.0)
            pool.memset(BP[:, :], 0.0)
            pool.memset(CT[:, :], 0.0).then_inc(sp, 1)
            pool.wait_ge(sp, 1)
            pool.affine_select(out=IDN[:, :], in_=IDN[:, :], compare_op=ALU.not_equal, fill=1.0,
                               base=0, pattern=[[-1, P]], channel_multiplier=1)
            pool.affine_select(out=IDB[:, :], in_=IDB[:, :], compare_op=ALU.not_equal, fill=1.0,
                               base=0, pattern=[[-1, P]], channel_multiplier=1)
            pool.affine_select(out=CMB[:, :], in_=CMB[:, :], compare_op=ALU.is_ge, fill=NEG,
                               base=0, pattern=[[-1, P]], channel_multiplier=1).then_inc(consts, 1)
            pool.engine_nop().then_inc(fox["s_summed"], 16)
            pool.engine_nop().then_inc(ca["s_summed"], 16)
            pool.engine_nop().then_inc(ca_masked, 1)
            for n in (2, 3):
                split_lo(pool, n, n % 2)
            pool.wait_ge(su, CUM_STEP)
            pool.dma_start(cum_scratch, FFE[0:8, :]).then_inc(cum_out, 16)
            pool.wait_ge(cum_out, 16)
            pool.wait_ge(w_used, 3)

            def rows(i, hh):
                pool.wait_ge(fox["s_summed"], 16 * i + 8 * hh + 8)
                pool.dma_start(MB[:, hh * S:(hh + 1) * S],
                               cum_scratch[bass.ds(2 * i + hh, 1), :].partition_broadcast(P)
                               ).then_inc(mb_loaded["fox"][hh], 16)

            rows(0, 0)
            with pool.Fori(0, PAIRS - 1) as i:
                rows(i, 1)
                for k in range(NQ + 1):
                    pool_ssm(pool, i, k)
                    if k == 12:
                        rows(i + 1, 0)
            rows(PAIRS - 1, 1)
            for k in range(NQ + 1):
                pool_ssm(pool, PAIRS - 1, k)
            pool.wait_ge(h_ready, NQ * PAIRS)
            with pool.Fori(0, PAIRS) as i:
                for hh in range(2):
                    pool.wait_ge(ca["s_summed"], 16 * i + 8 * hh + 8)
                    pool.wait_ge(fox["s_summed"], 16 * PAIRS + 8 * hh + 8)
                    pool.dma_start(MB[:, hh * S:hh * S + CA_KEYS],
                                   rel[2 * i + hh]).then_inc(mb_loaded["ca"][hh], 16)
                    pool.wait_ge(mb_loaded["ca"][hh], 16 * i + 16)
                    pool.wait_ge(ca_masked, 4 * i + 2 * hh + 1)
                    pool.sem_inc(masks_due, 1)
                    pool.memset(MB[0:64, hh * S + CA_KEYS - 64:hh * S + CA_KEYS],
                                NEG).then_inc(ca_masked, 1)
                    pool.wait_ge(ca_masked, 4 * i + 2 * hh + 2)
                    pool.sem_inc(masks_due, 1)
                    pool.memset(MB[64:128, hh * S:hh * S + 64], NEG).then_inc(ca_masked, 1)
            pool.wait_ge(hid_lo, FF_TILES)
            pool.dma_start(LGB[:, 0:D], ln_rows[0:1, :].partition_broadcast(P)).then_inc(rows_loaded, 16)
            pool.dma_start(LGB[:, D:2 * D], ln_rows[1:2, :].partition_broadcast(P)).then_inc(rows_loaded, 16)
            pool.wait_ge(rows_loaded, 32)
            for j in range(POOL_TILES):
                tau = NB - POOL_TILES + j
                x = XN3[:, tau * D:(tau + 1) * D]
                pool.wait_ge(final_scaled, j + 1)
                pool.tensor_tensor(x, x, LGB[:, D:2 * D], ALU.add).then_inc(final_pool, 1)

        @block.scalar
        def _(act):
            act.dma_start(WFF[:, :], w_ff).then_inc(wff_loaded, 16)
            small = ((SP[:, 0:16], lam_re), (SP[:, 16:32], lam_im), (SP[:, 32:48], log_dt),
                     (BRAW[:, 0:256], b_re), (BRAW[:, 256:512], b_im),
                     (CRAW[:, 0:256], c_re), (CRAW[:, 256:512], c_im),
                     (DC[:, 0:4], ssm_d), (BC[:, :], b_cols), (DC[0:8, 6:7], b_ff),
                     (CONV[:, :], conv), (LNC[:, :], ln_cols))
            assert len(small) == N_SMALL
            for dst, src in small:
                act.dma_start(dst, src).then_inc(params, 16)
            for k in range(KD):
                if k in (0, 4):
                    n = k // 4
                    act.wait_ge(raw[n], 16)
                    act.activation(WH[:, n * D:(n + 1) * D], WR[:, n * D:(n + 1) * D],
                                   ACT.Copy).then_inc(w_hi, 1)
                act.wait_ge(xraw[k // 2], 16)
                act.activation(XH[:, k * S:(k + 1) * S], XRAW[:, k * S:(k + 1) * S],
                               ACT.Copy).then_inc(x_hi, 1)
            act.wait_ge(params, 16 * N_SMALL)
            act.activation(spv(4), spv(2), ACT.Exp).then_inc(sa, 1)
            act.wait_ge(su, EXP_STEP)
            act.activation(spv(6), spv(5), ACT.Exp).then_inc(sa, 1)
            act.wait_ge(su, FFEXP_STEP)
            act.activation(FFE[0:8, :], FFE[0:8, :], ACT.Exp, scale=-1.0).then_inc(sa, 1)
            act.wait_ge(su, SIN_STEP)
            act.activation(spv(11), spv(9), ACT.Sin)
            act.activation(spv(12), spv(10), ACT.Sin).then_inc(sa, 1)
            act.wait_ge(sa, 3)
            act.activation(FFE[0:8, :], FFE[0:8, :], ACT.Ln, bias=DC[0:8, 5:6]).then_inc(sa, 1)

            for k, dst in enumerate((QT, KT, VT, YS)):
                act.wait_ge(w_used, k + 3)
                for t in range(2):
                    act.activation(dst[:, t * HALF:(t + 1) * HALF],
                                   pair(k)[:, t * HALF:(t + 1) * HALF], ACT.Identity,
                                   bias=BC[:, k:k + 1],
                                   scale=0.125 if k == 0 else 1.0).then_inc(fox["proj_ready"], 1)
                split_hi(act, k + 2, k % 2, (k + 2) // 2 + 1)
            with act.Fori(0, PAIRS - 1) as i:
                act_attention(act, "fox", i, OF, ("fox", i + 1, 1))
            act_attention(act, "fox", PAIRS - 1, OF, ("ca", 0, 1))
            with act.Fori(0, PAIRS - 1) as i:
                act_attention(act, "ca", i, OC, ("ca", i + 1, 2))
            act_attention(act, "ca", PAIRS - 1, OC, None)

            for t, n0, br, src in (("ef", N_EF, 0, OF), ("ec", N_EC, 1, OC), ("es", N_ES, 2, YS)):
                if t == "es":
                    for c in range(4):
                        act.activation(YS[:, c * S:(c + 1) * S], YS[:, c * S:(c + 1) * S],
                                       ACT.Gelu_apprx_tanh).then_inc(y_act, 1)
                    act.wait_ge(y_act, 4)
                act.wait_ge(w_used, n0 + 2)
                if t == "ef":
                    act.wait_ge(ca["o_copied"], 4 * PAIRS)
                for c in range(4):
                    act.activation(OH[:, c * S:(c + 1) * S], src[:, c * S:(c + 1) * S],
                                   ACT.Copy).then_inc(o_hi[t], 1)
                gate = GS if t == "es" else GF
                if t == "ec":
                    act.wait_ge(m_step["ef"], KD + 1)
                with act.Fori(0, KD) as i:
                    n = n0 + 2 * i
                    act.wait_ge(w_used, n + 3)
                    if t == "ef":
                        act.wait_ge(o_lo[t], 4)
                        act.wait_ge(m_step["ef"], i + 1)
                    elif t == "ec":
                        act.wait_ge(m_step["ec"], 2 * i + 1)
                    else:
                        act.wait_ge(o_lo[t], 4)
                        act.wait_ge(m_step["es"], 3 * i + 1)
                    act.activation(gate[:, :], PA[:, :], ACT.Sigmoid,
                                   bias=BC[:, bass.ds(28 + KD * br + i, 1)]).then_inc(g_ready[t], 1)
                    split_hi(act, n + 2, 0, i + (rc(n0, 2)))
                    if t == "es":
                        act.wait_ge(w_used, n + 4)
                        act.activation(G2[:, :], TB[:, :], ACT.Sigmoid).then_inc(g_ready[t], 1)
                        split_hi(act, n + 3, 1, i + rc(n0, 3))
                        act.wait_ge(m_step["es"], 3 * i + 4)
                        act.activation(MH[:, bass.ds(i * S, S)], MT[:, bass.ds(i * S, S)],
                                       ACT.Copy).then_inc(m_hi, 1)
                    else:
                        split_hi(act, n + 3, 1, i + rc(n0, 3))

            act.wait_ge(mem_loaded, 16)

            def ring_only(n0, count):
                with act.Fori(0, count) as i:
                    for k in range(2):
                        split_hi(act, n0 + 2 * i + k + 2, k, i + rc(n0, k + 2))

            act.activation(MMH[:, :], MRAW[:, :], ACT.Copy).then_inc(mem_hi, 1)
            ring_only(N_WO, KD // 2)

            def kv_slot(j):
                n = N_KV + j
                bank = (OB, XB)[j % 2][:, 0:MEM]
                act.wait_ge(w_used, n + 3)
                if j < KD:
                    dst = KM[:, j * MEM:(j + 1) * MEM]
                else:
                    dst = VMT[:, j % 2 * MEM:(j % 2 + 1) * MEM]
                    if j >= KD + 2:
                        act.wait_ge(v_turned, j - KD - 1)
                act.activation(dst, bank, ACT.Copy).then_inc(kv_ready, 1)
                split_hi(act, n + 2, j % 2, rc(N_KV, j + 2))

            def copy_mem_v(j):
                act.wait_ge(v_turned, j + 1)
                act.activation(VM[:, :].rearrange("p (c f) -> p c f", c=2)[:, :, j * P:(j + 1) * P],
                               TB[:, j % 2 * HALF:j % 2 * HALF + MEM].rearrange("p (c f) -> p c f", c=2),
                               ACT.Copy).then_inc(v_ready, 1)

            for what, j in KV_LN1:
                if what == "kv":
                    kv_slot(j)
                else:
                    act_ln_copy(act, lns[0], XN1, j)
                    if j == NB - 1:
                        act_ln_sqrt(act, lns[0])
            for k in range(KD):
                kv_slot(KD + k)
                act_ln_scale(act, 0, k)
                copy_mem_v(k)

            for k in range(2):
                n = N_XQ + k
                act.wait_ge(w_used, n + 3)
                for t in range(2):
                    act.activation(QX[:, k * S + t * HALF:k * S + (t + 1) * HALF],
                                   pair(k)[:, t * HALF:(t + 1) * HALF], ACT.Copy,
                                   scale=0.0625).then_inc(xa["q_ready"], 1)
                split_hi(act, n + 2, k, rc(N_XQ, k + 2))

            def x_exp(i, u):
                act.wait_ge(xa["nmax"], 8 * i + u + 1)
                act.activation(SX[:, u % 2 * MEM:(u % 2 + 1) * MEM],
                               TB[:, u % 2 * HALF:u % 2 * HALF + MEM], ACT.Exp,
                               bias=MX[:, 2 + u % 2:3 + u % 2],
                               accum_out=MX[:, 4 + u % 2:5 + u % 2]).then_inc(xa["exp"], 1)

            def x_copy(i, u):
                act.wait_ge(xa["t_ready"], 8 * i + u + 1)
                g, q = divmod(u, 4)
                act.activation(
                    PTX[:, g * 2 * HALF:(g + 1) * 2 * HALF].rearrange("p (c t) -> p c t", c=2)[
                        :, :, q * P:(q + 1) * P],
                    (XB, OB)[u % 2][:, 0:MEM].rearrange("p (c t) -> p c t", c=2),
                    ACT.Copy).then_inc(xa["t_copied"], 1)

            def x_hi_part(i, g):
                act.wait_ge(xa["pv"], 2 * i + g + 1)
                for c in range(2):
                    act.activation(OHX[:, bass.ds(i * 2 * S + c * S + g * HALF, HALF)],
                                   PA[:, c * HALF:(c + 1) * HALF],
                                   ACT.Copy).then_inc(xa["hi"], 1)

            def act_cross(i, fill):
                act.activation(VX[:, :].rearrange("p (c f) -> p c f", c=2),
                               VM[:, :].rearrange("p (c f) -> p c f", c=2)[:, :, bass.ds(i * MEM, MEM)],
                               ACT.Copy).then_inc(xa["v_staged"], 1)
                for u in range(8):
                    x_copy(i, u)
                    if u < 7:
                        x_exp(i, u + 1)
                    elif fill:
                        x_exp(i + 1, 0)
                    if u == 5:
                        x_hi_part(i, 0)
                    if fill and u % 2:
                        k, t = divmod(u // 2, 2)
                        n = N_XQ + 2 * i + 2 + k
                        if t == 0:
                            act.wait_ge(half_done, (FOX_SLOTS + CA_SLOTS) * (PAIRS - 1) + CA_SLOTS
                                        + 2 * i + k + 1)
                        else:
                            act.wait_ge(w_used, n + 3)
                        if u == 1:
                            act.wait_ge(xq_staged, i + 1)
                        q = QX if u == 7 else Q2X
                        act.activation(q[:, k * S + t * HALF:k * S + (t + 1) * HALF],
                                       PB[:, t * HALF:(t + 1) * HALF], ACT.Copy,
                                       scale=0.0625).then_inc(xa["q_ready"], 1)
                        if t:
                            split_hi(act, n + 2, k, i + rc(N_XQ, k + 4))
                x_hi_part(i, 1)

            x_exp(0, 0)
            with act.Fori(0, XH_HEADS - 1) as i:
                act_cross(i, True)
            act_cross(XH_HEADS - 1, False)

            ring_only(N_XO, KD // 2)
            for tau in range(NB):
                act_ln_copy(act, lns[1], XN2, tau)
            act_ln_sqrt(act, lns[1])
            for k in range(KD):
                act_ln_scale(act, 1, k)

            act.preload_act_table(ACT.Gelu_apprx_tanh)
            n0, t0 = N_FF, 0
            for g, tiles in enumerate(FF_GROUPS):
                with act.Fori(0, tiles) as i:
                    n = n0 + 2 * i
                    split_hi(act, n + 2, 0, i + rc(n0, 2))
                    act.wait_ge(cv_step, 3 * (t0 + i) + 3)
                    act.activation(GL[:, :], CV[:, :], ACT.Gelu_apprx_tanh).then_inc(gelu_done, 1)
                    split_hi(act, n + 3, 1, i + rc(n0, 3))
                    act.wait_ge(hid, t0 + i + 1)
                    act.activation(HDH[:, bass.ds(i * S, S)], HF[:, :], ACT.Copy).then_inc(hid_hi, 1)
                n0, t0 = n0 + 2 * tiles, t0 + tiles
                last = g == len(FF_GROUPS) - 1
                ring_only(n0, KD // 2 - (1 if last else 0))
                n0 += KD
            for tau in range(NB):
                act_ln_copy(act, lns[2], XN3, tau)
            act_ln_sqrt(act, lns[2])
            for tau in range(NB - POOL_TILES, NB):
                x = XN3[:, tau * D:(tau + 1) * D]
                act.wait_ge(lns[2]["step"], 30)
                act.wait_ge(lns[2]["normed"], tau + 1)
                act.activation(x, x, ACT.Copy, scale=rstd[:, tau:tau + 1]).then_inc(final_scaled, 1)

        @block.tensor
        def _(pe):
            pe.wait_ge(wff_loaded, 16)
            for k in range(KD):
                pe.wait_ge(xraw[k // 2], 16)
                for t in range(2):
                    mm = pe.matmul((OB, XB)[t][0:8, :], WFF[:, 8 * k:8 * k + 8],
                                   XRAW[:, k * S + t * HALF:k * S + (t + 1) * HALF],
                                   start=(k == 0), stop=(k == KD - 1))
            mm.then_inc(st_pe, 1)
            pe.nop().then_inc(w_used, 2)
            for k in range(FOX_SLOTS):
                if k >= 2:
                    pe.wait_ge(fox["proj_ready"], 2 * (k - 1))
                product(pe, k, k % 2, pair(k), XH, XL,
                        before=None if k else lambda j: pe.wait_ge(x_lo, j + 1)).then_inc(w_used, 1)
            pe.wait_ge(consts, 1)
            pe.wait_ge(su, BP_STEP)
            for t in range(4):
                for c in range(2):
                    mm = pe.transpose(TB[:, (2 * t + c) * P:(2 * t + c + 1) * P],
                              BP[:, c * 512 + t * P:c * 512 + (t + 1) * P], IDN[:, :])
            mm.then_inc(st_pe, 1)
            pe.wait_ge(fox["proj_ready"], 6)
            pe_scores(pe, "fox", fox, 0)
            pe.wait_ge(su, BT_STEP)
            with pe.Fori(0, PAIRS - 1) as i:
                pe_attention(pe, "fox", i, ("fox", i + 1, 1))
            pe_attention(pe, "fox", PAIRS - 1, ("ca", 0, 1))
            with pe.Fori(0, PAIRS - 1) as i:
                pe_attention(pe, "ca", i, ("ca", i + 1, 2))
            pe_attention(pe, "ca", PAIRS - 1, None)

            for t, n0 in (("ef", N_EF), ("ec", N_EC), ("es", N_ES)):
                with pe.Fori(0, KD) as i:
                    n = n0 + 2 * i
                    product(pe, n, 0, PA, XH, XL).then_inc(w_used, 1)
                    pe.wait_ge(o_lo[t], 4)
                    if t == "es":
                        product(pe, n + 1, 1, PB, OH, OL, nk=4)
                        product(pe, n + 1, 1, TB, OH, OL, nk=4, k0=4).then_inc(w_used, 1)
                    else:
                        product(pe, n + 1, 1, PB, OH, OL, nk=4).then_inc(w_used, 1)

            def dense(n0, xh, xl, nk=KD, before=None):
                if before:
                    for k in range(2):
                        product(pe, n0 + k, k, pair(k), xh, xl, nk=nk,
                                before=None if k else before).then_inc(w_used, 1)
                with pe.Fori(1 if before else 0, KD // 2) as i:
                    for k in range(2):
                        product(pe, n0 + 2 * i + k, k, pair(k), xh, xl, nk=nk).then_inc(w_used, 1)

            dense(N_WO, MH, ML, before=lambda k: pe.wait_ge(m_lo, k + 1))
            pe.wait_ge(mem_lo, 1)

            def kv_slot(j):
                if j >= 2:
                    pe.wait_ge(kv_ready, j - 1)
                product(pe, N_KV + j, j % 2, (OB, XB)[j % 2], MMH, MML, width=MEM).then_inc(w_used, 1)

            for what, j in KV_LN1:
                if what == "kv":
                    kv_slot(j)
                else:
                    pe_ln_forward(pe, lns[0], RT1, j, (rt_step["wo"], 2 * KD))
            for k in range(KD):
                kv_slot(KD + k)
                pe_ln_back(pe, 0, XN1, k)
                pe.wait_ge(kv_ready, KD + k + 1)
                if k >= 2:
                    pe.wait_ge(v_ready, k - 1)
                for c in range(2):
                    mm = pe.transpose(TB[:, k % 2 * HALF + c * P:k % 2 * HALF + (c + 1) * P],
                                      VMT[:, k % 2 * MEM + c * P:k % 2 * MEM + (c + 1) * P], IDN[:, :])
                mm.then_inc(v_turned, 1)
            pe.wait_ge(lns[0]["scaled"], 2 * KD - 2)

            for k in range(2):
                product(pe, N_XQ + k, k, pair(k), XH, XL,
                        before=None if k else lambda j: pe.wait_ge(lns[0]["lo"], j + 1)
                        ).then_inc(w_used, 1)
            pe.wait_ge(v_ready, KD)
            pe.wait_ge(xa["q_ready"], 4)

            def x_scores(i, u):
                for c in range(2):
                    mm = pe.matmul(TB[:, u % 2 * HALF:u % 2 * HALF + MEM],
                                   QX[:, c * S + u * P:c * S + (u + 1) * P],
                                   KM[:, bass.ds(i * 2 * MEM + c * MEM, MEM)],
                                   start=(c == 0), stop=(c == 1))
                mm.then_inc(xa["s_ready"], 1)

            def x_piece(p, g):
                h, at_ = divmod(g, 6)
                k, t = divmod(h, 2)
                n = N_XQ + 2 * p + k
                if at_ == 0:
                    if t == 0:
                        pe.wait_ge(w_lo, n + 3)
                    pe.wait_ge(xa["q_ready"], 4 * p + h - 1)
                for j in range(4 * at_, 4 * at_ + 4):
                    k0, pas = divmod(j, 3)
                    w, x = ((WH, XH), (WH, XL), (WL, XH))[pas]
                    mm = pe.matmul(PB[:, t * HALF:(t + 1) * HALF], w[:, k * D + k0 * P:k * D + k0 * P + P],
                                   x[:, k0 * S + t * HALF:k0 * S + (t + 1) * HALF],
                                   start=(j == 0), stop=(j == 3 * KD - 1))
                if at_ == 5:
                    mm.then_inc(w_used if t else half_done, 1)

            def pe_cross(i, fill):
                for u in range(8):
                    if fill:
                        x_piece(i + 1, 3 * u)
                    pe.wait_ge(xa["p_ready"], 8 * i + u + 1)
                    if u >= 2:
                        pe.wait_ge(xa["t_copied"], 8 * i + u - 1)
                    for c in range(2):
                        mm = pe.transpose((XB, OB)[u % 2][:, c * P:(c + 1) * P],
                                          SX[:, u % 2 * MEM + c * P:u % 2 * MEM + (c + 1) * P], IDN[:, :])
                    mm.then_inc(xa["t_ready"], 1)
                    if u == 2:
                        pe.wait_ge(xa["q_ready"], 4 * i + 4)
                    if fill and u < 7:
                        x_piece(i + 1, 3 * u + 1)
                    if u < 6:
                        x_scores(i, u + 2)
                    elif fill:
                        if u == 6:
                            pe.wait_ge(xq_staged, i + 2)
                        x_scores(i + 1, u - 6)
                    if fill and u == 7:
                        x_piece(i + 1, 3 * u + 1)
                    if u in (4, 7):
                        g = u // 5
                        pe.wait_ge(xa["v_staged"], i + 1)
                        pe.wait_ge(xa["lo"], 4 * i + 2 * g + 1)
                        pe.wait_ge(xa["t_copied"], 8 * i + 4 * g + 4)
                        for c2 in range(2):
                            for c in range(2):
                                mm = pe.matmul(PA[:, c2 * HALF:(c2 + 1) * HALF],
                                               VX[:, c * MEM + c2 * P:c * MEM + (c2 + 1) * P],
                                               PTX[:, (2 * g + c) * HALF:(2 * g + c + 1) * HALF],
                                               start=(c == 0), stop=(c == 1))
                        mm.then_inc(xa["pv"], 1)
                    if fill:
                        x_piece(i + 1, 3 * u + 2)

            x_scores(0, 0)
            x_scores(0, 1)
            with pe.Fori(0, XH_HEADS - 1) as i:
                pe_cross(i, True)
            pe_cross(XH_HEADS - 1, False)
            pe.wait_ge(xa["lo"], 4 * XH_HEADS + 1)
            dense(N_XO, OHX, OLX)
            for tau in range(NB):
                pe_ln_forward(pe, lns[1], RT2, tau, (rt_step["xo"], 2 * KD))
            for k in range(3):
                pe_ln_back(pe, 1, XN2, k)

            def with_ln_back(k):
                if k and k + 2 < KD:
                    pe_ln_back(pe, 1, XN2, k + 2)
                pe.wait_ge(lns[1]["lo"], k + 1)

            n0, t0 = N_FF, 0
            for g, tiles in enumerate(FF_GROUPS):
                if g == 0:
                    product(pe, n0, 0, PA, XH, XL, before=with_ln_back).then_inc(w_used, 1)
                    product(pe, n0 + 1, 1, PB, XH, XL).then_inc(w_used, 1)
                with pe.Fori(1 if g == 0 else 0, tiles) as i:
                    for k in range(2):
                        product(pe, n0 + 2 * i + k, k, pair(k), XH, XL).then_inc(w_used, 1)
                n0, t0 = n0 + 2 * tiles, t0 + tiles
                dense(n0, HDH, HDL, nk=tiles,
                      before=lambda k: pe.wait_ge(hid_lo, t0 - tiles + k + 1))
                n0 += KD
            for tau in range(NB):
                pe_ln_forward(pe, lns[2], YT, tau, (y_sum, (len(FF_GROUPS) + 1) * KD))

        @block.vector
        def _(dve):
            chain = [0]

            def link(ins):
                chain[0] += 1
                ins.then_inc(su, 1)
                dve.wait_ge(su, chain[0])

            def step(ins):
                chain[0] += 1
                ins.then_inc(su, 1)

            v = spv
            E = lambda c, m: PRM[:, :].rearrange("p (t n) -> p t n", n=NPRM)[:, :, 8 * c + m]
            TT, TS, STT = dve.tensor_tensor, dve.tensor_scalar, dve.scalar_tensor_tensor

            dve.memset(DC[:, 5:6], 1.0).then_inc(su, 1)
            chain[0] += 1
            dve.engine_nop().then_inc(w_lo, 2)
            for k in range(KD):
                if k in (0, 4):
                    split_lo(dve, k // 4, k // 4)
                dve.wait_ge(x_hi, k + 1)
                dve.tensor_tensor(XL[:, k * S:(k + 1) * S], XRAW[:, k * S:(k + 1) * S],
                                  XH[:, k * S:(k + 1) * S].bitcast(F32), ALU.subtract).then_inc(x_lo, 1)
            dve.wait_ge(params, 16 * N_SMALL)
            link(TS(BC[:, 0:16:4], BC[:, 0:16:4], 0.125, None, ALU.mult))
            link(TS(BC[:, 16:28:3], BC[:, 16:28:3], 0.125, None, ALU.mult))
            dve.wait_ge(st_pe, 1)
            for t, bank in enumerate((OB, XB)):
                link(TS(FFB[0:8, t * HALF:(t + 1) * HALF], bank[0:8, :], DC[0:8, 6:7], None, ALU.add))
            link(STT(FFE[0:8, :], FFB[0:8, :], -1.0, FFB[0:8, :], ALU.mult, ALU.max))
            assert chain[0] == FFEXP_STEP, chain[0]
            link(TS(v(3), v(0), -1e-4, None, ALU.min))
            dve.wait_ge(sa, 1)
            link(TT(v(5), v(3), v(4), ALU.mult))
            assert chain[0] == EXP_STEP, chain[0]
            link(TT(v(7), v(1), v(4), ALU.mult))
            link(TS(v(8), v(7), 1.0 / TWO_PI, RND, ALU.mult, ALU.add))
            link(TS(v(8), v(8), -RND, None, ALU.add))
            link(STT(v(9), v(8), -PI_A, v(7), ALU.mult, ALU.add))
            link(STT(v(9), v(8), -PI_B, v(9), ALU.mult, ALU.add))
            link(STT(v(9), v(8), -PI_C, v(9), ALU.mult, ALU.add))
            link(TS(v(9), v(9), 0.5, -1.5707963, ALU.mult, ALU.max))
            link(TS(v(9), v(9), 1.5707963, None, ALU.min))
            link(STT(v(10), v(9), -1.0, v(9), ALU.mult, ALU.max))
            link(TS(v(10), v(10), -1.0, 1.5707963267948966, ALU.mult, ALU.add))
            link(TS(v(10), v(10), 0.0, None, ALU.max))
            assert chain[0] == SIN_STEP, chain[0]
            dve.wait_ge(sa, 4)
            link(TT(v(13), v(11), v(11), ALU.mult))
            link(TS(E(0, 0), v(13), -2.0, 1.0, ALU.mult, ALU.add))
            link(STT(E(1, 0), v(11), 2.0, v(12), ALU.mult, ALU.mult))

            def unit(c, s):
                step(TT(v(16), c, c, ALU.mult))
                link(TT(v(17), s, s, ALU.mult))
                link(TT(v(16), v(16), v(17), ALU.add))
                link(TS(v(16), v(16), -0.5, 1.5, ALU.mult, ALU.add))
                step(TT(c, c, v(16), ALU.mult))
                link(TT(s, s, v(16), ALU.mult))

            unit(E(0, 0), E(1, 0))
            link(TT(v(14), v(6), E(0, 0), ALU.mult))
            link(TS(v(14), v(14), -1.0, None, ALU.add))
            link(TT(v(15), v(6), E(1, 0), ALU.mult))
            step(TT(v(16), v(3), v(3), ALU.mult))
            link(TT(v(17), v(1), v(1), ALU.mult))
            link(TT(v(16), v(16), v(17), ALU.add))
            link(dve.reciprocal(v(18), v(16)))
            step(TT(v(16), v(14), v(3), ALU.mult))
            link(TT(v(17), v(15), v(1), ALU.mult))
            link(TT(v(16), v(16), v(17), ALU.add))
            link(TT(v(19), v(16), v(18), ALU.mult))
            step(TT(v(16), v(15), v(3), ALU.mult))
            link(TT(v(17), v(14), v(1), ALU.mult))
            link(TT(v(16), v(16), v(17), ALU.subtract))
            link(TT(v(20), v(16), v(18), ALU.mult))
            gb = lambda a: v(a).unsqueeze(2).to_broadcast([P, 16, 16])
            t3 = lambda a: a.rearrange("p (t c) -> p t c", t=16)
            br, bi = t3(BRAW[:, 0:256]), t3(BRAW[:, 256:512])
            dve.wait_ge(sp, 1)
            for c, (x1, x2, op) in enumerate(((br, bi, ALU.subtract), (bi, br, ALU.add))):
                step(TT(t3(BTMP[:, 0:256]), x2, gb(20), ALU.mult))
                link(TT(t3(BBAR[:, c * 256:(c + 1) * 256]), x1, gb(19), ALU.mult))
                for g in range(2):
                    r = slice(64 * g, 64 * g + 64)
                    step(TT(BP[r, c * 512:(c + 1) * 512].rearrange("p (t c) -> p t c", t=16)[
                                :, :, 16 * g:16 * g + 16],
                            t3(BBAR[r, c * 256:(c + 1) * 256]), t3(BTMP[r, 0:256]), op))
                    link(TS(CT[r, :].rearrange("p (t q c) -> p t q c", t=16, q=2)[
                                :, :, c, 16 * g:16 * g + 16],
                            t3(CRAW[r, c * 256:(c + 1) * 256]), 1.0 - 2.0 * c, None, ALU.mult))
            assert chain[0] == BP_STEP, chain[0]
            link(dve.tensor_copy(PRM[:, :].rearrange("p (t n) -> p t n", n=NPRM)[:, :, 24], v(6)))
            for m in range(1, 8):
                c, s = E(0, m - 1), E(1, m - 1)
                step(TT(v(16), c, c, ALU.mult))
                link(TT(v(17), s, s, ALU.mult))
                step(TT(E(0, m), v(16), v(17), ALU.subtract))
                link(STT(E(1, m), c, 2.0, s, ALU.mult, ALU.mult))
                unit(E(0, m), E(1, m))
                if m == 1:
                    link(TS(FFB[0:8, :], FFB[0:8, :], 0.0, None, ALU.min))
                    dve.wait_ge(sa, 5)
                    link(TT(FFB[0:8, :], FFB[0:8, :], FFE[0:8, :], ALU.subtract))
                    link(dve.tensor_tensor_scan(FFE[0:8, :], DC[0:8, 5:6].to_broadcast([8, S]),
                                                FFB[0:8, :], 0.0, ALU.mult, ALU.subtract))
                    assert chain[0] == CUM_STEP, chain[0]
            pr = PRM[:, :].rearrange("p (t n) -> p t n", n=NPRM)
            link(TS(pr[:, :, 16:24], pr[:, :, 8:16], -1.0, None, ALU.mult))
            w16 = W16[:, :].rearrange("p (t c n) -> p t c n", t=16, c=2)
            step(dve.tensor_copy(w16[:, :, 0, 0:1], pr[:, :, 0:1]))
            link(dve.tensor_copy(w16[:, :, 1, 0:1], pr[:, :, 8:9]))
            for m in range(4):
                n = 2 ** m
                wt = lambda c: W16T[:, c * 256:c * 256 + 16 * n].rearrange("p (t n) -> p t n", n=n)
                eb = lambda c: pr[:, :, 8 * c + m:8 * c + m + 1].to_broadcast([P, 16, n])
                wr, wi = w16[:, :, 0, 0:n], w16[:, :, 1, 0:n]
                step(TT(wt(0), wr, eb(0), ALU.mult))
                link(TT(wt(1), wi, eb(1), ALU.mult))
                link(TT(w16[:, :, 0, n:2 * n], wt(0), wt(1), ALU.subtract))
                step(TT(wt(0), wr, eb(1), ALU.mult))
                link(TT(wt(1), wi, eb(0), ALU.mult))
                link(TT(w16[:, :, 1, n:2 * n], wt(0), wt(1), ALU.add))
            dve.wait_ge(st_pe, 2)
            link(dve.tensor_copy(BT[:, :], TB[:, :]))
            assert chain[0] == BT_STEP, chain[0]
            dve.engine_nop().then_inc(y_done, 1)
            dve.engine_nop().then_inc(m_step["ef"], 1)
            dve.engine_nop().then_inc(m_step["ec"], 1)
            dve.engine_nop().then_inc(m_step["es"], 1)

            dve.engine_nop().then_inc(k_staged, 1)
            dve.wait_ge(w_lo, 6)
            for k in range(2, FOX_SLOTS):
                split_lo(dve, k + 2, k % 2)
            dve.wait_ge(cum_out, 16)
            for part in range(3):
                dve_table(dve, 0, 0, part, PRM[:, 0:NPRM])
            with dve.Fori(0, PAIRS - 1) as i:
                dve_attention(dve, "fox", i, ("fox", i + 1, 1))
            dve_attention(dve, "fox", PAIRS - 1, ("ca", 0, 1))
            with dve.Fori(0, PAIRS - 1) as i:
                dve_attention(dve, "ca", i, ("ca", i + 1, 2))
            dve_attention(dve, "ca", PAIRS - 1, None)

            for t, n0, src in (("ef", N_EF, OF), ("ec", N_EC, OC), ("es", N_ES, YS)):
                for c in range(4):
                    dve.wait_ge(o_hi[t], c + 1)
                    dve.tensor_tensor(OL[:, c * S:(c + 1) * S], src[:, c * S:(c + 1) * S],
                                      OH[:, c * S:(c + 1) * S].bitcast(F32),
                                      ALU.subtract).then_inc(o_lo[t], 1)
                with dve.Fori(0, KD) as i:
                    n = n0 + 2 * i
                    split_lo(dve, n + 2, 0)
                    mt = MT[:, bass.ds(i * S, S)]
                    dve.wait_ge(w_used, n + 4)
                    if t == "ef":
                        dve.wait_ge(g_ready[t], i + 1)
                        dve.tensor_tensor(mt, PB[:, :], GF[:, :], ALU.mult).then_inc(m_step[t], 1)
                    elif t == "ec":
                        dve.wait_ge(g_ready[t], i + 1)
                        dve.tensor_tensor(GF[:, :], PB[:, :], GF[:, :], ALU.mult).then_inc(m_step[t], 1)
                        dve.wait_ge(m_step[t], 2 * i + 2)
                        dve.tensor_tensor(mt, mt, GF[:, :], ALU.add).then_inc(m_step[t], 1)
                    else:
                        dve.wait_ge(g_ready[t], 2 * i + 2)
                        dve.tensor_tensor(GS[:, :], PB[:, :], GS[:, :], ALU.mult).then_inc(m_step[t], 1)
                        dve.wait_ge(m_step[t], 3 * i + 2)
                        dve.tensor_tensor(GS[:, :], GS[:, :], G2[:, :], ALU.mult).then_inc(m_step[t], 1)
                        dve.wait_ge(m_step[t], 3 * i + 3)
                        dve.tensor_tensor(mt, mt, GS[:, :], ALU.add).then_inc(m_step[t], 1)
                    split_lo(dve, n + 3, 1)
                    if t == "es":
                        dve.wait_ge(m_hi, i + 1)
                        dve.tensor_tensor(ML[:, bass.ds(i * S, S)], mt,
                                          MH[:, bass.ds(i * S, S)].bitcast(F32),
                                          ALU.subtract).then_inc(m_lo, 1)

            def residual(tag):
                rt, n0 = RES[tag]
                with dve.Fori(0, KD // 2) as i:
                    for k in range(2):
                        n = n0 + 2 * i + k
                        sl = bass.ds(i * 2 * S + k * S, S)
                        dve.wait_ge(w_used, n + 3)
                        dve.scalar_tensor_tensor(rt[:, sl], XH[:, sl].bitcast(F32), ALPHA, pair(k)[:, :],
                                                 ALU.mult, ALU.add).then_inc(rt_step[tag], 1)
                        dve.wait_ge(rt_step[tag], 4 * i + 2 * k + 1)
                        dve.scalar_tensor_tensor(rt[:, sl], XL[:, sl].bitcast(F32), ALPHA, rt[:, sl],
                                                 ALU.mult, ALU.add).then_inc(rt_step[tag], 1)
                        split_lo(dve, n + 2, k)

            dve.wait_ge(mem_hi, 1)
            dve.tensor_tensor(MML[:, :], MRAW[:, :], MMH[:, :].bitcast(F32),
                              ALU.subtract).then_inc(mem_lo, 1)
            residual("wo")
            for what, j in KV_LN1:
                if what == "ln":
                    dve_ln_stats(dve, lns[0], XN1, j)
                elif j < KD - 2:
                    split_lo(dve, N_KV + j + 2, j % 2)
            dve_ln_normalise(dve, lns[0], XN1, lambda: split_lo(dve, N_KV + KD, 0))
            split_lo(dve, N_KV + KD + 1, 1)
            for k in range(KD):
                split_lo(dve, N_KV + KD + k + 2, k % 2)
                dve_ln_split(dve, 0, k)

            dve.engine_nop().then_inc(xq_staged, 1)
            dve.engine_nop().then_inc(xa["lo"], 1)
            for k in range(2):
                split_lo(dve, N_XQ + k + 2, k)

            def x_max(i, u):
                b = u % 2
                dve.wait_ge(xa["s_ready"], 8 * i + u + 1)
                dve.reduce_max(MX[:, b:b + 1], TB[:, b * HALF:b * HALF + MEM],
                               mybir.AxisListType.X).then_inc(xa["max"], 1)
                dve.wait_ge(xa["max"], 8 * i + u + 1)
                dve.tensor_scalar(MX[:, 2 + b:3 + b], MX[:, b:b + 1], -1.0, None,
                                  ALU.mult).then_inc(xa["nmax"], 1)

            def x_norm(i, u):
                b = u % 2
                dve.wait_ge(xa["exp"], 8 * i + u + 1)
                dve.reciprocal(MX[:, 6 + b:7 + b], MX[:, 4 + b:5 + b]).then_inc(xa["rsum"], 1)
                dve.wait_ge(xa["rsum"], 8 * i + u + 1)
                x = SX[:, b * MEM:(b + 1) * MEM]
                dve.tensor_scalar(x, x, MX[:, 6 + b:7 + b], None, ALU.mult).then_inc(xa["p_ready"], 1)

            def x_lo_part(i, g):
                for c in range(2):
                    sl = bass.ds(i * 2 * S + c * S + g * HALF, HALF)
                    dve.wait_ge(xa["hi"], 4 * i + 2 * g + c + 1)
                    dve.tensor_tensor(OLX[:, sl], PA[:, c * HALF:(c + 1) * HALF],
                                      OHX[:, sl].bitcast(F32), ALU.subtract).then_inc(xa["lo"], 1)

            def dve_cross(i, fill):
                for u in range(8):
                    if u:
                        x_norm(i, u)
                    if u < 7:
                        x_max(i, u + 1)
                    elif fill:
                        x_max(i + 1, 0)
                        x_norm(i + 1, 0)
                    if fill and u == 6:
                        dve.wait_ge(xa["q_ready"], 4 * i + 7)
                        dve.tensor_copy(QX[:, 0:3 * HALF],
                                        Q2X[:, :]).then_inc(xq_staged, 1)
                    if u == 6:
                        x_lo_part(i, 0)
                    if fill and u == 4:
                        split_lo(dve, N_XQ + 2 * i + 4, 0)
                x_lo_part(i, 1)
                if fill:
                    split_lo(dve, N_XQ + 2 * i + 5, 1)

            x_max(0, 0)
            x_norm(0, 0)
            with dve.Fori(0, XH_HEADS - 1) as i:
                dve_cross(i, True)
            dve_cross(XH_HEADS - 1, False)

            residual("xo")
            for tau in range(NB):
                dve_ln_stats(dve, lns[1], XN2, tau)
            dve_ln_normalise(dve, lns[1], XN2)
            for k in range(KD):
                dve_ln_split(dve, 1, k)

            dve.wait_ge(lns[1]["lo"], KD)
            n0, t0 = N_FF, 0
            for g, tiles in enumerate(FF_GROUPS):
                with dve.Fori(0, tiles) as i:
                    n = n0 + 2 * i
                    col = lambda m: CONV[:, bass.ds(4 * t0 + 4 * i + m, 1)]
                    dve.wait_ge(w_used, n + 3)
                    dve.tensor_scalar(CV[:, :], PA[:, :], col(2), col(3), ALU.mult,
                                      ALU.add).then_inc(cv_step, 1)
                    dve.wait_ge(cv_step, 3 * (t0 + i) + 1)
                    dve.scalar_tensor_tensor(CV[:, 1:S], PA[:, 0:S - 1], col(1), CV[:, 1:S], ALU.mult,
                                             ALU.add).then_inc(cv_step, 1)
                    dve.wait_ge(cv_step, 3 * (t0 + i) + 2)
                    dve.scalar_tensor_tensor(CV[:, 2:S], PA[:, 0:S - 2], col(0), CV[:, 2:S], ALU.mult,
                                             ALU.add).then_inc(cv_step, 1)
                    split_lo(dve, n + 2, 0)
                    dve.wait_ge(w_used, n + 4)
                    dve.wait_ge(gelu_done, t0 + i + 1)
                    dve.tensor_tensor(HF[:, :], PB[:, :], GL[:, :], ALU.mult).then_inc(hid, 1)
                    split_lo(dve, n + 3, 1)
                    dve.wait_ge(hid_hi, t0 + i + 1)
                    dve.tensor_tensor(HDL[:, bass.ds(i * S, S)], HF[:, :],
                                      HDH[:, bass.ds(i * S, S)].bitcast(F32),
                                      ALU.subtract).then_inc(hid_lo, 1)
                n0, t0 = n0 + 2 * tiles, t0 + tiles
                last = g == len(FF_GROUPS) - 1
                if g:
                    dve.wait_ge(y_sum, (g + 1) * KD)

                def down(i, split):
                    for k in range(2):
                        n = n0 + 2 * i + k
                        yt = YT[:, bass.ds(i * 2 * S + k * S, S)]
                        dve.wait_ge(w_used, n + 3)
                        if g == 0:
                            sl = bass.ds(i * 2 * S + k * S, S)
                            dve.scalar_tensor_tensor(yt, XH[:, sl].bitcast(F32), ALPHA, pair(k)[:, :],
                                                     ALU.mult, ALU.add).then_inc(y_sum, 1)
                        else:
                            dve.tensor_tensor(yt, pair(k)[:, :], yt, ALU.add).then_inc(y_sum, 1)
                        if split:
                            split_lo(dve, n + 2, k)
                        if g == 0:
                            dve.wait_ge(y_sum, 4 * i + 2 * k + 1)
                            dve.scalar_tensor_tensor(yt, XL[:, sl].bitcast(F32), ALPHA, yt,
                                                     ALU.mult, ALU.add).then_inc(y_sum, 1)

                with dve.Fori(0, KD // 2 - (1 if last else 0)) as i:
                    down(i, True)
                if last:
                    down(KD // 2 - 1, False)
                n0 += KD
            dve.wait_ge(rows_loaded, 32)
            for tau in range(NB):
                x = XN3[:, tau * D:(tau + 1) * D]
                dve_ln_stats(dve, lns[2], XN3, tau)
                dve.wait_ge(lns[2]["step"], 3 * tau + 3)
                dve.scalar_tensor_tensor(x, x, mean(tau), LGB[:, 0:D], ALU.subtract,
                                         ALU.mult).then_inc(lns[2]["normed"], 1)
            rstd_chain(dve, lns[2])
            for tau in range(NB - POOL_TILES):
                x = XN3[:, tau * D:(tau + 1) * D]
                dve.wait_ge(lns[2]["normed"], tau + 1)
                dve.scalar_tensor_tensor(x, x, rstd[:, tau:tau + 1], LGB[:, D:2 * D], ALU.mult,
                                         ALU.add).then_inc(final_step, 1)



def kernel(**inputs):
    import numpy as np
    import concourse.bacc as bacc
    from concourse.bass_utils import run_bass_kernel_spmd

    g = {k: np.asarray(v) for k, v in inputs.items()}
    chunks = lambda a: a.reshape(-1, P, a.shape[-1])

    def tiles(w):
        k, m = w.shape
        return w.reshape(k // P, P, m // P, P).transpose(2, 1, 0, 3).reshape(m // P, P, k)

    w_in, b_in = g["w_in"][0], g["b_in"][0]
    cuts = np.cumsum([0, 512, 512, 512, 8, 512, 512, 512, 512, 1024, 1024, 1024])
    part = {n: (w_in[:, a:b], b_in[a:b]) for n, a, b in
            zip(("fq", "fk", "fv", "ff", "su", "cq", "ck", "cv", "gf", "gs", "gc"), cuts, cuts[1:])}
    wt = {n: tiles(w) for n, (w, _) in part.items() if n != "ff"}
    bt = {n: b.reshape(-1, P) for n, (_, b) in part.items() if n != "ff"}
    inter = lambda d, names: np.stack([d[n] for n in names], 1).reshape((-1,) + d[names[0]].shape[1:])
    fox, ca = ("fq", "fk", "fv", "su"), ("cq", "ck", "cv")
    gates = ("gf", "gc", "gs")
    glu = g["w_ssm_glu"][0]
    dn = g["ffn_w_down"][0]
    up = tiles(g["ffn_w_up"][0])
    state = lambda a: a.reshape(16, P, *a.shape[2:]).swapaxes(0, 1).reshape(P, -1)
    edges = np.cumsum((0,) + FF_GROUPS) * P
    rel_at = np.clip(CA_BACK * P + np.arange(P)[:, None] - np.arange(CA_KEYS), -63, 256) + 63
    cw = np.concatenate([g["ffn_conv_w"][0], g["ffn_conv_b"]], 0)
    arrays = {
        "xT": chunks(g["x"][0].T), "memT": chunks(g["mem"][0].T),
        "w_ff": chunks(part["ff"][0]).transpose(1, 0, 2).reshape(P, 64),
        "b_ff": part["ff"][1].reshape(8, 1),
        "w_fox": inter(wt, fox), "w_ca": inter(wt, ca),
        "w_gate": np.concatenate([wt[n] for n in gates]),
        "w_foxo": tiles(g["w_fox_o"][0]), "w_cao": tiles(g["w_ca_o"][0]),
        "w_glu": np.concatenate([tiles(glu[:, :D]), tiles(glu[:, D:])], 2),
        "w_o": tiles(g["w_o"][0]), "w_kv": tiles(g["xa_wkv"][0]),
        "w_xq": tiles(g["xa_wq"][0]), "w_xo": tiles(g["xa_wo"][0]),
        "w_up": np.stack([up[:FF_TILES], up[FF_TILES:]], 1).reshape(2 * FF_TILES, P, D),
        **{f"w_dn{j}": tiles(dn[edges[j]:edges[j + 1]]) for j in range(3)},
        "b_cols": np.concatenate([inter(bt, fox), inter(bt, ca)] + [bt[n] for n in gates]).T,
        "lam_re": state(g["ssm_lambda_re"].reshape(1, -1)), "lam_im": state(g["ssm_lambda_im"].reshape(1, -1)),
        "log_dt": state(np.repeat(g["ssm_log_dt"], 64, axis=1)),
        "b_re": state(g["ssm_b_re"].reshape(1, -1, 16)), "b_im": state(g["ssm_b_im"].reshape(1, -1, 16)),
        "c_re": state(g["ssm_c_re"].swapaxes(2, 3).reshape(1, -1, 16)),
        "c_im": state(g["ssm_c_im"].swapaxes(2, 3).reshape(1, -1, 16)),
        "ssm_d": g["ssm_d"].reshape(4, P).T,
        "rel": g["ca_rel_bias"][0][:, rel_at],
        "conv": cw.reshape(4, FF_TILES, P).transpose(2, 1, 0).reshape(P, -1),
        "ln_cols": np.stack([g["ln_g"][0], g["ln_b"][0]], 1).reshape(6 * KD, P).T,
        "ln_rows": np.stack([g["ln_g"][0, 2], g["ln_b"][0, 2]]),
    }
    nc = bacc.Bacc("TRN2", target_bir_lowering=False, num_devices=1)
    arrays = {k: np.ascontiguousarray(a) for k, a in arrays.items()}
    args = {k: nc.dram_tensor(f"in_{k}", a.shape, mybir.dt.from_np(a.dtype), kind="ExternalInput").ap()
            for k, a in arrays.items()}
    args["cum_scratch"] = nc.dram_tensor("cum_scratch", (8, S), F32, kind="Internal").ap()
    args["out"] = nc.dram_tensor("out_dram", (1, S, D), F32, kind="ExternalOutput").ap()
    hybrid_layer(nc, **args)
    r = run_bass_kernel_spmd(nc, [{f"in_{k}": a for k, a in arrays.items()}], core_ids=[0])
    return r.results[0]["out_dram"]
```
